# Optimizing a Trainium2 kernel written in Bass

```python
import math
import jax
import jax.numpy as jnp
from jax import lax
import numpy as np
import jax, jax.numpy as jnp

D_MODEL = 1024
BATCH = 1
SEQ = 512
DEPTH = 2

GRID_W = 64
CTX_LEN = 256
N_EVEN = (DEPTH + 1) // 2
N_ODD = DEPTH // 2

GLA_HEADS = 4
GLA_DK = 64
GLA_DV = 128
GLA_GATE_RANK = 16
GLA_TAU = 16.0
GLA_CHUNK = 64

DIFF_HEADS = 4
DIFF_DQK = 64
DIFF_DV = 2 * DIFF_DQK
Q_BLOCK = 128
ROPE_BASE = 10000.0

SSD_D_INNER = 2 * D_MODEL
SSD_HEAD_DIM = 64
SSD_HEADS = SSD_D_INNER // SSD_HEAD_DIM
SSD_GROUPS = 4
SSD_STATE = 128
SSD_CONV = 5
SSD_CHUNK = 128
SSD_CONV_CH = SSD_D_INNER + 2 * SSD_GROUPS * SSD_STATE
SSD_IN = SSD_D_INNER + SSD_CONV_CH + 2 * SSD_HEADS

FFN_HIDDEN = 256 * (-(-8 * D_MODEL // (3 * 256)))

EV_SIZES = (GLA_HEADS * GLA_DK, GLA_HEADS * GLA_DK, GLA_HEADS * GLA_DV, GLA_HEADS * GLA_DV,
            GLA_GATE_RANK, GLA_GATE_RANK,
            DIFF_HEADS * 2 * DIFF_DQK, DIFF_HEADS * 2 * DIFF_DQK, DIFF_HEADS * DIFF_DV)
EV_IN = sum(EV_SIZES)
EV_MIX = GLA_HEADS * GLA_DV + DIFF_HEADS * DIFF_DV

ALPHA = (2 * DEPTH) ** 0.25
BETA = (8 * DEPTH) ** -0.25
LN_EPS = 1e-6
RMS_EPS = 1e-6
F32 = jnp.float32


def _split(t, sizes):
    out, start = [], 0
    for s in sizes:
        out.append(t[..., start:start + s])
        start += s
    return out

def layer_norm(x, g, b):
    xf = x.astype(F32)
    mu = jnp.mean(xf, -1, keepdims=True)
    var = jnp.mean(jnp.square(xf - mu), -1, keepdims=True)
    return ((xf - mu) * lax.rsqrt(var + LN_EPS) * g + b).astype(x.dtype)

def rms_norm(x, g):
    xf = x.astype(F32)
    return (xf * lax.rsqrt(jnp.mean(xf * xf, -1, keepdims=True) + RMS_EPS) * g).astype(x.dtype)

def group_rms_norm(y, g):
    yf = y.astype(F32)
    yg = yf.reshape(yf.shape[:-1] + (SSD_GROUPS, -1))
    yg = yg * lax.rsqrt(jnp.mean(yg * yg, -1, keepdims=True) + RMS_EPS)
    return (yg.reshape(yf.shape) * g).astype(y.dtype)

def to_heads(t, n):
    b, s, _ = t.shape
    return t.reshape(b, s, n, -1).transpose(0, 2, 1, 3)

def from_heads(t):
    b, h, s, d = t.shape
    return t.transpose(0, 2, 1, 3).reshape(b, s, h * d)

def swiglu(h, w_in, w_out):
    gate, up = jnp.split(h @ w_in, 2, axis=-1)
    return (jax.nn.silu(gate) * up) @ w_out

def rope_angles(n_tokens):
    rows = n_tokens // GRID_W
    row = jnp.repeat(jnp.arange(rows, dtype=F32), GRID_W)
    col = jnp.tile(jnp.arange(GRID_W, dtype=F32), rows)
    n_freq = DIFF_DQK // 4
    inv = ROPE_BASE ** (-jnp.arange(n_freq, dtype=F32) / n_freq)
    return row[:, None] * inv, col[:, None] * inv

def _rotate(t, ang):
    t1, t2 = jnp.split(t, 2, axis=-1)
    cos, sin = jnp.cos(ang), jnp.sin(ang)
    return jnp.concatenate([t1 * cos - t2 * sin, t2 * cos + t1 * sin], axis=-1)

def axial_rope(t, ang_row, ang_col):
    tr, tc = jnp.split(t.astype(F32), 2, axis=-1)
    return jnp.concatenate([_rotate(tr, ang_row), _rotate(tc, ang_col)], axis=-1).astype(t.dtype)

def centred_dwconv(t, w):
    pad = SSD_CONV // 2
    return lax.conv_general_dilated(t, w[:, None, :].astype(t.dtype), window_strides=(1,),
                                    padding=[(pad, pad)], dimension_numbers=('NWC', 'WIO', 'NWC'),
                                    feature_group_count=t.shape[-1])

def gla_chunked(q, k, v, log_a, s0):
    bsz, h, t, _ = k.shape
    n, c = t // GLA_CHUNK, GLA_CHUNK
    k, v, log_a = [z.astype(F32).reshape(bsz, h, n, c, -1) for z in (k, v, log_a)]
    b = jnp.cumsum(log_a, axis=3)
    b_last = b[:, :, :, -1:]
    chunk_kv = jnp.einsum('bhnck,bhncv->bhnkv', k * jnp.exp(b_last - b), v)
    decay = jnp.exp(b_last[:, :, :, 0])

    def step(s, inp):
        d, kv = inp
        return d[..., None] * s + kv, s

    s_final, s_start = lax.scan(step, s0.astype(F32),
                                (jnp.moveaxis(decay, 2, 0), jnp.moveaxis(chunk_kv, 2, 0)))
    if q is None:
        return None, s_final
    s_start = jnp.moveaxis(s_start, 0, 2)
    q_dec = q.astype(F32).reshape(bsz, h, n, c, -1) * jnp.exp(b)
    mask = jnp.tril(jnp.ones((c, c), dtype=bool))
    att = jnp.where(mask, jnp.einsum('bhnik,bhnjk->bhnij', q_dec, k * jnp.exp(-b)), 0.0)
    o = jnp.einsum('bhnij,bhnjv->bhniv', att, v) + jnp.einsum('bhnck,bhnkv->bhncv', q_dec, s_start)
    return o.reshape(bsz, h, t, -1), s_final

def gla_mixer(parts_c, parts_x, w_gate2, b_gate, norm_w, need_ctx):
    def prep(parts):
        q, k, v, g, r_f, r_b = parts
        la_f = jax.nn.log_sigmoid((r_f @ w_gate2[0] + b_gate[0]).astype(F32)) / GLA_TAU
        la_b = jax.nn.log_sigmoid((r_b @ w_gate2[1] + b_gate[1]).astype(F32)) / GLA_TAU
        return (to_heads(q, GLA_HEADS) * GLA_DK ** -0.5, to_heads(k, GLA_HEADS), to_heads(v, GLA_HEADS),
                to_heads(la_f, GLA_HEADS), to_heads(la_b, GLA_HEADS), g)

    qc, kc, vc, lfc, lbc, gc = prep(parts_c)
    qx, kx, vx, lfx, lbx, gx = prep(parts_x)
    flip = lambda t: jnp.flip(t, axis=2)
    s0 = jnp.zeros(kc.shape[:2] + (GLA_DK, GLA_DV), F32)
    o_cf, s_f = gla_chunked(qc if need_ctx else None, kc, vc, lfc, s0)
    o_cb, s_b = gla_chunked(flip(qc) if need_ctx else None, flip(kc), flip(vc), flip(lbc), s0)
    o_xf, _ = gla_chunked(qx, kx, vx, lfx, s_f)
    o_xb, _ = gla_chunked(flip(qx), flip(kx), flip(vx), flip(lbx), s_b)

    def finish(o, g):
        return from_heads(rms_norm(o, norm_w)).astype(g.dtype) * jax.nn.silu(g)

    out_x = finish(o_xf + flip(o_xb), gx)
    out_c = finish(o_cf + flip(o_cb), gc) if need_ctx else None
    return out_c, out_x

def diff_attend(q, k, v, lam):
    s = jnp.einsum('bhmqd,bhmkd->bhmqk', q, k).astype(F32) * DIFF_DQK ** -0.5
    p = jax.nn.softmax(s, axis=-1)
    w = p[:, :, 0] - lam * p[:, :, 1]
    return jnp.einsum('bhqk,bhkd->bhqd', w.astype(v.dtype), v)

def diff_mixer(parts_c, parts_x, lam_p, norm_w, layer, ang_row, ang_col, need_ctx):
    def prep(q, k, v):
        b, s, _ = q.shape
        q = q.reshape(b, s, DIFF_HEADS, 2, DIFF_DQK).transpose(0, 2, 3, 1, 4)
        k = k.reshape(b, s, DIFF_HEADS, 2, DIFF_DQK).transpose(0, 2, 3, 1, 4)
        return q, k, to_heads(v, DIFF_HEADS)

    qc, kc, vc = prep(*parts_c)
    qx, kx, vx = prep(*parts_x)
    qx = axial_rope(qx, ang_row, ang_col)
    kx = axial_rope(kx, ang_row, ang_col)
    lam_init = 0.8 - 0.6 * math.exp(-0.3 * layer)
    lp = lam_p.astype(F32)
    lam = jnp.exp(jnp.sum(lp[0] * lp[1])) - jnp.exp(jnp.sum(lp[2] * lp[3])) + lam_init
    k_all = jnp.concatenate([kc, kx], axis=3)
    v_all = jnp.concatenate([vc, vx], axis=2)
    b, h, _, t, d = qx.shape
    nb = t // Q_BLOCK
    q_blocks = jnp.moveaxis(qx.reshape(b, h, 2, nb, Q_BLOCK, d), 3, 0)
    o_blocks = lax.map(lambda qb: diff_attend(qb, k_all, v_all, lam), q_blocks)
    o_x = jnp.moveaxis(o_blocks, 0, 2).reshape(b, h, t, DIFF_DV)

    def finish(o):
        return from_heads(rms_norm(o, norm_w) * (1.0 - lam_init))

    out_x = finish(o_x)
    out_c = finish(diff_attend(qc, kc, vc, lam)) if need_ctx else None
    return out_c, out_x

def even_mixer(hc, hx, w_in, w_out, gla_w_gate2, gla_b_gate, gla_norm_w, diff_lambda, diff_norm_w,
               layer, ang_row, ang_col, need_ctx):
    pc = _split(hc @ w_in, EV_SIZES)
    px = _split(hx @ w_in, EV_SIZES)
    gla_c, gla_x = gla_mixer(pc[:6], px[:6], gla_w_gate2, gla_b_gate, gla_norm_w, need_ctx)
    dif_c, dif_x = diff_mixer(pc[6:], px[6:], diff_lambda, diff_norm_w, layer, ang_row, ang_col, need_ctx)
    out_x = jnp.concatenate([gla_x, dif_x], axis=-1) @ w_out
    out_c = jnp.concatenate([gla_c, dif_c], axis=-1) @ w_out if need_ctx else None
    return out_c, out_x

def ssd_chunked(x, dt, a, bm, cm, s0, with_out):
    bsz, t, h, p = x.shape
    g, s = bm.shape[-2:]
    e, c = h // g, SSD_CHUNK
    n = t // c
    x = x.astype(F32).reshape(bsz, n, c, g, e, p)
    dt = dt.astype(F32).reshape(bsz, n, c, g, e)
    bm = bm.astype(F32).reshape(bsz, n, c, g, s)
    cm = cm.astype(F32).reshape(bsz, n, c, g, s)
    acs = jnp.cumsum(dt * a.astype(F32).reshape(g, e), axis=2)
    a_last = acs[:, :, -1]
    xdt = x * dt[..., None]
    chunk_state = jnp.einsum('bncgs,bncge,bncgep->bngeps', bm, jnp.exp(a_last[:, :, None] - acs), xdt)

    def step(st, inp):
        d, cs = inp
        return jnp.exp(d)[..., None, None] * st + cs, st

    s_final, s_start = lax.scan(step, s0.astype(F32),
                                (jnp.moveaxis(a_last, 1, 0), jnp.moveaxis(chunk_state, 1, 0)))
    if not with_out:
        return None, s_final
    s_start = jnp.moveaxis(s_start, 0, 1)
    acs_t = jnp.moveaxis(acs, 2, -1)
    mask = jnp.tril(jnp.ones((c, c), dtype=bool))
    decay = jnp.exp(jnp.where(mask, acs_t[..., :, None] - acs_t[..., None, :], -jnp.inf))
    cb = jnp.einsum('bnigs,bnjgs->bngij', cm, bm)
    y_diag = jnp.einsum('bngij,bngeij,bnjgep->bnigep', cb, decay, xdt)
    y_off = jnp.einsum('bncgs,bngeps,bncge->bncgep', cm, s_start, jnp.exp(acs))
    return (y_diag + y_off).reshape(bsz, t, h, p), s_final

def odd_mixer(hc, hx, w_in, conv_w, conv_b, dt_bias, a_log, d_skip, norm_w, w_out, need_ctx):
    def prep(hh):
        b, s, _ = hh.shape
        z, xbc, dt = _split(hh @ w_in, (SSD_D_INNER, SSD_CONV_CH, 2 * SSD_HEADS))
        xbc = jax.nn.silu(centred_dwconv(xbc, conv_w) + conv_b)
        xs, bm, cm = _split(xbc, (SSD_D_INNER, SSD_GROUPS * SSD_STATE, SSD_GROUPS * SSD_STATE))
        dt = jax.nn.softplus(dt.astype(F32).reshape(b, s, 2, SSD_HEADS) + dt_bias.astype(F32))
        return (z, xs.reshape(b, s, SSD_HEADS, SSD_HEAD_DIM), bm.reshape(b, s, SSD_GROUPS, SSD_STATE),
                cm.reshape(b, s, SSD_GROUPS, SSD_STATE), dt[:, :, 0], dt[:, :, 1])

    zc, xc, bc, cc, dfc, dbc = prep(hc)
    zx, xx, bx, cx, dfx, dbx = prep(hx)
    a = -jnp.exp(a_log.astype(F32))
    flip = lambda t: jnp.flip(t, axis=1)
    s0 = jnp.zeros((hc.shape[0], SSD_GROUPS, SSD_HEADS // SSD_GROUPS, SSD_HEAD_DIM, SSD_STATE), F32)
    y_cf, s_f = ssd_chunked(xc, dfc, a[0], bc, cc, s0, need_ctx)
    y_cb, s_b = ssd_chunked(flip(xc), flip(dbc), a[1], flip(bc), flip(cc), s0, need_ctx)
    y_xf, _ = ssd_chunked(xx, dfx, a[0], bx, cx, s_f, True)
    y_xb, _ = ssd_chunked(flip(xx), flip(dbx), a[1], flip(bx), flip(cx), s_b, True)

    def finish(yf, yb, xs, z):
        y = yf + flip(yb) + d_skip.astype(F32)[:, None] * xs.astype(F32)
        b, s = y.shape[:2]
        y = y.reshape(b, s, SSD_D_INNER) * jax.nn.silu(z.astype(F32))
        return group_rms_norm(y, norm_w).astype(z.dtype) @ w_out

    out_x = finish(y_xf, y_xb, xx, zx)
    out_c = finish(y_cf, y_cb, xc, zc) if need_ctx else None
    return out_c, out_x

def first_inputs(seed: int = 0) -> dict:
    key = jax.random.key(seed)
    keys = iter(jax.random.split(key, 40))

    def nrm(shape, scale):
        return scale * jax.random.normal(next(keys), shape, F32)

    def gain(shape):
        return 1.0 + nrm(shape, 0.02)

    D = D_MODEL
    dt0 = jnp.exp(jax.random.uniform(next(keys), (N_ODD, 2, SSD_HEADS), F32, math.log(1e-3), math.log(1e-1)))
    dt_bias = dt0 + jnp.log(-jnp.expm1(-dt0))
    a_log = jnp.log(jax.random.uniform(next(keys), (N_ODD, 2, SSD_HEADS), F32, 1.0, 16.0))
    return {
        'x': nrm((BATCH, SEQ, D), 1.0),
        'c': nrm((BATCH, D), 1.0),
        'ctx': nrm((BATCH, CTX_LEN, D), 1.0),
        'c_ctx': nrm((D,), 1.0),
        'mod_w': nrm((DEPTH, D, 6 * D), D ** -0.5),
        'mod_b': nrm((DEPTH, 6 * D), 0.01),
        'ln_g': gain((DEPTH, 2, D)),
        'ln_b': nrm((DEPTH, 2, D), 0.02),
        'ffn_w_in': nrm((DEPTH, D, 2 * FFN_HIDDEN), D ** -0.5),
        'ffn_w_out': nrm((DEPTH, FFN_HIDDEN, D), BETA * FFN_HIDDEN ** -0.5),
        'ev_w_in': nrm((N_EVEN, D, EV_IN), D ** -0.5),
        'ev_w_out': nrm((N_EVEN, EV_MIX, D), BETA * EV_MIX ** -0.5),
        'gla_w_gate2': nrm((N_EVEN, 2, GLA_GATE_RANK, GLA_HEADS * GLA_DK), GLA_GATE_RANK ** -0.5),
        'gla_b_gate': nrm((N_EVEN, 2, GLA_HEADS * GLA_DK), 0.1),
        'gla_norm_w': gain((N_EVEN, GLA_DV)),
        'diff_lambda': nrm((N_EVEN, 4, DIFF_DQK), 0.1),
        'diff_norm_w': gain((N_EVEN, DIFF_DV)),
        'ssd_w_in': nrm((N_ODD, D, SSD_IN), D ** -0.5),
        'ssd_conv_w': nrm((N_ODD, SSD_CONV, SSD_CONV_CH), SSD_CONV ** -0.5),
        'ssd_conv_b': nrm((N_ODD, SSD_CONV_CH), 0.02),
        'ssd_dt_bias': dt_bias,
        'ssd_a_log': a_log,
        'ssd_d': gain((N_ODD, SSD_HEADS)),
        'ssd_norm_w': gain((N_ODD, SSD_D_INNER)),
        'ssd_w_out': nrm((N_ODD, SSD_D_INNER, D), BETA * SSD_D_INNER ** -0.5),
    }

def first_block(x, c, ctx, c_ctx, mod_w, mod_b, ln_g, ln_b, ffn_w_in, ffn_w_out, ev_w_in, ev_w_out,
              gla_w_gate2, gla_b_gate, gla_norm_w, diff_lambda, diff_norm_w, ssd_w_in, ssd_conv_w,
              ssd_conv_b, ssd_dt_bias, ssd_a_log, ssd_d, ssd_norm_w, ssd_w_out):
    ang_row, ang_col = rope_angles(x.shape[1])
    for layer in range(DEPTH):
        need_ctx = layer < DEPTH - 1
        mod_x = jax.nn.silu(c) @ mod_w[layer] + mod_b[layer]
        mod_c = jax.nn.silu(c_ctx) @ mod_w[layer] + mod_b[layer]
        shm_x, scm_x, gm_x, shf_x, scf_x, gf_x = [m[:, None, :] for m in jnp.split(mod_x, 6, axis=-1)]
        shm_c, scm_c, gm_c, shf_c, scf_c, gf_c = jnp.split(mod_c, 6, axis=-1)
        hx = x * (1.0 + scm_x) + shm_x
        hc = ctx * (1.0 + scm_c) + shm_c
        if layer % 2 == 0:
            e = layer // 2
            mix_c, mix_x = even_mixer(hc, hx, ev_w_in[e], ev_w_out[e], gla_w_gate2[e], gla_b_gate[e],
                                      gla_norm_w[e], diff_lambda[e], diff_norm_w[e], layer,
                                      ang_row, ang_col, need_ctx)
        else:
            o = layer // 2
            mix_c, mix_x = odd_mixer(hc, hx, ssd_w_in[o], ssd_conv_w[o], ssd_conv_b[o], ssd_dt_bias[o],
                                     ssd_a_log[o], ssd_d[o], ssd_norm_w[o], ssd_w_out[o], need_ctx)
        x = layer_norm(ALPHA * x + gm_x * mix_x, ln_g[layer, 0], ln_b[layer, 0])
        x = layer_norm(ALPHA * x + gf_x * swiglu(x * (1.0 + scf_x) + shf_x, ffn_w_in[layer], ffn_w_out[layer]),
                       ln_g[layer, 1], ln_b[layer, 1])
        if need_ctx:
            ctx = layer_norm(ALPHA * ctx + gm_c * mix_c, ln_g[layer, 0], ln_b[layer, 0])
            ctx = layer_norm(ALPHA * ctx + gf_c * swiglu(ctx * (1.0 + scf_c) + shf_c, ffn_w_in[layer],
                                                         ffn_w_out[layer]),
                             ln_g[layer, 1], ln_b[layer, 1])
    return x


_first_inputs = first_inputs


def first_inputs(seed=0):
    import zlib

    import numpy as np

    out = dict(_first_inputs(seed))
    spreads = {}
    factors = {'mod_b': 5.64,
     'gla_b_gate': 8.0,
     'gla_norm_w': 8.0,
     'diff_lambda': 8.0,
     'diff_norm_w': 8.0,
     'ssd_conv_b': 8.0,
     'ssd_d': 8.0,
     'ssd_norm_w': 8.0}
    for name, (base, spread) in spreads.items():
        noise = np.random.default_rng([zlib.crc32(name.encode()), seed]).standard_normal(out[name].shape)
        drawn = base * np.exp(spread * noise) if base else spread * noise
        out[name] = jnp.asarray(drawn.astype(out[name].dtype))
    for name, factor in factors.items():
        out[name] = (out[name] * factor).astype(out[name].dtype)
    return out


_narrow_inputs = first_inputs


def first_inputs(seed=0):
    out = dict(_narrow_inputs(seed))
    wider = {'gla_norm_w': 5.12, 'diff_norm_w': 4.69, 'ssd_d': 7.79, 'ssd_norm_w': 3.92}
    for name, times in wider.items():
        mean = out[name].mean()
        out[name] = (mean + times * (out[name] - mean)).astype(out[name].dtype)
    return out


DEPTH_2 = 1

ATT_HEADS = 8
ATT_KV_HEADS = 2
ATT_GROUP = ATT_HEADS // ATT_KV_HEADS
ATT_HEAD_DIM = 64
ATT_WIDTH = ATT_HEADS * ATT_HEAD_DIM
ATT_KV_WIDTH = ATT_KV_HEADS * ATT_HEAD_DIM
WINDOW = 128
BLOCK = 128
HG_WIDTH = D_MODEL // 2
HG_EXPAND = 128
HG_HEADS = HG_WIDTH // HG_EXPAND
CHUNK = 64
D_FF = 2816
N_MOD = 9
IN_WIDTH = ATT_WIDTH + 2 * ATT_KV_WIDTH + 5 * HG_WIDTH + 2 * D_MODEL
EPS = 1e-6
NEG_INF = -1e30


def rmsnorm(x, g):
    x32 = x.astype(jnp.float32)
    y = x32 * lax.rsqrt(jnp.mean(x32 * x32, axis=-1, keepdims=True) + EPS)
    return (y * g.astype(jnp.float32)).astype(x.dtype)

def swiglu_2(h, w_in, w_out):
    gate, up = jnp.split(h @ w_in, 2, axis=-1)
    return (jax.nn.silu(gate) * up) @ w_out

def ada_pre(z, g, shift, scale):
    return rmsnorm(z, g) * (1 + scale) + shift

def ada_post(z, y, g, gate, w):
    return z + w * gate * rmsnorm(y, g)

def rope_1d(x, pos):
    half = x.shape[-1] // 2
    freqs = ROPE_BASE ** (-jnp.arange(half, dtype=jnp.float32) / half)
    ang = pos.astype(jnp.float32)[:, None] * freqs[None, :]
    cos, sin = jnp.cos(ang).astype(x.dtype), jnp.sin(ang).astype(x.dtype)
    x1, x2 = x[..., :half], x[..., half:]
    return jnp.concatenate([x1 * cos - x2 * sin, x1 * sin + x2 * cos], axis=-1)

def rope_2d(x, row, col):
    h = x.shape[-1] // 2
    return jnp.concatenate([rope_1d(x[..., :h], row), rope_1d(x[..., h:], col)], axis=-1)

def split_in(p):
    sizes = (ATT_WIDTH, ATT_KV_WIDTH, ATT_KV_WIDTH, HG_WIDTH, HG_WIDTH, HG_WIDTH, HG_WIDTH, HG_WIDTH, D_MODEL, D_MODEL)
    points = [int(v) for v in np.cumsum(sizes)[:-1]]
    return jnp.split(p, points, axis=-1)

def q_heads(z):
    B, T, _ = z.shape
    return z.reshape(B, T, ATT_KV_HEADS, ATT_GROUP, ATT_HEAD_DIM).transpose(0, 2, 3, 1, 4)

def kv_heads(z):
    B, T, _ = z.shape
    return z.reshape(B, T, ATT_KV_HEADS, ATT_HEAD_DIM).transpose(0, 2, 1, 3)

def hg_heads(z):
    B, T, _ = z.shape
    return z.reshape(B, T, HG_HEADS, HG_EXPAND).transpose(0, 2, 1, 3)

def hg_merge(o):
    B, H, T, d = o.shape
    return o.transpose(0, 2, 1, 3).reshape(B, T, H * d)

def softmax_with_sink(logits, sink):
    sink_col = jnp.broadcast_to(sink, logits.shape[:-1] + (1,))
    p = jax.nn.softmax(jnp.concatenate([logits, sink_col], axis=-1), axis=-1)
    return p[..., :-1]

def window_attention(q, k, v, kc, vc, sink):
    B, KVH, G, T, hd = q.shape
    nb = T // BLOCK
    scale = hd ** -0.5
    qb = q.reshape(B, KVH, G, nb, BLOCK, hd)

    def band(z):
        zp = jnp.pad(z, ((0, 0), (0, 0), (BLOCK, BLOCK), (0, 0))).reshape(B, KVH, nb + 2, BLOCK, hd)
        return jnp.concatenate([zp[:, :, :nb], zp[:, :, 1:nb + 1], zp[:, :, 2:]], axis=3)

    kb, vb = band(k), band(v)
    blk = jnp.arange(nb)[:, None, None] * BLOCK
    qpos = blk + jnp.arange(BLOCK)[None, :, None]
    kpos = blk - BLOCK + jnp.arange(3 * BLOCK)[None, None, :]
    valid = (jnp.abs(kpos - qpos) <= WINDOW) & (kpos >= 0) & (kpos < T)
    s_band = jnp.einsum('bkgnqd,bknsd->bkgnqs', qb, kb).astype(jnp.float32) * scale
    s_band = jnp.where(valid, s_band, NEG_INF)
    s_ctx = jnp.einsum('bkgnqd,bksd->bkgnqs', qb, kc).astype(jnp.float32) * scale
    sink_b = sink.astype(jnp.float32).reshape(KVH, G)[None, :, :, None, None, None]
    p = softmax_with_sink(jnp.concatenate([s_band, s_ctx], axis=-1), sink_b).astype(v.dtype)
    o = (jnp.einsum('bkgnqs,bknsd->bkgnqd', p[..., :3 * BLOCK], vb)
         + jnp.einsum('bkgnqs,bksd->bkgnqd', p[..., 3 * BLOCK:], vc))
    return o.reshape(B, KVH, G, T, hd).transpose(0, 3, 1, 2, 4).reshape(B, T, KVH * G * hd)

def context_attention(qc, kc, vc, sink):
    B, KVH, G, L, hd = qc.shape
    s = jnp.einsum('bkgqd,bksd->bkgqs', qc, kc).astype(jnp.float32) * (hd ** -0.5)
    sink_b = sink.astype(jnp.float32).reshape(KVH, G)[None, :, :, None, None]
    p = softmax_with_sink(s, sink_b).astype(vc.dtype)
    o = jnp.einsum('bkgqs,bksd->bkgqd', p, vc)
    return o.transpose(0, 3, 1, 2, 4).reshape(B, L, KVH * G * hd)

def gated_scan(q, k, v, logf, s0):
    B, H, T, dk = q.shape
    dv = v.shape[-1]
    n = T // CHUNK

    def chunks(z):
        return jnp.moveaxis(z.reshape(B, H, n, CHUNK, z.shape[-1]), 2, 0)

    tril = jnp.tril(jnp.ones((CHUNK, CHUNK), dtype=bool))

    def step(S, inp):
        qc, kc, vc, lf = inp
        b = jnp.cumsum(lf, axis=-2)
        o_inter = jnp.einsum('bhtd,bhde->bhte', qc * jnp.exp(b), S)
        diff = b[:, :, :, None, :] - b[:, :, None, :, :]
        decay = jnp.where(tril[:, :, None], jnp.exp(jnp.minimum(diff, 0.0)), 0.0)
        scores = jnp.einsum('bhtsd,bhsd->bhts', qc[:, :, :, None, :] * decay, kc)
        o_intra = jnp.einsum('bhts,bhse->bhte', scores, vc)
        b_last = b[:, :, -1:, :]
        k_dec = kc * jnp.exp(b_last - b)
        S_new = jnp.exp(b_last[:, :, 0, :])[..., None] * S + jnp.einsum('bhsd,bhse->bhde', k_dec, vc)
        return S_new, o_inter + o_intra

    S_fin, o = lax.scan(step, s0, (chunks(q), chunks(k), chunks(v), chunks(logf)))
    return jnp.moveaxis(o, 0, 2).reshape(B, H, T, dv), S_fin

def hgrn_bidir(q, v, lf_f, k_f, lf_b, k_b, s0_f, s0_b):
    flip = lambda z: jnp.flip(z, axis=2)
    o_f, s_f = gated_scan(q, k_f, v, lf_f, s0_f)
    o_b, s_b = gated_scan(flip(q), flip(k_b), flip(v), flip(lf_b), s0_b)
    return o_f + flip(o_b), s_f, s_b

def hg_forget(z, lb):
    f = lb + (1.0 - lb) * jax.nn.sigmoid(z.astype(jnp.float32))
    return hg_heads(jnp.log(f)), hg_heads(1.0 - f)

def mixer(h, hc, w_in, sink, lb_f, lb_b, g_hnorm, w_o_attn, w_o_hgrn, w_out, need_ctx):
    B, T, _ = h.shape
    rows = T // GRID_W
    row = jnp.repeat(jnp.arange(rows, dtype=jnp.int32), GRID_W)
    col = jnp.tile(jnp.arange(GRID_W, dtype=jnp.int32), rows)
    f32 = jnp.float32
    aq, ak, av, hq, hff, hfb, hi, hg, ga, gh = split_in(h @ w_in)
    aqc, akc, avc, hqc, hffc, hfbc, hic, hgc, gac, ghc = split_in(hc @ w_in)
    q = rope_2d(q_heads(aq), row, col)
    k = rope_2d(kv_heads(ak), row, col)
    kc, vc = kv_heads(akc), kv_heads(avc)
    o_att = window_attention(q, k, kv_heads(av), kc, vc, sink)
    qhc = hg_heads(jax.nn.silu(hqc.astype(f32)))
    vhc = hg_heads(hic.astype(f32))
    lfc_f, kc_f = hg_forget(hffc, lb_f)
    lfc_b, kc_b = hg_forget(hfbc, lb_b)
    s0 = jnp.zeros((B, HG_HEADS, HG_EXPAND, HG_EXPAND), f32)
    o_hc, s_f, s_b = hgrn_bidir(qhc, vhc, lfc_f, kc_f, lfc_b, kc_b, s0, s0)
    qh = hg_heads(jax.nn.silu(hq.astype(f32)))
    vh = hg_heads(hi.astype(f32))
    lf_f, k_f = hg_forget(hff, lb_f)
    lf_b, k_b = hg_forget(hfb, lb_b)
    o_h, _, _ = hgrn_bidir(qh, vh, lf_f, k_f, lf_b, k_b, s_f, s_b)

    def readout(o, gate):
        return rmsnorm(hg_merge(o), g_hnorm).astype(gate.dtype) * jax.nn.silu(gate)

    def merge(o_a, o_r, g_a, g_r):
        return (jax.nn.sigmoid(g_a) * (o_a @ w_o_attn) + jax.nn.sigmoid(g_r) * (o_r @ w_o_hgrn)) @ w_out

    y = merge(o_att, readout(o_h, hg), ga, gh)
    if not need_ctx:
        return y, None
    o_attc = context_attention(q_heads(aqc), kc, vc, sink)
    yc = merge(o_attc, readout(o_hc, hgc), gac, ghc)
    return y, yc

def second_inputs(seed: int = 0) -> dict:
    key = jax.random.key(seed)
    ks = jax.random.split(key, 20)
    f32 = jnp.float32

    def nrm(k, shape, scale):
        return jax.random.normal(k, shape, f32) * scale

    D = D_MODEL
    return {
        'x': nrm(ks[0], (BATCH, SEQ, D), 1.0),
        'c': nrm(ks[1], (BATCH, D), 1.0),
        'ctx': nrm(ks[2], (BATCH, CTX_LEN, D), 1.0),
        'c_ctx': nrm(ks[3], (D,), 1.0),
        'w_ada': nrm(ks[4], (DEPTH_2, D, N_MOD * D), 0.5 * D ** -0.5),
        'b_ada': nrm(ks[5], (DEPTH_2, N_MOD * D), 0.02),
        'norm_pre': 1.0 + nrm(ks[6], (DEPTH_2, 3, D), 0.02),
        'norm_post': 1.0 + nrm(ks[7], (DEPTH_2, 3, D), 0.02),
        'ffn1_w_in': nrm(ks[8], (DEPTH_2, D, 2 * D_FF), D ** -0.5),
        'ffn1_w_out': nrm(ks[9], (DEPTH_2, D_FF, D), D_FF ** -0.5),
        'ffn2_w_in': nrm(ks[10], (DEPTH_2, D, 2 * D_FF), D ** -0.5),
        'ffn2_w_out': nrm(ks[11], (DEPTH_2, D_FF, D), D_FF ** -0.5),
        'mix_w_in': nrm(ks[12], (DEPTH_2, D, IN_WIDTH), D ** -0.5),
        'attn_sink': nrm(ks[13], (DEPTH_2, ATT_HEADS), 0.5),
        'hgrn_lb_fwd': nrm(ks[14], (DEPTH_2 + 1, HG_WIDTH), 0.5),
        'hgrn_lb_bwd': nrm(ks[15], (DEPTH_2 + 1, HG_WIDTH), 0.5),
        'hgrn_norm': 1.0 + nrm(ks[16], (DEPTH_2, HG_WIDTH), 0.02),
        'w_o_attn': nrm(ks[17], (DEPTH_2, ATT_WIDTH, D), ATT_WIDTH ** -0.5),
        'w_o_hgrn': nrm(ks[18], (DEPTH_2, HG_WIDTH, D), HG_WIDTH ** -0.5),
        'w_out': nrm(ks[19], (DEPTH_2, D, D), D ** -0.5),
    }

def second_block(x, c, ctx, c_ctx, w_ada, b_ada, norm_pre, norm_post, ffn1_w_in, ffn1_w_out,
              ffn2_w_in, ffn2_w_out, mix_w_in, attn_sink, hgrn_lb_fwd, hgrn_lb_bwd, hgrn_norm,
              w_o_attn, w_o_hgrn, w_out):
    B, T, D = x.shape
    lb_f_all = jnp.cumsum(jax.nn.softmax(hgrn_lb_fwd.astype(jnp.float32), axis=0), axis=0)
    lb_b_all = jnp.cumsum(jax.nn.softmax(hgrn_lb_bwd.astype(jnp.float32), axis=0), axis=0)
    xc = ctx
    for l in range(DEPTH_2):
        need_ctx = l < DEPTH_2 - 1
        mod = (jax.nn.silu(c) @ w_ada[l] + b_ada[l]).reshape(B, N_MOD, 1, D)
        mod_c = (jax.nn.silu(c_ctx) @ w_ada[l] + b_ada[l]).reshape(N_MOD, D)
        m = [mod[:, j] for j in range(N_MOD)]
        mc = [mod_c[j] for j in range(N_MOD)]
        h = ada_pre(x, norm_pre[l, 0], m[0], m[1])
        x = ada_post(x, swiglu_2(h, ffn1_w_in[l], ffn1_w_out[l]), norm_post[l, 0], m[2], 0.5)
        hc = ada_pre(xc, norm_pre[l, 0], mc[0], mc[1])
        xc = ada_post(xc, swiglu_2(hc, ffn1_w_in[l], ffn1_w_out[l]), norm_post[l, 0], mc[2], 0.5)
        h = ada_pre(x, norm_pre[l, 1], m[3], m[4])
        hc = ada_pre(xc, norm_pre[l, 1], mc[3], mc[4])
        y, yc = mixer(h, hc, mix_w_in[l], attn_sink[l], lb_f_all[l], lb_b_all[l], hgrn_norm[l],
                      w_o_attn[l], w_o_hgrn[l], w_out[l], need_ctx)
        x = ada_post(x, y, norm_post[l, 1], m[5], 1.0)
        h = ada_pre(x, norm_pre[l, 2], m[6], m[7])
        x = ada_post(x, swiglu_2(h, ffn2_w_in[l], ffn2_w_out[l]), norm_post[l, 2], m[8], 0.5)
        if need_ctx:
            xc = ada_post(xc, yc, norm_post[l, 1], mc[5], 1.0)
            hc = ada_pre(xc, norm_pre[l, 2], mc[6], mc[7])
            xc = ada_post(xc, swiglu_2(hc, ffn2_w_in[l], ffn2_w_out[l]), norm_post[l, 2], mc[8], 0.5)
    return x


def setup_inputs(seed=0):
    out = dict(first_inputs(seed))
    for name, value in second_inputs(seed + 1).items():
        if name != "x":
            out[name + "_2"] = value
    return out


def reference(
    x, c, ctx, c_ctx, mod_w, mod_b, ln_g, ln_b, ffn_w_in, ffn_w_out, ev_w_in, ev_w_out,
    gla_w_gate2, gla_b_gate, gla_norm_w, diff_lambda, diff_norm_w, ssd_w_in, ssd_conv_w,
    ssd_conv_b, ssd_dt_bias, ssd_a_log, ssd_d, ssd_norm_w, ssd_w_out, c_2, ctx_2, c_ctx_2,
    w_ada_2, b_ada_2, norm_pre_2, norm_post_2, ffn1_w_in_2, ffn1_w_out_2, ffn2_w_in_2,
    ffn2_w_out_2, mix_w_in_2, attn_sink_2, hgrn_lb_fwd_2, hgrn_lb_bwd_2, hgrn_norm_2,
    w_o_attn_2, w_o_hgrn_2, w_out_2,
):
    x = first_block(
        x, c, ctx, c_ctx, mod_w, mod_b, ln_g, ln_b, ffn_w_in, ffn_w_out, ev_w_in, ev_w_out,
        gla_w_gate2, gla_b_gate, gla_norm_w, diff_lambda, diff_norm_w, ssd_w_in, ssd_conv_w,
        ssd_conv_b, ssd_dt_bias, ssd_a_log, ssd_d, ssd_norm_w, ssd_w_out,
    )
    return second_block(
        x, c_2, ctx_2, c_ctx_2, w_ada_2, b_ada_2, norm_pre_2, norm_post_2, ffn1_w_in_2,
        ffn1_w_out_2, ffn2_w_in_2, ffn2_w_out_2, mix_w_in_2, attn_sink_2, hgrn_lb_fwd_2,
        hgrn_lb_bwd_2, hgrn_norm_2, w_o_attn_2, w_o_hgrn_2, w_out_2,
    )


_drawn_inputs = setup_inputs


def setup_inputs(seed=0):
    import zlib

    import numpy as np

    out = dict(_drawn_inputs(seed))
    spreads = {}
    factors = {'norm_pre_2': 5.631,
     'norm_post_2': 7.841,
     'attn_sink_2': 8.0,
     'hgrn_lb_fwd_2': 8.0,
     'hgrn_lb_bwd_2': 8.0,
     'hgrn_norm_2': 8.0}
    for name, (base, spread) in spreads.items():
        noise = np.random.default_rng([zlib.crc32(name.encode()), seed]).standard_normal(out[name].shape)
        drawn = base * np.exp(spread * noise) if base else spread * noise
        out[name] = jnp.asarray(drawn.astype(out[name].dtype))
    for name, factor in factors.items():
        out[name] = (out[name] * factor).astype(out[name].dtype)
    return out
```

```python
import math

import numpy as np
import concourse.bass as bass
from concourse import mybir

F = mybir.dt.float32
U32 = mybir.dt.uint32
ALU = mybir.AluOpType
ACT = mybir.ActivationFunctionType
AX = mybir.AxisListType
D = 1024
T = 768
TC = 256
ALPHA = 4 ** 0.25
EPS = 1e-6
NEG = -1e30
FF = 2816
FT = 22
STOP = 99


class Lane:

    def __init__(self, sem):
        self.sem, self.n, self.seen, self.list = sem, 0, {}, []

    def wait(self, deps):
        for d in deps:
            if isinstance(d, list) or isinstance(d, tuple) and not (len(d) == 2 and isinstance(d[1], int)):
                self.wait(d)
            elif d is not None:
                sem, val = d
                if self.seen.get(id(sem), 0) < val:
                    self.seen[id(sem)] = val
                    self.list.append((None, sem, val))

    def do(self, fn, *deps, inc=True):
        self.wait(deps)
        if not inc:
            self.list.append((fn, None, 0))
            return None
        self.n += 1
        self.list.append((fn, self.sem, 1))
        return (self.sem, self.n)

    def dma(self, fn, sem, counts, *deps):
        self.wait(deps)
        counts[id(sem)] = counts.get(id(sem), 0) + 16
        self.list.append((fn, sem, 16))
        return (sem, counts[id(sem)])

    def emit(self, eng):
        for fn, sem, val in self.list:
            if fn is None:
                eng.wait_ge(sem, val)
            else:
                ins = fn(eng)
                if sem is not None:
                    ins.then_inc(sem, val)


class Slots:

    def __init__(self, views):
        self.v, self.free, self.i = views, [[] for _ in views], -1

    def take(self):
        self.i = (self.i + 1) % len(self.v)
        free = self.free[self.i]
        assert free is not None
        self.free[self.i] = None
        return self.i, self.v[self.i], free


def program(nc, a, con, out, dbg=None):
    from contextlib import ExitStack
    ctx = ExitStack()
    with ctx:
        def sb(name, shape):
            return ctx.enter_context(nc.sbuf_tensor(name, shape, F))

        def sem(name):
            return ctx.enter_context(nc.semaphore(name))

        XT = sb("XT", [128, 8, T])
        HT = sb("HT", [128, 8, T])
        RW = sb("RW", [128, 3, 4096])
        A = sb("A", [128, 20736])
        TM = sb("TM", [128, 4992])
        VEC = sb("VEC", [128, 5, 128])
        M0 = sb("M0", [128, 48, 2])
        M1 = sb("M1", [128, 48, 2])
        M2 = sb("M2", [128, 72, 2])
        CC = sb("CC", [128, 4, 128])
        SM = sb("SM", [128, 256])
        PS = ctx.enter_context(nc.psum_tensor("PS", [128, 4096], F))
        ident, triF, triB, perm = (CC[:, i, :] for i in range(4))
        ones = sb("ones", [128, 128])
        cols = sb("cols", [128, 8])
        G0 = sb("G0", [128, 8, 128])
        epsc, onec = cols[:, 0:1], cols[:, 1:2]

        P, V, S, G = (Lane(sem(n)) for n in ("s_pe", "s_dve", "s_act", "s_pool"))
        Y = Lane(None)
        cnt = {}
        wsem = [sem(f"s_w{i}") for i in range(3)]
        lsem = [sem(f"s_l{i}") for i in range(8)]
        osem = sem("s_out")
        ring = Slots([RW[:, i, :] for i in range(3)])
        banks = Slots([PS[:, 1024 * i:1024 * i + 1024] for i in range(4)])

        def bar():
            return [(l.sem, l.n) for l in (P, V, S, G) if l.n]

        def load(parts):
            i, v, free = ring.take()
            tok = None
            for dst, src in parts:
                tok = Y.dma(lambda e, d=dst(v), s=src: e.dma_start(d, s), wsem[i], cnt, free)
            return i, v, tok

        nl = [0]

        def small(pairs, *deps):
            s = lsem[nl[0] % 8]
            nl[0] += 1
            tok = None
            for dst, src in pairs:
                tok = Y.dma(lambda e, d=dst, s_=src: e.dma_start(d, s_), s, cnt, *deps)
            return tok

        def mm(o, l, r, start, stop, *deps, inc=None):
            return P.do(lambda e: e.matmul(o, l, r, start=start, stop=stop, skip_group_check=True), *deps,
                        inc=stop if inc is None else inc)

        def tr(o, i, *deps, n=128):
            return P.do(lambda e: e.transpose(o, i, ident[0:n, 0:n]), *deps)

        def act(o, i, f, *deps, **kw):
            return S.do(lambda e: e.activation(o, i, f, **kw), *deps)

        def copyS(o, i, *deps):
            return S.do(lambda e: e.activation(o, i, ACT.Copy), *deps)

        def tt(o, i0, i1, op, *deps, eng=None):
            return (eng or V).do(lambda e: e.tensor_tensor(out=o, in0=i0, in1=i1, op=op), *deps)

        def ts(o, i, s1, s2, op0, op1, *deps, eng=None):
            if op1 is None:
                return (eng or V).do(lambda e: e.tensor_scalar(out=o, in0=i, scalar1=s1, scalar2=None, op0=op0), *deps)
            return (eng or V).do(lambda e: e.tensor_scalar(out=o, in0=i, scalar1=s1, scalar2=s2, op0=op0, op1=op1), *deps)

        def stt(o, i0, s, i1, op0, op1, *deps):
            return V.do(lambda e: e.scalar_tensor_tensor(out=o, in0=i0, scalar=s, in1=i1, op0=op0, op1=op1), *deps)

        def cpV(o, i, *deps):
            return V.do(lambda e: e.tensor_copy(o, i), *deps)

        def rcp(o, i, *deps):
            return V.do(lambda e: e.reciprocal(o, i), *deps)

        def ms(o, val, *deps, eng=None):
            return (eng or V).do(lambda e: e.memset(o, val), *deps)

        def wsrc(w, c0, n):
            return w[:, c0:c0 + n].rearrange("(k p) n -> p k n", p=128)

        def wpanel(*cuts):
            width = sum(c[2] for c in cuts)
            parts, at = [], 0
            for w, c0, n in cuts:
                parts.append((lambda v, at=at, n=n, wd=width:
                              v[:, 0:8 * wd].rearrange("p (k n) -> p k n", k=8)[:, :, at:at + n], wsrc(w, c0, n)))
                at += n
            i, v, tok = load(parts)
            return i, v[:, 0:8 * width].rearrange("p (k n) -> p k n", k=8), tok

        def proj(lhs, rhs, nk, t0, t1, *deps, perk=None, M=128):
            b, pv, free = banks.take()
            n = t1 - t0
            tok = None
            for c0 in range(0, n, 512):
                c1 = min(c0 + 512, n)
                for k in range(nk):
                    tok = mm(pv[0:M, c0:c1], lhs(k), rhs(k, t0 + c0, t0 + c1), k == 0, k == nk - 1,
                             free, deps, perk[k] if perk else None)
            return b, pv, tok

        def hx(k, t0, t1):
            return HT[:, k, t0:t1]

        t_c = small([(CC[:, :, :], con["base"].rearrange("p (c n) -> p c n", c=4))])
        t_ones = ms(ones[:, :], 1.0)
        tk = ms(epsc, EPS)
        t_cols = ms(onec, 1.0)
        ST = A[:, 0:640].rearrange("p (c n) -> p c n", c=5)
        t_z = ms(A[:, 0:640], 0.0)

        def rows(ap, n):
            return ap.rearrange("(r n) -> r n", n=128) if len(ap.shape) == 1 else ap

        spots = {}
        items = []
        fill = [0] * 5

        def put(col, key, ap, n):
            spots[key] = (col, fill[col], n)
            items.append((ST[fill[col]:fill[col] + n, col, :], ap))
            fill[col] += n

        r128 = "(r n) -> r n"
        put(0, "ln_g", a["ln_g"].rearrange("a b (r n) -> (a b r) n", n=128), 32)
        put(0, "ln_b", a["ln_b"].rearrange("a b (r n) -> (a b r) n", n=128), 32)
        put(0, "npre", a["norm_pre_2"].rearrange("o b (r n) -> (o b r) n", n=128), 24)
        put(0, "npost", a["norm_post_2"].rearrange("o b (r n) -> (o b r) n", n=128), 24)
        put(1, "mod_b", a["mod_b"].rearrange("a (r n) -> (a r) n", n=128), 96)
        put(2, "b_ada", a["b_ada_2"].rearrange("a (r n) -> (a r) n", n=128), 72)
        put(2, "c", a["c"].rearrange("a (r n) -> (a r) n", n=128), 8)
        put(2, "c_ctx", a["c_ctx"].rearrange(r128, n=128), 8)
        put(2, "c2", a["c_2"].rearrange("a (r n) -> (a r) n", n=128), 8)
        put(2, "c_ctx2", a["c_ctx_2"].rearrange(r128, n=128), 8)
        put(3, "conv_w", a["ssd_conv_w"].rearrange("o k (r n) -> (o k r) n", n=128), 120)
        put(4, "gla_b", a["gla_b_gate"].rearrange("o d (r n) -> (o d r) n", n=128), 4)
        put(4, "gla_n", a["gla_norm_w"], 1)
        put(4, "diff_n", a["diff_norm_w"], 1)
        put(4, "conv_b", a["ssd_conv_b"].rearrange("o (r n) -> (o r) n", n=128), 24)
        put(4, "ssd_n", a["ssd_norm_w"].rearrange("o (r n) -> (o r) n", n=128), 16)
        put(4, "lbf", a["hgrn_lb_fwd_2"].rearrange("o (r n) -> (o r) n", n=128), 8)
        put(4, "lbb", a["hgrn_lb_bwd_2"].rearrange("o (r n) -> (o r) n", n=128), 8)
        put(4, "hgn", a["hgrn_norm_2"].rearrange("o (r n) -> (o r) n", n=128), 4)
        t_st = small(items, t_z)
        b, pv, free = banks.take()
        for c in range(5):
            tk = tr(pv[:, c * 128:(c + 1) * 128], ST[:, c, :], t_st, t_c, free)
        t_vec = cpV(VEC[:, :, :], pv[:, 0:640].rearrange("p (c n) -> p c n", c=5), tk)
        banks.free[b] = [t_vec]

        def vec(key, i=0, n=1):
            c, r, _ = spots[key]
            return VEC[:, c, r + i:r + i + n]

        CS = SM[:, 0:32].rearrange("p (k v) -> p k v", v=4)
        t_cs = None
        for v, key in enumerate(("c", "c_ctx", "c2", "c_ctx2")):
            t_cs = act(CS[:, :, v], vec(key, 0, 8), ACT.Silu, t_vec)

        def load_tokens(src, ntile, t0, scale, *deps):
            stage = A[:, 1024:1024 + ntile * D].rearrange("p (i c) -> p i c", c=D)
            tl = small([(stage, src.rearrange("o (i p) c -> p (o i) c", p=128))], *deps)
            last = []
            for k in range(8):
                b, pv, free = banks.take()
                for i in range(ntile):
                    tk = tr(pv[:, i * 128:(i + 1) * 128], stage[:, i, k * 128:(k + 1) * 128], tl, free, t_c)
                tok = act(XT[:, k, t0:t0 + ntile * 128], pv[:, 0:ntile * 128], ACT.Copy, tk, deps, scale=scale)
                banks.free[b] = [tok]
                last.append(tok)
            return last

        l1 = load_tokens(a["x"], 4, TC, ALPHA)
        l2 = load_tokens(a["ctx"], 2, 0, ALPHA, l1)
        xt = [[p, q] for p, q in zip(l1, l2)]

        def mods(w, M, ntile, v0, bias, *deps):
            rb = Slots([TM[0:2, 0:512], TM[0:2, 512:1024]])
            rb.free = [list(deps), list(deps)]
            tok = None
            for c in range(ntile // 4):
                i, wv, tw = wpanel((w, c * 512, 512))
                b, pv, free = banks.take()
                for k in range(8):
                    tk = mm(pv[0:2, 0:512], CS[:, k, v0:v0 + 2], wv[:, k, :], k == 0, k == 7, tw, free, t_cs)
                ring.free[i] = [tk]
                r, rv, rfree = rb.take()
                tcp = copyS(rv, pv[0:2, 0:512], tk, rfree)
                for q in range(4):
                    tk = mm(pv[:, 512 + 2 * q:514 + 2 * q], rv[:, q * 128:(q + 1) * 128], ident[0:2, 0:2], True, True,
                            tcp)
                rb.free[r] = [tk]
                tok = tt(M[:, 4 * c:4 * c + 4, :], pv[:, 512:520].rearrange("p (q v) -> p q v", v=2),
                         bias(4 * c).unsqueeze(2).to_broadcast([128, 4, 2]), ALU.add, tk, t_vec)
                banks.free[b] = [tcp, tok]
            return tok

        PX = [(0, TC, 1), (TC, T, 0)]
        XX = [(TC, T, 0)]

        def ln_layer(l, M, *deps):
            tk = None
            for j in (1, 4):
                tk = ts(M[:, 8 * j:8 * j + 8, :], M[:, 8 * j:8 * j + 8, :], 1.0, 1.0 / ALPHA, ALU.add, ALU.mult, *deps)
            return tk

        sq = Slots([TM[:, 1024:1536], TM[:, 1536:2048], TM[:, 2048:2560]])
        RS = TM[:, 2560:3072]

        def rstd(src, nk, t0, t1, div, *deps, perk=None):
            n = t1 - t0
            b, pv, free = banks.take()
            for k in range(nk):
                s, sv, sfree = sq.take()
                tq = act(sv[:, 0:n], src(k, t0, t1), ACT.Square, sfree, deps, perk[k] if perk else None)
                tk = mm(pv[:, 0:n], ones[:, :], sv[:, 0:n], k == 0, k == nk - 1, tq, free, t_ones, inc=True)
                sq.free[s] = [tk]
            t1_ = act(pv[:, 512:512 + n], pv[:, 0:n], ACT.Sqrt, tk, t_cols, bias=epsc, scale=1.0 / div)
            t2 = rcp(RS[:, 0:n], pv[:, 512:512 + n], t1_)
            banks.free[b] = [t2]
            return t2

        def layer_norm(l, j, parts, scale, M, mj, xt):
            new, ht = [[] for _ in range(8)], [[] for _ in range(8)]
            gb = SM[:, 32:48]
            tg = ts(gb[:, 0:8], vec("ln_g", (2 * l + j) * 8, 8), scale, None, ALU.mult, None, *bar())
            tb = ts(gb[:, 8:16], vec("ln_b", (2 * l + j) * 8, 8), scale, None, ALU.mult, None)
            for t0, t1, ci in parts:
                n = t1 - t0
                b, pv, free = banks.take()
                for k in range(8):
                    tk = mm(pv[:, 0:n], ones[:, :], XT[:, k, t0:t1], k == 0, k == 7, xt[k], free)
                sub = []
                for k in range(8):
                    sub.append([stt(XT[:, k, t0:t1], pv[:, 0:n], -1.0 / D, XT[:, k, t0:t1], ALU.mult, ALU.add, tk)])
                banks.free[b] = sub[-1]
                tr_ = rstd(lambda k, t0, t1: XT[:, k, t0:t1], 8, t0, t1, D, perk=sub)
                for k in range(8):
                    ta = tt(XT[:, k, t0:t1], XT[:, k, t0:t1], RS[:, 0:n], ALU.mult, tr_)
                    tc = act(XT[:, k, t0:t1], XT[:, k, t0:t1], ACT.Identity, ta, tb,
                             scale=gb[:, k:k + 1], bias=gb[:, 8 + k:9 + k])
                    new[k].append(tc)
                    if mj is not None:
                        ht[k].append(ts(HT[:, k, t0:t1], XT[:, k, t0:t1], M[:, 8 * (mj + 1) + k, ci:ci + 1],
                                        M[:, 8 * mj + k, ci:ci + 1], ALU.mult, ALU.add, tc))
            return new, ht

        def modulate(parts, M, mj, xt, *deps):
            ht = [[] for _ in range(8)]
            for t0, t1, ci in parts:
                for k in range(8):
                    ht[k].append(ts(HT[:, k, t0:t1], XT[:, k, t0:t1], M[:, 8 * (mj + 1) + k, ci:ci + 1],
                                    M[:, 8 * mj + k, ci:ci + 1], ALU.mult, ALU.add, xt[k], *deps))
            return ht

        def ffn(w_in, w_out, t0, ht, done):
            H = A[:, 0:FT * T].rearrange("p (f t) -> p f t", t=T)
            n = T - t0
            hid = []
            tg = tu = None
            start = bar()
            for c in range(11):
                i, wv, tw = wpanel((w_in, c * 256, 256), (w_in, FF + c * 256, 256))
                for f in range(2):
                    bg, pg, tg = proj(lambda k: wv[:, k, f * 128:f * 128 + 128], hx, 8, t0, T, tw, perk=ht)
                    bu, pu, tu = proj(lambda k: wv[:, k, 256 + f * 128:384 + f * 128], hx, 8, t0, T, tw)
                    h = H[:, 2 * c + f, 0:n]
                    ta = act(h, pg[:, 0:n], ACT.Silu, tg, start)
                    banks.free[bg] = [ta]
                    tm = tt(h, h, pu[:, 0:n], ALU.mult, ta, tu)
                    banks.free[bu] = [tm]
                    hid.append([tm])
                ring.free[i] = [tu]
            res = []
            for m in range(8):
                i, v, tw = load([(lambda v: v[:, 0:FF].rearrange("p (k n) -> p k n", k=FT),
                                  w_out[:, m * 128:(m + 1) * 128].rearrange("(k p) n -> p k n", p=128))])
                wv = v[:, 0:FF].rearrange("p (k n) -> p k n", k=FT)
                b, pv, tk = proj(lambda k: wv[:, k, :], lambda k, a0, a1: H[:, k, a0 - t0:a1 - t0], FT, t0, T, tw,
                                 perk=hid)
                ring.free[i] = [tk]
                res.append(done(m, pv, tk))
                banks.free[b] = res[-1]
            return res

        def residual(M, gj, parts, t0):
            def done(m, pv, tk):
                return [stt(XT[:, m, p0:p1], pv[:, p0 - t0:p1 - t0], M[:, 8 * gj + m, ci:ci + 1], XT[:, m, p0:p1],
                            ALU.mult, ALU.add, tk) for p0, p1, ci in parts]
            return done

        def dump(view, k):
            if dbg is not None and STOP == k:
                n = view.free_size() if callable(view.free_size) else view.free_size
                tk = Y.dma(lambda e: e.dma_start(dbg[:, 0:n], view), osem, cnt, bar())
                return True
            return False

        def layer0(xt):
            w = a["ev_w_in"][0]
            tm0 = mods(a["mod_w"][0], M0, 48, 0, lambda c: vec("mod_b", c, 4))
            tm0 = ln_layer(0, M0, tm0)
            ht = modulate(PX, M0, 0, xt, tm0)
            MIX = A[:, 0:6144].rearrange("p (m t) -> p m t", t=T)
            if dump(HT[:, :, :], 1):
                return None, None

            def u(i, n=1):
                return A[:, (8 + i) * T:(8 + i + n) * T]
            start = bar()
            W2 = TM[0:32, 3072:3584].rearrange("p (d n) -> p d n", d=2)
            t0_ = ms(TM[0:32, 3072:3584], 0.0, start)
            tw2 = small([(W2[0:16, 0, :], a["gla_w_gate2"][0, 0]), (W2[16:32, 1, :], a["gla_w_gate2"][0, 1])], t0_)
            MK = TM[:, 3584:3840].rearrange("p (d n) -> p d n", d=2)
            tmk = small([(MK, con["glam"].rearrange("p (d n) -> p d n", d=2))], start)
            RST = TM[:, 3840:4608]
            tq = ms(RST, 1.0, start)
            trs = ms(RST.rearrange("p (c t) -> p c t", t=64)[:, :, 0], 0.0, tq)
            R = u(0)
            i, wv, tw = wpanel((w, 1536, 32))
            b, pv, tk = proj(lambda k: wv[:, k, :], hx, 8, 0, T, tw, perk=ht, M=32)
            ring.free[i] = [tk]
            t_r = copyS(R[0:32, :], pv[0:32, 0:T], tk, start)
            banks.free[b] = [t_r]
            for j in range(2):
                start = bar()
                q, k_ = u(1), u(2)
                vt = u(3, 2).rearrange("p (c n) -> p c n", c=6)
                qd, kd = (u(5), u(6)), (u(7), u(8))
                klT = (u(9).rearrange("p (c n) -> p c n", c=6), u(10).rearrange("p (c n) -> p c n", c=6))
                SS = (u(11, 2).rearrange("p (c n) -> p c n", c=12), u(13, 2).rearrange("p (c n) -> p c n", c=12))
                la, kl, bb = u(15), u(16), u(17)
                dec = (SM[:, 48:60], SM[:, 60:72])
                i, wv, tw = wpanel((w, 128 * j, 128), (w, 256 + 128 * j, 128), (w, 512 + 256 * j, 256))
                b, pv, tk = proj(lambda k: wv[:, k, 0:128], hx, 8, 0, T, tw)
                t_q = act(q, pv[:, 0:T], ACT.Copy, tk, start, scale=0.125)
                banks.free[b] = [t_q]
                b, pv, tk = proj(lambda k: wv[:, k, 128:256], hx, 8, 0, T, tw)
                t_k = copyS(k_, pv[:, 0:T], tk, start)
                banks.free[b] = [t_k]
                t_v = []
                for c in range(6):
                    b, pv, free = banks.take()
                    for k in range(8):
                        tk = mm(pv[:, 0:256], HT[:, k, c * 128:(c + 1) * 128], wv[:, k, 256:512], k == 0, k == 7, tw,
                                free)
                    t_v.append(copyS(vt[:, c, :], pv[:, 0:256], tk, start))
                    banks.free[b] = [t_v[-1]]
                ring.free[i] = [tk]
                t_qd, t_kd, t_klT, t_S = [], [], [], []
                tprev = None
                for d in range(2):
                    b, pv, tk = proj(lambda k: W2[:, d, 128 * j:128 * j + 128], lambda k, a0, a1: R[0:32, a0:a1], 1,
                                     0, T, t_r, tw2)
                    tz = ts(la, pv[:, 0:T], vec("gla_b", 2 * d + j), None, ALU.add, None, tk, start, tprev)
                    banks.free[b] = [tz]
                    te = act(kl, la, ACT.Abs, tz, tprev)
                    te = act(kl, kl, ACT.Exp, te, scale=-1.0)
                    te = act(kl, kl, ACT.Ln, te, t_cols, bias=onec)
                    te = stt(la, la, 0.0, kl, ALU.min, ALU.subtract, te)
                    sl = slice(None, None, 1 if d == 0 else -1)
                    tb = V.do(lambda e, o=bb[:, sl], i_=la[:, sl]: e.tensor_tensor_scan(
                        out=o, data0=RST, data1=i_, initial=0.0, op0=ALU.mult, op1=ALU.add), te, trs, tprev)
                    b3 = bb.rearrange("p (c t) -> p c t", t=64)
                    bl = b3[:, :, 63:64] if d == 0 else b3[:, :, 0:1]
                    tdec = act(dec[d], bl.squeeze(2), ACT.Exp, tb, start, scale=1 / 16)
                    tl = tt(la.rearrange("p (c t) -> p c t", t=64), bl.to_broadcast([128, 12, 64]), b3, ALU.subtract, tb)
                    te = act(qd[d], bb, ACT.Exp, tb, start, scale=1 / 16)
                    t_qd.append(tt(qd[d], qd[d], q, ALU.mult, te, t_q))
                    te = act(kd[d], bb, ACT.Exp, tb, start, scale=-1 / 16)
                    t_kd.append(tt(kd[d], kd[d], k_, ALU.mult, te, t_k))
                    te = act(kl, la, ACT.Exp, tl, scale=1 / 16)
                    tl = tt(kl, kl, k_, ALU.mult, te, t_k)
                    b, pv, free = banks.take()
                    for c in range(6):
                        tk = tr(pv[:, c * 128:(c + 1) * 128], kl[:, c * 128:(c + 1) * 128], tl, free)
                    tc = cpV(klT[d], pv[:, 0:T].rearrange("p (c n) -> p c n", c=6), tk, start)
                    t_klT.append(tc)
                    banks.free[b] = [tc]
                    tprev = [tk, tdec, te, tc]
                    order = list(range(12)) if d == 0 else [3, 2, 1, 0] + list(range(11, 3, -1))
                    tS = ms(SS[d][:, order[0], :], 0.0, start)
                    allS = {order[0]: tS}
                    for x in range(11):
                        c, nx = order[x], order[x + 1]
                        h0 = 64 * (c % 2)
                        b, pv, free = banks.take()
                        tk = mm(pv[:, 0:256], klT[d][h0:h0 + 64, c // 2, :], vt[h0:h0 + 64, c // 2, :], True, True,
                                tc, t_v[c // 2], free)
                        for hh in range(2):
                            r = slice(64 * hh, 64 * hh + 64)
                            tS = stt(SS[d][r, nx, :], SS[d][r, c, :], dec[d][r, c:c + 1],
                                     pv[r, 128 * hh:128 * hh + 128], ALU.mult, ALU.add, tk, tS, tdec)
                        banks.free[b] = [tS]
                        allS[nx] = tS
                    t_S.append(allS)
                i, wg, tw = wpanel((w, 1024 + 256 * j, 256))
                at = Slots([TM[:, 0:1024], G0[:, :, :].rearrange("p a b -> p (a b)")])
                at.free = [list(start), list(start)]
                for hh in range(2):
                    r = slice(64 * hh, 64 * hh + 64)
                    h = 2 * j + hh
                    for p0, p1, ci in PX:
                        n = p1 - p0
                        bo, po, freeo = banks.take()
                        b, pv, free = banks.take()
                        cc0 = p0 // 128
                        for c in range(cc0, p1 // 128):
                            cs = slice(128 * c, 128 * c + 128)
                            for d in range(2):
                                o = 256 * (c - cc0) + 128 * d
                                tk = mm(pv[:, o:o + 128], kd[d][r, cs], qd[d][r, cs], True, True, free,
                                        t_kd[d], t_qd[d])
                        s, sv, sfree = at.take()
                        tm = None
                        for o in range(0, 2 * n, 512):
                            tm = tt(sv[:, o:o + 512].rearrange("p (c n) -> p c n", c=2),
                                    pv[:, o:o + 512].rearrange("p (c n) -> p c n", c=2),
                                    MK.rearrange("p d n -> p (d n)").unsqueeze(1).to_broadcast([128, 2, 256]),
                                    ALU.mult, tk, sfree, tmk)
                        banks.free[b] = [tm]
                        for c in range(cc0, p1 // 128):
                            o = slice(128 * (c - cc0), 128 * (c - cc0) + 128)
                            for d in range(2):
                                o1 = 256 * (c - cc0) + 128 * d
                                tk = mm(po[:, o], vt[:, c, 128 * hh:128 * hh + 128], sv[:, o1:o1 + 128],
                                        d == 0, False, tm, freeo)
                            for d in range(2):
                                for e2 in range(2):
                                    cc = 2 * c + e2
                                    o2 = slice(128 * (c - cc0) + 64 * e2, 128 * (c - cc0) + 64 * e2 + 64)
                                    tk = mm(po[:, o2], SS[d][r, cc, :], qd[d][r, 64 * cc:64 * cc + 64], False,
                                            d == 1 and e2 == 1, t_S[d][cc])
                        at.free[s] = [tk]
                        to = cpV(MIX[:, h, p0:p1], po[:, 0:n], tk, start)
                        banks.free[bo] = [to]
                        tr_ = rstd(lambda k, a0, a1: MIX[:, h, a0:a1], 1, p0, p1, 128, to)
                        tn = stt(MIX[:, h, p0:p1], RS[:, 0:n], vec("gla_n"), MIX[:, h, p0:p1], ALU.mult, ALU.mult, tr_)
                        b, pv, tk = proj(lambda k: wg[:, k, 128 * hh:128 * hh + 128], hx, 8, p0, p1, tw)
                        s, sv, sfree = sq.take()
                        tg = act(sv[:, 0:n], pv[:, 0:n], ACT.Silu, tk, sfree)
                        banks.free[b] = [tg]
                        tn = tt(MIX[:, h, p0:p1], MIX[:, h, p0:p1], sv[:, 0:n], ALU.mult, tg, tn)
                        sq.free[s] = [tn]
                ring.free[i] = [tk]
            start = bar()
            CO = u(6, 1)[:, 0:512]
            SI = u(7, 1)[:, 0:512]
            tcs = small([(CO, con["cos"]), (SI, con["sin"])], start)
            LP = SM[:, 0:256]
            LQ = TM[:, 3072:3328]
            tlp = small([(LQ, a["diff_lambda"][0].rearrange("a n -> (a n)").partition_broadcast(128))], start)
            l4 = LQ.rearrange("p (a n) -> p a n", a=4)
            tl = tt(LQ[:, 0:64], l4[:, 0, :], l4[:, 1, :], ALU.mult, tlp)
            tl2 = tt(LQ[:, 128:192], l4[:, 2, :], l4[:, 3, :], ALU.mult, tlp)
            lam = SM[:, 80:84]
            ta = V.do(lambda e: e.reduce_sum(lam[:, 0:1], LQ[:, 0:64], AX.X), tl)
            tb = V.do(lambda e: e.reduce_sum(lam[:, 1:2], LQ[:, 128:192], AX.X), tl2)
            tl = act(lam[:, 0:2], lam[:, 0:2], ACT.Exp, ta, tb)
            tl = tt(lam[:, 2:3], lam[:, 1:2], lam[:, 0:1], ALU.subtract, tl)
            lam_init = 0.8 - 0.6 * math.exp(0.0)
            t_lam = ts(lam[:, 2:3], lam[:, 2:3], lam_init, None, ALU.subtract, None, tl)
            for h in range(4):
                start = bar()
                qk = (u(0), u(1))
                raw, rt = u(2), u(3)
                vt = u(4).rearrange("p (c n) -> p c n", c=6)
                i, wv, tw = wpanel((w, 1568 + 128 * h, 128), (w, 2080 + 128 * h, 128), (w, 2592 + 128 * h, 128))
                t_qk = []
                tprev = None
                for x in range(2):
                    b, pv, tk = proj(lambda k: wv[:, k, 128 * x:128 * x + 128], hx, 8, 0, T, tw)
                    t1 = copyS(qk[x][:, 0:TC], pv[:, 0:TC], tk, start)
                    t2 = copyS(raw[:, 0:512], pv[:, TC:T], tk, start, tprev)
                    banks.free[b] = [t2]
                    b, pv, free = banks.take()
                    tk = mm(pv[:, 0:512], perm, raw[:, 0:512], True, True, t2, free)
                    t3 = tt(rt[:, 0:512], pv[:, 0:512], SI, ALU.mult, tk, tcs)
                    banks.free[b] = [t3]
                    t4 = tt(raw[:, 0:512], raw[:, 0:512], CO, ALU.mult, tk, tcs)
                    t5 = tt(qk[x][:, TC:T], raw[:, 0:512], rt[:, 0:512], ALU.add, t3, t4)
                    t_qk += [t1, t5]
                    tprev = t5
                t_v = []
                b, pv, free = banks.take()
                for c in range(6):
                    for k in range(8):
                        tk = mm(pv[:, c * 128:c * 128 + 128], HT[:, k, c * 128:(c + 1) * 128], wv[:, k, 256:384],
                                k == 0, k == 7, tw, free)
                ring.free[i] = [tk]
                t_v = copyS(vt, pv[:, 0:T].rearrange("p (c n) -> p c n", c=6), tk, start)
                banks.free[b] = [t_v]
                st = Slots([SM[:, 96:104], SM[:, 104:112]])
                es = Slots([(u(8), u(9)), (u(10), u(11))])
                wt = Slots([u(12), u(13)])
                st.free = [[start], [start]]
                es.free = [[start], [start]]
                wt.free = [[start], [start]]
                for p0, p1, ci in PX:
                    nk = TC if ci else T
                    bo = po = None
                    tof = []
                    for qt in range(p0 // 128, p1 // 128):
                        si, sv, sfree = st.take()
                        ei, ev, efree = es.take()
                        te = []
                        for x in range(2):
                            r = slice(64 * x, 64 * x + 64)
                            b, pv, free = banks.take()
                            for c0 in range(0, nk, 512):
                                c1 = min(c0 + 512, nk)
                                tk = mm(pv[:, c0:c1], qk[0][r, qt * 128:qt * 128 + 128], qk[1][r, c0:c1], True, True,
                                        free, t_qk)
                            t1 = V.do(lambda e, o=sv[:, x:x + 1], i_=pv[:, 0:nk]: e.reduce_max(o, i_, AX.X), tk, sfree)
                            t1 = ts(sv[:, 2 + x:3 + x], sv[:, x:x + 1], -0.125, None, ALU.mult, None, t1)
                            t2 = act(ev[x][:, 0:nk], pv[:, 0:nk], ACT.Exp, t1, efree, bias=sv[:, 2 + x:3 + x],
                                     scale=0.125, accum_out=sv[:, 4 + x:5 + x])
                            banks.free[b] = [t2]
                            te.append(t2)
                        t1 = rcp(sv[:, 6:8], sv[:, 4:6], te)
                        t2 = tt(sv[:, 7:8], sv[:, 7:8], lam[:, 2:3], ALU.mult, t1, t_lam)
                        t3 = ts(ev[1][:, 0:nk], ev[1][:, 0:nk], sv[:, 7:8], None, ALU.mult, None, t2)
                        t4 = stt(ev[0][:, 0:nk], ev[0][:, 0:nk], sv[:, 6:7], ev[1][:, 0:nk], ALU.mult, ALU.add, t3)
                        st.free[si] = [t4]
                        b, pv, free = banks.take()
                        for c in range(nk // 128):
                            tk = tr(pv[:, c * 128:c * 128 + 128], ev[0][:, c * 128:c * 128 + 128], t4, free)
                        es.free[ei] = [tk, t4]
                        wi, wvv, wfree = wt.take()
                        t5 = copyS(wvv[:, 0:nk], pv[:, 0:nk], tk, wfree)
                        banks.free[b] = [t5]
                        b, pv, free = banks.take()
                        for c in range(nk // 128):
                            tk = mm(pv[:, 0:128], vt[:, c, :], wvv[:, c * 128:c * 128 + 128], c == 0,
                                    c == nk // 128 - 1, t5, t_v, free)
                        wt.free[wi] = [tk]
                        to = cpV(MIX[:, 4 + h, qt * 128:qt * 128 + 128], pv[:, 0:128], tk, start)
                        banks.free[b] = [to]
                        tof.append(to)
                    tr_ = rstd(lambda k, a0, a1: MIX[:, 4 + h, a0:a1], 1, p0, p1, 128, tof)
                    tn = stt(MIX[:, 4 + h, p0:p1], RS[:, 0:p1 - p0], vec("diff_n"), MIX[:, 4 + h, p0:p1],
                             ALU.mult, ALU.mult, tr_)
                    tn = ts(MIX[:, 4 + h, p0:p1], MIX[:, 4 + h, p0:p1], 1.0 - lam_init, None, ALU.mult, None, tn)
            if dump(A[:, 0:6144], 2):
                return None, None
            start = bar()
            res = []
            for m2 in range(2):
                i, wv, tw = wpanel((a["ev_w_out"][0], 512 * m2, 512))
                for mm_ in range(4):
                    m = 4 * m2 + mm_
                    b, pv, tk = proj(lambda k: wv[:, k, mm_ * 128:mm_ * 128 + 128],
                                     lambda k, a0, a1: MIX[:, k, a0:a1], 8, 0, T, tw, start)
                    res.append(residual(M0, 2, PX, 0)(m, pv, tk))
                    banks.free[b] = res[-1]
                ring.free[i] = [tk]
            xt, ht = layer_norm(0, 0, PX, ALPHA, M0, 3, res)
            if dump(XT[:, :, :], 3):
                return None, None
            res = ffn(a["ffn_w_in"][0], a["ffn_w_out"][0], 0, ht, residual(M0, 5, PX, 0))
            tm1 = mods(a["mod_w"][1], M1, 48, 0, lambda c: vec("mod_b", 48 + c, 4), bar())
            ln_layer(1, M1, tm1)
            return layer_norm(0, 1, PX, ALPHA, M1, 0, res)

        def layer1(xt, ht):
            w = a["ssd_w_in"][0]
            start = bar()
            at = [0]

            def al(n, buf=A):
                at[0] += n
                return A[:, at[0] - n:at[0]]
            YT = al(8192).rearrange("p (m t) -> p m t", t=512)
            xs = al(3072).rearrange("p (c n) -> p c n", c=6)
            zz = al(2048).rearrange("p (c n) -> p c n", c=4)
            Bc = al(768)
            Cc = al(768)
            Bt = al(768).rearrange("p (c n) -> p c n", c=6)
            SS = al(4096).rearrange("p (d c n) -> p d c n", d=2, c=4)
            DT = TM[:, 0:384].rearrange("p (c h) -> p c h", c=6)
            DA = TM[:, 384:768].rearrange("p (c h) -> p c h", c=6)
            AC = TM[:, 768:1152].rearrange("p (c h) -> p c h", c=6)
            ED = TM[:, 1152:1536].rearrange("p (c h) -> p c h", c=6)
            EL = TM[:, 1536:1920].rearrange("p (c h) -> p c h", c=6)
            EA = TM[:, 1920:2304].rearrange("p (c h) -> p c h", c=6)
            row = TM[:, 2304:2464]
            tro = small([(row[:, 0:64], a["ssd_dt_bias"][0].rearrange("a n -> (a n)").partition_broadcast(128)),
                         (row[:, 64:128], a["ssd_a_log"][0].rearrange("a n -> (a n)").partition_broadcast(128)),
                         (row[:, 128:160], a["ssd_d"][0].partition_broadcast(128))], start)
            MN = TM[:, 2560:2816].rearrange("p (d n) -> p d n", d=2)
            tmn = small([(MN, con["minm"].rearrange("p (d n) -> p d n", d=2))], start)
            ta = act(row[:, 64:128], row[:, 64:128], ACT.Exp, tro)
            i, wv, tw = wpanel((w, 5120, 64))
            b, pv, free = banks.take()
            for c in range(6):
                for k in range(8):
                    tk = mm(pv[:, c * 64:c * 64 + 64], HT[:, k, c * 128:c * 128 + 128], wv[:, k, :], k == 0, k == 7,
                            tw, free, ht[k])
            ring.free[i] = [tk]
            p6 = pv[:, 0:384].rearrange("p (c h) -> p c h", c=6)
            t1 = tt(DT, p6, row[:, 0:64].unsqueeze(1).to_broadcast([128, 6, 64]), ALU.add, tk, tro, start)
            banks.free[b] = [t1]
            t2 = act(DA, DT, ACT.Abs, t1)
            t2 = act(DA, DA, ACT.Exp, t2, scale=-1.0)
            t2 = act(DA, DA, ACT.Ln, t2, bias=onec)
            t2 = stt(DT, DT, 0.0, DA, ALU.max, ALU.add, t2)
            t_dt = t2
            t2 = stt(DA, DT, -1.0, row[:, 64:128].unsqueeze(1).to_broadcast([128, 6, 64]), ALU.mult, ALU.mult, t2, ta)
            t_da = t2
            b, pv, free = banks.take()
            for c in range(6):
                mm(pv[:, c * 64:c * 64 + 32], triF, DA[:, c, 0:32], True, True, t2, free)
                mm(pv[:, c * 64 + 32:c * 64 + 64], triB, DA[:, c, 32:64], True, True)
                tk = mm(pv[:, 512 + c * 64:576 + c * 64], ones[:, :], DA[:, c, :], True, True)
            p6 = pv[:, 0:384].rearrange("p (c h) -> p c h", c=6)
            p7 = pv[:, 512:896].rearrange("p (c h) -> p c h", c=6)
            t1 = cpV(AC, p6, tk)
            t3 = act(ED, p7, ACT.Exp, tk, start)
            t4 = tt(EL, p7, AC, ALU.subtract, t1, t3)
            banks.free[b] = [t3, t4]
            t4 = act(EL, EL, ACT.Exp, t4)
            t_el = tt(EL, EL, DT, ALU.mult, t4)
            t_ea = act(EA, AC, ACT.Exp, t1, start)
            t_ac = [t1, t3]
            CV = TM[:, 2816:3592]
            cv = TM[:, 3592:4360]
            tz = ms(CV[:, :], 0.0, start)
            tcv = [tz]
            tfin = [start]

            def conv(b, pv, tk, ch, dst, *deps):
                t1 = copyS(CV[:, 2:258], pv[:, 0:TC], tk, tcv, deps)
                t2 = copyS(CV[:, 262:774], pv[:, TC:T], tk)
                banks.free[b] = [t2]
                prev = [t2]
                for o0, n, s0 in ((0, 256, 0), (256, 512, 260)):
                    for s in range(5):
                        wc = vec("conv_w", s * 24 + ch)
                        if s == 0:
                            prev = [ts(cv[:, o0:o0 + n], CV[:, s0 + s:s0 + s + n], wc, vec("conv_b", ch), ALU.mult,
                                       ALU.add, prev)]
                        else:
                            prev = [stt(cv[:, o0:o0 + n], CV[:, s0 + s:s0 + s + n], wc, cv[:, o0:o0 + n], ALU.mult,
                                        ALU.add, prev)]
                tcv[:] = prev
                ta = act(dst, cv, ACT.Silu, prev)
                tcv.append(ta)
                return ta

            for g in range(4):
                start = bar()
                i, wv, tw = wpanel((w, 4096 + 128 * g, 128), (w, 4608 + 128 * g, 128))
                tbc = []
                for x, dst in enumerate((Bc, Cc)):
                    b, pv, tk = proj(lambda k: wv[:, k, 128 * x:128 * x + 128], hx, 8, 0, T, tw)
                    tbc.append(conv(b, pv, tk, 16 + 4 * x + g, dst, start))
                ring.free[i] = [tk]
                b, pv, free = banks.take()
                for c in range(6):
                    tk = tr(pv[:, c * 128:c * 128 + 128], Bc[:, c * 128:c * 128 + 128], tbc[0], free)
                t_bt = cpV(Bt, pv[:, 0:T].rearrange("p (c n) -> p c n", c=6), tk, start)
                banks.free[b] = [t_bt]
                i, wv, tw = wpanel((w, 2048 + 512 * g, 512))
                t_xs = []
                for m in range(4):
                    b, pv, tk = proj(lambda k: wv[:, k, 128 * m:128 * m + 128], hx, 8, 0, T, tw)
                    dst = zz[:, 0:2, :].rearrange("p c n -> p (c n)")[:, 0:T]
                    tq = conv(b, pv, tk, 4 * g + m, dst, start, t_xs)
                    b, pv, free = banks.take()
                    for c in range(6):
                        tk2 = tr(pv[:, c * 128:c * 128 + 128], dst[:, c * 128:c * 128 + 128], tq, free)
                    tq = cpV(xs[:, :, m * 128:m * 128 + 128], pv[:, 0:T].rearrange("p (c n) -> p c n", c=6), tk2, start)
                    banks.free[b] = [tq]
                    t_xs.append(tq)
                    tcv.append(tk2)
                ring.free[i] = [tk]
                i, wv, tw = wpanel((w, 512 * g, 512))
                t_z = []
                for c in range(4):
                    b, pv, free = banks.take()
                    for k in range(8):
                        tk = mm(pv[:, 0:512], HT[:, k, TC + c * 128:TC + c * 128 + 128], wv[:, k, :], k == 0, k == 7,
                                tw, free)
                    t_z.append(act(zz[:, c, :], pv[:, 0:512], ACT.Silu, tk, t_xs))
                    banks.free[b] = [t_z[-1]]
                ring.free[i] = [tk]
                work = TM[:, 2816:4992]
                w1 = Slots([work[:, 0:512], work[:, 512:1024]])
                stt0 = bar()
                w1.free = [[stt0], [stt0]]
                cur = [work[:, 1024:1536], work[:, 1536:2048]]
                tS = {}

                def h8(v):
                    return v.rearrange("p (h n) -> p h n", h=8)

                def hb(v, n=64):
                    return v.unsqueeze(2).to_broadcast([128, 8, n])
                for d in range(2):
                    order = [0, 1, 2, 3, 4] if d == 0 else [1, 0, 5, 4, 3]
                    stop_at = order[-1]
                    hs = slice(32 * d + 8 * g, 32 * d + 8 * g + 8)
                    prev = None
                    src = None
                    for x, c in enumerate(order):
                        wi, wvv, wfree = w1.take()
                        t1 = tt(h8(wvv), h8(xs[:, c, :]), hb(EL[:, c, hs]), ALU.mult, wfree, t_xs, t_el)
                        b, pv, free = banks.take()
                        tk = mm(pv[:, 0:512], Bt[:, c, :], wvv, True, True, t1, t_bt, free)
                        w1.free[wi] = [tk]
                        nx = (order + [5 if d == 0 else 2])[x + 1]
                        dst = SS[:, d, nx - 2, :] if nx >= 2 else cur[d]
                        if src is None:
                            prev = cpV(dst, pv[:, 0:512], tk, start)
                        else:
                            t2 = tt(h8(dst), h8(src), hb(ED[:, c, hs]), ALU.mult, prev, t_ac, start)
                            prev = tt(dst, dst, pv[:, 0:512], ALU.add, t2, tk)
                        banks.free[b] = [prev]
                        src = dst
                        tS[(d, nx)] = prev
                t_out = []
                end = bar()
                xd = work[:, 0:512]
                GG = (G0[:, :, :], al(1024).rearrange("p (h n) -> p h n", h=8) if g == 0 else GG[1])
                for c in range(2, 6):
                    cs = slice(c * 128, c * 128 + 128)
                    b, pv, free = banks.take()
                    tcb = mm(pv[:, 0:128], Bc[:, cs], Cc[:, cs], True, True, free, tbc)
                    tcb = copyS(work[:, 1024:1152], pv[:, 0:128], tcb, end, t_out)
                    banks.free[b] = [tcb]
                    cbt = work[:, 1024:1152]
                    tG = []
                    for d in range(2):
                        hs0 = 32 * d + 8 * g
                        tri = triF if d == 0 else triB
                        b, pv, free = banks.take()
                        for h in range(8):
                            tk = mm(pv[:, 128 * h:128 * h + 128],
                                    DA[:, c, hs0 + h:hs0 + h + 1].to_broadcast([128, 128]), tri, True, True, free,
                                    t_da)
                        for h in range(8):
                            t1 = stt(GG[d][:, h, :], pv[:, 128 * h:128 * h + 128], AC[:, c, hs0 + h:hs0 + h + 1],
                                     MN[:, d, :], ALU.subtract, ALU.min, tk, t_ac, tmn, t_out, end)
                        banks.free[b] = [t1]
                        t2 = act(GG[d], GG[d], ACT.Exp, t1)
                        tG.append(tt(GG[d], GG[d], cbt.unsqueeze(1).to_broadcast([128, 8, 128]), ALU.mult, t2, tcb))
                    y = YT[:, 4 * g:4 * g + 4, (c - 2) * 128:(c - 2) * 128 + 128]
                    yy = work[:, 1152:1664]
                    yo = work[:, 1664:2176]
                    txd = []
                    xdv = (work[:, 0:512], work[:, 512:1024])
                    for d in range(2):
                        hs = slice(32 * d + 8 * g, 32 * d + 8 * g + 8)
                        txd.append(tt(h8(xdv[d]), h8(xs[:, c, :]), hb(DT[:, c, hs]), ALU.mult, end, t_out, t_dt))
                    b, pv, free = banks.take()
                    for h in range(8):
                        for d in range(2):
                            tk = mm(pv[:, 64 * h:64 * h + 64], GG[d][:, h, :], xdv[d][:, 64 * h:64 * h + 64], d == 0,
                                    d == 1, tG, txd, free)
                    b2, pw, free2 = banks.take()
                    for d in range(2):
                        tk2 = mm(pw[:, 512 * d:512 * d + 512], Cc[:, cs], SS[:, d, c - 2, :], True, True,
                                 tS[(d, c)], free2)
                    t1 = tt(h8(yy), h8(pw[:, 0:512]), hb(EA[:, c, 8 * g:8 * g + 8]), ALU.mult, tk2, t_ea, t_out, end)
                    t2 = tt(h8(yo), h8(pw[:, 512:1024]), hb(EA[:, c, 32 + 8 * g:40 + 8 * g]), ALU.mult, tk2, t_out, end)
                    banks.free[b2] = [t1, t2]
                    t1 = tt(yy, yy, yo, ALU.add, t1, t2)
                    t1 = tt(yy, yy, pv[:, 0:512], ALU.add, t1, tk)
                    banks.free[b] = [t1]
                    t2 = tt(h8(yo), h8(xs[:, c, :]), hb(row[:, 128 + 8 * g:136 + 8 * g]), ALU.mult, t1, tro)
                    t1 = tt(yy, yy, yo, ALU.add, t1, t2)
                    t1 = tt(yy, yy, zz[:, c - 2, :], ALU.mult, t1, t_z)
                    rs = SM[:, 112:116]
                    t2 = act(yo, yy, ACT.Square, t1, accum_out=rs[:, 0:1])
                    t2 = act(rs[:, 1:2], rs[:, 0:1], ACT.Sqrt, t2, bias=epsc, scale=1.0 / 512)
                    t2 = rcp(rs[:, 2:3], rs[:, 1:2], t2)
                    t1 = ts(yy, yy, rs[:, 2:3], None, ALU.mult, None, t2)
                    b, pv, free = banks.take()
                    for m in range(4):
                        tk = tr(pv[:, m * 128:m * 128 + 128], yy[:, m * 128:m * 128 + 128], t1, free)
                    t3 = tt(y, pv[:, 0:512].rearrange("p (m t) -> p m t", m=4),
                            vec("ssd_n", 4 * g, 4).unsqueeze(2).to_broadcast([128, 4, 128]), ALU.mult, tk, start)
                    banks.free[b] = [t3]
                    t_out = [t3, tk]
                tzz = bar()
                t1 = ms(CV[:, 0:2], 0.0, tzz)
                t2 = ms(CV[:, 258:262], 0.0)
                t3 = ms(CV[:, 774:776], 0.0)
                tcv[:] = [t3, tzz]
            start = bar()
            if dump(A[:, 0:8192], 5):
                return None
            res = []
            wo = a["ssd_w_out"][0]
            for m in range(8):
                if m % 2 == 0:
                    i, v, tw = load([(lambda v: v[:, 0:4096].rearrange("p (k n) -> p k n", k=16),
                                      wo[:, m * 128:m * 128 + 256].rearrange("(k p) n -> p k n", p=128))])
                wv = v[:, 0:4096].rearrange("p (k n) -> p k n", k=16)
                o = 128 * (m % 2)
                b, pv, tk = proj(lambda k: wv[:, k, o:o + 128], lambda k, a0, a1: YT[:, k, a0 - TC:a1 - TC], 16, TC,
                                 T, tw, start)
                ring.free[i] = [tk]
                res.append(residual(M1, 2, XX, TC)(m, pv, tk))
                banks.free[b] = res[-1]
            xt, ht = layer_norm(1, 0, XX, ALPHA, M1, 3, res)
            res = ffn(a["ffn_w_in"][1], a["ffn_w_out"][1], TC, ht, residual(M1, 5, XX, TC))
            return layer_norm(1, 1, XX, 1.0, M1, None, res)[0]

        def pre(j, parts, xt):
            ht = [[] for _ in range(8)]
            start = bar()
            for t0, t1, ci in parts:
                gg = SM[:, 120:128]
                tg = ts(gg, M2[:, 8 * (3 * j + 1):8 * (3 * j + 1) + 8, ci], 1.0, None, ALU.add, None, start, ht)
                tg = tt(gg, gg, vec("npre", 8 * j, 8), ALU.mult, tg)
                tr_ = rstd(lambda k, a0, a1: XT[:, k, a0:a1], 8, t0, t1, D, perk=xt)
                for k in range(8):
                    ta = stt(HT[:, k, t0:t1], XT[:, k, t0:t1], gg[:, k:k + 1], RS[:, 0:t1 - t0], ALU.mult, ALU.mult,
                             tr_, start, tg)
                    ht[k].append(act(HT[:, k, t0:t1], HT[:, k, t0:t1], ACT.Identity, ta,
                                     bias=M2[:, 8 * 3 * j + k, ci:ci + 1]))
            return ht

        def post(j, parts, yt, wgt):
            xt = [[] for _ in range(8)]
            start = bar()
            for t0, t1, ci in parts:
                gg = SM[:, 128:136]
                tg = stt(gg, M2[:, 8 * (3 * j + 2):8 * (3 * j + 2) + 8, ci], wgt, vec("npost", 8 * j, 8), ALU.mult,
                         ALU.mult, start, xt)
                tr_ = rstd(lambda k, a0, a1: HT[:, k, a0:a1], 8, t0, t1, D, perk=yt)
                for k in range(8):
                    ta = stt(HT[:, k, t0:t1], HT[:, k, t0:t1], gg[:, k:k + 1], RS[:, 0:t1 - t0], ALU.mult, ALU.mult,
                             tr_, tg)
                    xt[k].append(tt(XT[:, k, t0:t1], XT[:, k, t0:t1], HT[:, k, t0:t1], ALU.add, ta))
            return xt

        def to_ht(t0):
            free = []

            def done(m, pv, tk):
                return [copyS(HT[:, m, t0:T], pv[:, 0:T - t0], tk)]
            return done

        def block2(xt):
            start = bar()
            l2 = load_tokens(a["ctx_2"], 2, 0, 1.0, start)
            xt = [x + [y] for x, y in zip(xt, l2)]
            tm = mods(a["w_ada_2"][0], M2, 72, 2, lambda c: vec("b_ada", c, 4), start)
            ht = pre(0, PX, xt)
            res = ffn(a["ffn1_w_in_2"][0], a["ffn1_w_out_2"][0], 0, ht, to_ht(0))
            xt = post(0, PX, res, 0.5)
            if dump(XT[:, :, :], 7):
                return
            ht = pre(1, PX, xt)
            w = a["mix_w_in_2"][0]
            start = bar()
            at = [0]

            def al(n):
                at[0] += n
                return A[:, at[0] - n:at[0]]
            OA = al(2048).rearrange("p (m t) -> p m t", t=512)
            OH = al(2048).rearrange("p (m t) -> p m t", t=512)
            base = at[0]
            CO, SI = al(512), al(512)
            WM = al(256).rearrange("p (d n) -> p d n", d=2)
            q = al(2048).rearrange("p (m t) -> p m t", t=512)
            kk = al(1536).rearrange("p (m t) -> p m t", t=768)
            vt = al(768).rearrange("p (c n) -> p c n", c=6)
            raw, rt = al(512), al(512)
            tcs = small([(CO, con["cos"]), (SI, con["sin"]), (WM, con["winm"].rearrange("p (d n) -> p d n", d=2))],
                        start)
            SK = SM[:, 136:144]
            tsk = small([(SK, a["attn_sink_2"][0].partition_broadcast(128))], start)
            tprev = [None]

            def rope(dst, t_raw):
                b, pv, free = banks.take()
                tk = mm(pv[:, 0:512], perm, raw, True, True, t_raw, free)
                t3 = tt(rt, pv[:, 0:512], SI, ALU.mult, tk, tcs)
                banks.free[b] = [t3]
                t4 = tt(raw, raw, CO, ALU.mult, tk)
                tprev[0] = tt(dst, raw, rt, ALU.add, t3, t4)
                return tprev[0]
            i, wv, tw = wpanel((w, 0, 512))
            t_q = []
            for m in range(4):
                b, pv, tk = proj(lambda k: wv[:, k, m * 128:m * 128 + 128], hx, 8, TC, T, tw, perk=ht)
                t1 = copyS(raw, pv[:, 0:512], tk, tprev[0], start)
                banks.free[b] = [t1]
                t_q.append(rope(q[:, m, :], t1))
            ring.free[i] = [tk]
            i, wv, tw = wpanel((w, 512, 64), (w, 512, 64), (w, 576, 64), (w, 576, 64), (w, 640, 128))
            t_k = []
            for m in range(2):
                b, pv, tk = proj(lambda k: wv[:, k, m * 128:m * 128 + 128], hx, 8, 0, T, tw, perk=ht)
                t_k.append(copyS(kk[:, m, 0:TC], pv[:, 0:TC], tk))
                t1 = copyS(raw, pv[:, TC:T], tk, tprev[0])
                banks.free[b] = [t1]
                t_k.append(rope(kk[:, m, TC:T], t1))
            b, pv, free = banks.take()
            for c in range(6):
                for k in range(8):
                    tk = mm(pv[:, c * 128:c * 128 + 128], HT[:, k, c * 128:c * 128 + 128], wv[:, k, 256:384], k == 0,
                            k == 7, tw, free)
            ring.free[i] = [tk]
            t_v = copyS(vt, pv[:, 0:T].rearrange("p (c n) -> p c n", c=6), tk, start)
            banks.free[b] = [t_v]
            st = Slots([SM[:, 144:152], SM[:, 152:160]])
            es = Slots([al(640), al(640)])
            wt = Slots([al(640), al(640)])
            oo = Slots([al(512), al(512)])
            for s_ in (st, es, wt, oo):
                s_.free = [[start], [start]]
            for n in range(4):
                lo = 0 if n > 0 else 128
                hi = 384 if n < 3 else 256
                nb = hi - lo
                nk = nb + TC
                oi, ov, ofree = oo.take()
                t_o = []
                for h in range(8):
                    kv = h // 4
                    r = slice(64 * (h % 2), 64 * (h % 2) + 64)
                    si, sv, sfree = st.take()
                    ei, ev, efree = es.take()
                    b, pv, free = banks.take()
                    k0 = TC + (n - 1) * 128 + lo
                    lq = q[r, h // 2, n * 128:n * 128 + 128]
                    mm(pv[:, 0:nb], lq, kk[r, kv, k0:k0 + nb], True, True, free, t_q, t_k)
                    tk = mm(pv[:, 512:768], lq, kk[r, kv, 0:TC], True, True)
                    ts_ = []
                    if n > 0:
                        ts_.append(stt(ev[:, 0:128], pv[:, 0:128], 0.125, WM[:, 0, :], ALU.mult, ALU.add, tk, efree, tcs))
                    mid = 128 - lo
                    ts_.append(ts(ev[:, mid:mid + 128], pv[:, mid:mid + 128], 0.125, None, ALU.mult, None, tk, efree))
                    if n < 3:
                        ts_.append(stt(ev[:, mid + 128:mid + 256], pv[:, mid + 128:mid + 256], 0.125, WM[:, 1, :],
                                       ALU.mult, ALU.add, tk, efree, tcs))
                    ts_.append(act(ev[:, nb:nk], pv[:, 512:768], ACT.Copy, tk, efree, scale=0.125))
                    banks.free[b] = ts_
                    t1 = V.do(lambda e, o=sv[:, 0:1], i_=ev[:, 0:nk]: e.reduce_max(o, i_, AX.X), ts_, sfree)
                    t1 = ts(sv[:, 1:2], sv[:, 0:1], SK[:, h:h + 1], -1.0, ALU.max, ALU.mult, t1, tsk)
                    t2 = act(ev[:, 0:nk], ev[:, 0:nk], ACT.Exp, t1, bias=sv[:, 1:2], accum_out=sv[:, 2:3])
                    t3 = act(sv[:, 3:4], SK[:, h:h + 1], ACT.Exp, t1, bias=sv[:, 1:2])
                    t4 = tt(sv[:, 4:5], sv[:, 2:3], sv[:, 3:4], ALU.add, t2, t3)
                    t4 = rcp(sv[:, 5:6], sv[:, 4:5], t4)
                    b, pv, free = banks.take()
                    for c in range(nk // 128):
                        tk = tr(pv[:, c * 128:c * 128 + 128], ev[:, c * 128:c * 128 + 128], t2, free)
                    es.free[ei] = [tk]
                    wi, wvv, wfree = wt.take()
                    t5 = cpV(wvv[:, 0:nk], pv[:, 0:nk], tk, wfree)
                    banks.free[b] = [t5]
                    b, pv, free = banks.take()
                    vc = [2 + n - 1 + (lo // 128) + c for c in range(nb // 128)] + [0, 1]
                    for x, c in enumerate(vc):
                        tk = mm(pv[:, 0:64], wvv[:, x * 128:x * 128 + 128], vt[:, c, 64 * kv:64 * kv + 64], x == 0,
                                x == len(vc) - 1, t5, t_v, free)
                    wt.free[wi] = [tk]
                    t6 = act(ov[:, 64 * h:64 * h + 64], pv[:, 0:64], ACT.Copy, tk, t4, ofree, scale=sv[:, 5:6])
                    banks.free[b] = [t6]
                    st.free[si] = [t6]
                    t_o.append(t6)
                b, pv, free = banks.take()
                for m in range(4):
                    tk = tr(pv[:, m * 128:m * 128 + 128], ov[:, m * 128:m * 128 + 128], t_o, free)
                oo.free[oi] = [tk]
                t7 = cpV(OA[:, :, n * 128:n * 128 + 128], pv[:, 0:512].rearrange("p (m t) -> p m t", m=4), tk, start)
                banks.free[b] = [t7]
            if dump(A[:, 0:2048], 8):
                return
            start = bar()
            at[0] = base
            MK = al(14 * 128).rearrange("p (d n) -> p d n", d=14)
            tmk = small([(MK, con["hgm"].rearrange("p (d n) -> p d n", d=14))], start)
            RST = al(768)
            t1 = ms(RST, 1.0, start)
            trs = ms(RST.rearrange("p (c t) -> p c t", t=128)[:, :, 0], 0.0, t1)
            LB = SM[:, 160:184]
            tl = []
            for d, key in enumerate(("lbf", "lbb")):
                x0, x1 = vec(key, 0, 4), vec(key, 4, 4)
                mx, e0, e1 = LB[:, 0:4], LB[:, 4:8], LB[:, 8:12]
                lb, om = LB[:, 12 + 4 * d:16 + 4 * d], SM[:, 184 + 4 * d:188 + 4 * d]
                t1 = tt(mx, x0, x1, ALU.max, start, tl)
                t2 = tt(e0, x0, mx, ALU.subtract, t1)
                t3 = tt(e1, x1, mx, ALU.subtract, t1)
                t2 = act(LB[:, 4:12], LB[:, 4:12], ACT.Exp, t2, t3)
                t3 = tt(e1, e0, e1, ALU.add, t2)
                t3 = rcp(e1, e1, t3)
                t3 = tt(lb, e0, e1, ALU.mult, t3)
                t4 = ts(om, lb, -1.0, 1.0, ALU.mult, ALU.add, t3)
                tl = [t4]
            q = al(512)
            kx = (al(768), al(768))
            bx = (al(768), al(768))
            vt = al(768).rearrange("p (c n) -> p c n", c=6)
            kl = al(768)
            klT = al(768).rearrange("p (c n) -> p c n", c=6)
            SS = al(8 * 128).rearrange("p (d c n) -> p d c n", d=2, c=4)
            cur = (al(128), al(128))
            SC = (al(512), al(512))
            EE = Slots([al(512), al(512)])
            QQ = Slots([al(512), al(512)])
            KK = Slots([al(512), al(512)])
            QB = (al(512), al(512))
            DC = SM[:, 192:204]
            for h in range(4):
                start = bar()
                for s_ in (EE, QQ, KK):
                    s_.free = [[start], [start]]
                c0 = 768 + 128 * h
                i, wv, tw = wpanel((w, c0, 128), (w, c0 + 512, 128), (w, c0 + 1024, 128), (w, c0 + 1536, 128))
                b, pv, tk = proj(lambda k: wv[:, k, 0:128], hx, 8, TC, T, tw, perk=ht)
                t_q = act(q, pv[:, 0:512], ACT.Silu, tk, start)
                banks.free[b] = [t_q]
                t_kb, t_S = [], []
                b, pv, free = banks.take()
                for c in range(6):
                    for k in range(8):
                        tk = mm(pv[:, c * 128:c * 128 + 128], HT[:, k, c * 128:c * 128 + 128], wv[:, k, 384:512],
                                k == 0, k == 7, tw, free)
                t_v = copyS(vt, pv[:, 0:T].rearrange("p (c n) -> p c n", c=6), tk, start)
                banks.free[b] = [t_v]
                pf = []
                for d in range(2):
                    b, pv, tk = proj(lambda k: wv[:, k, 128 + 128 * d:256 + 128 * d], hx, 8, 0, T, tw)
                    t1 = act(kx[d], pv[:, 0:T], ACT.Sigmoid, tk, start)
                    banks.free[b] = [t1]
                    t2 = ts(kl, kx[d], SM[:, 184 + 4 * d + h:185 + 4 * d + h], LB[:, 12 + 4 * d + h:13 + 4 * d + h],
                            ALU.mult, ALU.add, t1, tl, pf, start)
                    t3 = ts(kx[d], kl, -1.0, 1.0, ALU.mult, ALU.add, t2)
                    t4 = act(kl, kl, ACT.Ln, t3)
                    sl = slice(None, None, 1 if d == 0 else -1)
                    tb = V.do(lambda e, o=bx[d][:, sl], i_=kl[:, sl]: e.tensor_tensor_scan(
                        out=o, data0=RST, data1=i_, initial=0.0, op0=ALU.mult, op1=ALU.add), t4, trs, start)
                    b3 = bx[d].rearrange("p (c t) -> p c t", t=128)
                    bl = b3[:, :, 127:128] if d == 0 else b3[:, :, 0:1]
                    dec = DC[:, 6 * d:6 * d + 6]
                    tdec = act(dec, bl.squeeze(2), ACT.Exp, tb, start)
                    t5 = tt(kl.rearrange("p (c t) -> p c t", t=128), bl.to_broadcast([128, 6, 128]), b3, ALU.subtract,
                            tb)
                    t5 = act(kl, kl, ACT.Exp, t5)
                    t5 = tt(kl, kl, kx[d], ALU.mult, t5, t3)
                    b, pv, free = banks.take()
                    for c in range(6):
                        tk2 = tr(pv[:, c * 128:c * 128 + 128], kl[:, c * 128:c * 128 + 128], t5, free)
                    t6 = cpV(klT, pv[:, 0:T].rearrange("p (c n) -> p c n", c=6), tk2, pf, start)
                    banks.free[b] = [t6]
                    order = [0, 1, 2, 3, 4] if d == 0 else [1, 0, 5, 4, 3]
                    src, prev, allS = None, None, {}
                    for x, c in enumerate(order):
                        b, pv, free = banks.take()
                        tk2 = mm(pv[:, 0:128], klT[:, c, :], vt[:, c, :], True, True, t6, t_v, free)
                        nx = (order + [5 if d == 0 else 2])[x + 1]
                        dst = SS[:, d, nx - 2, :] if nx >= 2 else cur[d]
                        if src is None:
                            prev = cpV(dst, pv[:, 0:128], tk2, start)
                        else:
                            prev = stt(dst, src, dec[:, c:c + 1], pv[:, 0:128], ALU.mult, ALU.add, tk2, prev, tdec)
                        banks.free[b] = [prev]
                        src = dst
                        allS[nx] = prev
                    t_S.append(allS)
                    t_kb.append([t3, tb])
                    pf = [tk2, t5]
                ring.free[i] = [tk]
                t_sc = []
                for d in range(2):
                    tsc = None
                    first = True
                    for lv in range(8):
                        b, pv, free = banks.take()
                        if lv == 7:
                            for c in range(4):
                                tk = mm(pv[:, c * 128:c * 128 + 128], kx[d][:, TC + c * 128:TC + c * 128 + 128],
                                        q[:, c * 128:c * 128 + 128], True, True, free, t_kb[d], t_q)
                            mask = ident
                        else:
                            m = 64 >> lv
                            b4 = bx[d][:, TC:T].rearrange("p (c e m) -> p c e m", e=2, m=m)
                            nb = 512 // (2 * m)
                            ei, ev, efree = EE.take()
                            e4 = ev.rearrange("p (c e m) -> p c e m", e=2, m=m)
                            ref = b4[:, :, 0, m - 1:m] if d == 0 else b4[:, :, 1, 0:1]
                            ref = ref.to_broadcast([128, nb, m])
                            up, dn = (1, 0) if d == 0 else (0, 1)
                            t1 = tt(e4[:, :, up, :], b4[:, :, up, :], ref, ALU.subtract, efree, t_kb[d])
                            t2 = tt(e4[:, :, dn, :], ref, b4[:, :, dn, :], ALU.subtract)
                            t2 = act(ev, ev, ACT.Exp, t1, t2)
                            qi, qv, qfree = QQ.take()
                            ki, kv_, kfree = KK.take()
                            t3 = tt(qv, q, ev, ALU.mult, t2, qfree, t_q, eng=G)
                            t4 = tt(kv_, kx[d][:, TC:T], ev, ALU.mult, t2, kfree, t_kb[d])
                            EE.free[ei] = [t3, t4]
                            for c in range(4):
                                tk = mm(pv[:, c * 128:c * 128 + 128], kv_[:, c * 128:c * 128 + 128],
                                        qv[:, c * 128:c * 128 + 128], True, True, free, t3, t4)
                            QQ.free[qi] = [tk]
                            KK.free[ki] = [tk]
                            mask = MK[:, 7 * d + lv, :]
                        p4 = pv[:, 0:512].rearrange("p (c n) -> p c n", c=4)
                        s4 = SC[d].rearrange("p (c n) -> p c n", c=4)
                        mb = mask.unsqueeze(1).to_broadcast([128, 4, 128])
                        if first:
                            tsc = tt(s4, p4, mb, ALU.mult, tk, tmk, start)
                            first = False
                        else:
                            tsc = V.do(lambda e, o=s4, m_=mb.bitcast(U32), i_=p4: e.copy_predicated(o, m_, i_), tk, tsc)
                        banks.free[b] = [tsc]
                    t_sc.append(tsc)
                t_qb = []
                for d in range(2):
                    t1 = act(QB[d], bx[d][:, TC:T], ACT.Exp, t_kb[d], start)
                    t_qb.append(tt(QB[d], QB[d], q, ALU.mult, t1, t_q))
                b, pv, free = banks.take()
                for c in range(4):
                    cs = slice(c * 128, c * 128 + 128)
                    mm(pv[:, cs], vt[:, 2 + c, :], SC[0][:, cs], True, False, t_sc, free, t_v)
                    mm(pv[:, cs], vt[:, 2 + c, :], SC[1][:, cs], False, False)
                    mm(pv[:, cs], SS[:, 0, c, :], QB[0][:, cs], False, False, t_qb, t_S[0][c + 2], t_S[1][c + 2])
                    tk = mm(pv[:, cs], SS[:, 1, c, :], QB[1][:, cs], False, True)
                t1 = copyS(OH[:, h, :], pv[:, 0:512], tk, start)
                banks.free[b] = [t1]
                if h == 0:
                    t_oh = []
                t_oh.append([t1])
            if dump(A[:, 2048:4096], 9):
                return
            tr_ = rstd(lambda k, a0, a1: OH[:, k, a0 - TC:a1 - TC], 4, TC, T, 512, perk=t_oh)
            i, wv, tw = wpanel((w, 2816, 512))
            t_r = []
            start = bar()
            for m in range(4):
                ta = stt(OH[:, m, :], OH[:, m, :], vec("hgn", m), RS[:, 0:512], ALU.mult, ALU.mult, tr_)
                b, pv, tk = proj(lambda k: wv[:, k, m * 128:m * 128 + 128], hx, 8, TC, T, tw)
                s, sv, sfree = sq.take()
                tb = act(sv, pv[:, 0:512], ACT.Silu, tk, sfree)
                banks.free[b] = [tb]
                t_r.append(tt(OH[:, m, :], OH[:, m, :], sv, ALU.mult, ta, tb))
                sq.free[s] = [t_r[-1]]
            ring.free[i] = [tk]
            at[0] = base
            MG = al(4096).rearrange("p (m t) -> p m t", t=512)
            s1, s2 = Slots([al(512), al(512)]), Slots([al(512), al(512)])
            s1.free = [[start], [start]]
            s2.free = [[start], [start]]
            t_mg = []
            for m in range(8):
                if m % 2 == 0:
                    i, wv, tw = wpanel((w, 3328 + 128 * m, 256), (w, 4352 + 128 * m, 256))
                    i2, v2, tw2 = load([
                        (lambda v: v[:, 0:1024].rearrange("p (k n) -> p k n", k=4),
                         a["w_o_attn_2"][0][:, 128 * m:128 * m + 256].rearrange("(k p) n -> p k n", p=128)),
                        (lambda v: v[:, 1024:2048].rearrange("p (k n) -> p k n", k=4),
                         a["w_o_hgrn_2"][0][:, 128 * m:128 * m + 256].rearrange("(k p) n -> p k n", p=128))])
                o = 128 * (m % 2)
                res = []
                for x in range(2):
                    b, pv, tk = proj(lambda k: wv[:, k, 256 * x + o:256 * x + o + 128], hx, 8, TC, T, tw)
                    si, sv, sfree = (s1, s2)[x].take()
                    t1 = act(sv, pv[:, 0:512], ACT.Sigmoid, tk, sfree)
                    banks.free[b] = [t1]
                    vv = v2[:, 1024 * x:1024 * x + 1024].rearrange("p (k n) -> p k n", k=4)
                    src = (OA, OH)[x]
                    b, pv, tk = proj(lambda k: vv[:, k, o:o + 128], lambda k, a0, a1: src[:, k, a0 - TC:a1 - TC], 4,
                                     TC, T, tw2, t_r, start)
                    t2 = tt(sv, sv, pv[:, 0:512], ALU.mult, t1, tk)
                    banks.free[b] = [t2]
                    res.append((sv, t2, si))
                t3 = tt(MG[:, m, :], res[0][0], res[1][0], ALU.add, res[0][1], res[1][1], start)
                s1.free[res[0][2]] = [t3]
                s2.free[res[1][2]] = [t3]
                t_mg.append([t3])
                ring.free[i] = [tk]
                ring.free[i2] = [tk]
            res = []
            done = to_ht(TC)
            for m2 in range(2):
                i, wv, tw = wpanel((a["w_out_2"][0], 512 * m2, 512))
                for mm_ in range(4):
                    b, pv, tk = proj(lambda k: wv[:, k, mm_ * 128:mm_ * 128 + 128],
                                     lambda k, a0, a1: MG[:, k, a0 - TC:a1 - TC], 8, TC, T, tw, perk=t_mg)
                    res.append(done(4 * m2 + mm_, pv, tk))
                    banks.free[b] = res[-1]
                ring.free[i] = [tk]
            xt = post(1, XX, res, 1.0)
            ht = pre(2, XX, xt)
            res = ffn(a["ffn2_w_in_2"][0], a["ffn2_w_out_2"][0], TC, ht, to_ht(TC))
            xt = post(2, XX, res, 0.5)
            start = bar()
            stage = A[:, 0:4096].rearrange("p (i c) -> p i c", c=D)
            for k in range(8):
                b, pv, free = banks.take()
                for i in range(4):
                    tk = tr(pv[:, i * 128:i * 128 + 128], XT[:, k, TC + i * 128:TC + i * 128 + 128], xt[k], free)
                t1 = copyS(stage[:, :, k * 128:k * 128 + 128], pv[:, 0:512].rearrange("p (i n) -> p i n", i=4), tk,
                           start)
                banks.free[b] = [t1]
            for i in range(4):
                Y.dma(lambda e, i=i: e.dma_start(out[0, i * 128:i * 128 + 128, :], stage[:, i, :]), osem, cnt, t1)

        
        xt, ht = layer0(xt)
        if xt is not None and not dump(XT[:, :, :], 4):
            xt = layer1(xt, ht)
            if xt is not None and xt[0] is not None and not dump(XT[:, :, :], 6):
                block2(xt)
        Y.wait([(osem, cnt[id(osem)])])

        block = ctx.enter_context(nc.Block())

        @block.sync
        def _(eng):
            Y.emit(eng)

        @block.tensor
        def _(eng):
            P.emit(eng)

        @block.vector
        def _(eng):
            V.emit(eng)

        @block.scalar
        def _(eng):
            S.emit(eng)

        @block.gpsimd
        def _(eng):
            G.emit(eng)


def constants():
    i = np.arange(128)
    r, c = i[:, None], i[None, :]
    f = np.float32
    perm = np.zeros((128, 128), f)
    for m in range(128):
        if m % 32 < 16:
            perm[m + 16, m] = -1
        else:
            perm[m - 16, m] = 1
    base = np.concatenate([np.eye(128), r <= c, r >= c, perm], 1).astype(f)
    blk = r // 64 == c // 64
    glam = np.concatenate([blk & (r <= c), blk & (r >= c)], 1).astype(f)
    minm = np.concatenate([np.where(r <= c, 0, -1e30), np.where(r >= c, 0, -1e30)], 1).astype(f)
    winm = np.concatenate([np.where(c >= r, 0, -1e30), np.where(c <= r, 0, -1e30)], 1).astype(f)
    lv = []
    for m in (64, 32, 16, 8, 4, 2, 1):
        same = r // (2 * m) == c // (2 * m)
        lv.append(same & (r % (2 * m) < m) & (c % (2 * m) >= m))
    hgm = np.concatenate(lv + [x.T for x in lv], 1).astype(f)
    t = np.arange(512)
    inv = (f(10000.0) ** (-np.arange(16, dtype=f) / f(16))).astype(f)
    pos = np.stack([t // 64, t % 64]).astype(f)
    ang = np.empty((128, 512), f)
    for p in range(128):
        ang[p] = pos[(p // 32) % 2] * inv[p % 16]
    return {"base": base, "glam": glam, "minm": minm, "winm": winm, "hgm": hgm,
            "cos": np.cos(ang).astype(f), "sin": np.sin(ang).astype(f)}


def kernel(**inputs):
    import numpy as _np
    import concourse.bacc as _bacc
    from concourse import mybir as _mybir
    from concourse.bass_utils import run_bass_kernel_spmd as _run

    nc = _bacc.Bacc("TRN2", target_bir_lowering=False, num_devices=1)
    arrays, a, con = {}, {}, {}
    for name, x in inputs.items():
        x = _np.ascontiguousarray(x)
        arrays[f"in_{name}"] = x
        a[name] = nc.dram_tensor(f"in_{name}", x.shape, _mybir.dt.from_np(x.dtype), kind="ExternalInput").ap()
    for name, x in constants().items():
        arrays[f"con_{name}"] = x
        con[name] = nc.dram_tensor(f"con_{name}", x.shape, _mybir.dt.from_np(x.dtype), kind="ExternalInput").ap()
    out = nc.dram_tensor("out_0", (1, 512, 1024), _mybir.dt.float32, kind="ExternalOutput").ap()
    dbg = None
    if STOP < 99:
        dbg = nc.dram_tensor("dbg", (128, 8192), _mybir.dt.float32, kind="ExternalOutput").ap()
    program(nc, a, con, out, dbg)
    r = _run(nc, [arrays], core_ids=[0])
    return r.results[0]["out_0"]
```

```python
import math

import numpy as np
import concourse.bass as bass
from concourse import mybir

F = mybir.dt.float32
U32 = mybir.dt.uint32
FR = mybir.dt.float32r
ALU = mybir.AluOpType
ACT = mybir.ActivationFunctionType
AX = mybir.AxisListType
D = 1024
T = 768
TC = 256
ALPHA = 4 ** 0.25
EPS = 1e-6
NEG = -1e30
FF = 2816
FT = 22
STOP = 99


class Lane:

    def __init__(self, sem):
        self.sem, self.n, self.seen, self.list = sem, 0, {}, []

    def wait(self, deps):
        for d in deps:
            if isinstance(d, list) or isinstance(d, tuple) and not (len(d) == 2 and isinstance(d[1], int)):
                self.wait(d)
            elif d is not None:
                sem, val = d
                if self.seen.get(id(sem), 0) < val:
                    self.seen[id(sem)] = val
                    self.list.append((None, sem, val))

    def do(self, fn, *deps, inc=True):
        self.wait(deps)
        if not inc:
            self.list.append((fn, None, 0))
            return None
        self.n += 1
        self.list.append((fn, self.sem, 1))
        return (self.sem, self.n)

    def dma(self, fn, sem, counts, *deps):
        self.wait(deps)
        counts[id(sem)] = counts.get(id(sem), 0) + 16
        self.list.append((fn, sem, 16))
        return (sem, counts[id(sem)])

    def emit(self, eng):
        for fn, sem, val in self.list:
            if fn is None:
                eng.wait_ge(sem, val)
            else:
                ins = fn(eng)
                if sem is not None:
                    ins.then_inc(sem, val)


class Slots:

    def __init__(self, views):
        self.v, self.free, self.i = views, [[] for _ in views], -1

    def take(self):
        for _ in self.v:
            self.i = (self.i + 1) % len(self.v)
            free = self.free[self.i]
            if free is not None:
                self.free[self.i] = None
                return self.i, self.v[self.i], free
        raise RuntimeError("no buffer is free")


def weave(gens, width):
    gens, live = list(gens), []
    while gens or live:
        while gens and len(live) < width:
            live.append(gens.pop(0))
        for g in list(live):
            try:
                next(g)
            except StopIteration:
                live.remove(g)
                if gens:
                    live.append(gens.pop(0))


def program(nc, a, con, out, dbg=None):
    from contextlib import ExitStack
    ctx = ExitStack()
    with ctx:
        def sb(name, shape, dt=F):
            return ctx.enter_context(nc.sbuf_tensor(name, shape, dt))

        def sb2(name, shape):
            with nc.sbuf_tensor(name, shape, F) as f:
                pass
            return f, sb(name + "r", shape, FR)

        def sem(name):
            return ctx.enter_context(nc.semaphore(name))

        XT = sb("XT", [128, 8, T])
        HTF, HTL = sb2("HT", [128, 8, T])
        HTH = sb("HTH", [128, 8, T], FR)
        RWF, RWL = sb2("RW", [128, 4, 1024])
        RWH = sb("RWH", [128, 4, 1024], FR)
        A, AR = sb2("A", [128, 18432])
        TM = sb("TM", [128, 4992])
        VEC = sb("VEC", [128, 5, 128])
        M0 = sb("M0", [128, 48, 2])
        M1 = sb("M1", [128, 48, 2])
        M2 = sb("M2", [128, 72, 2])
        CC = sb("CC", [128, 4, 128])
        SM = sb("SM", [128, 512])
        PS = ctx.enter_context(nc.psum_tensor("PS", [128, 4096], F))
        ident, triF, triB, perm = (CC[:, i, :] for i in range(4))
        ones = sb("ones", [128, 128])
        cols = sb("cols", [128, 8])
        G0 = sb("G0", [128, 8, 128])
        epsc, onec = cols[:, 0:1], cols[:, 1:2]
        sems = [sem(n) for n in ("s_pe", "s_dve", "s_act", "s_pool")]
        wsem = [sem(f"s_w{i}") for i in range(4)]
        lsem = [sem(f"s_l{i}") for i in range(8)]
        osem = sem("s_out")
        t = dict(locals())
        for x in ("nc", "a", "con", "out", "dbg", "ctx", "sb", "sb2", "sem", "ExitStack", "sems"):
            t.pop(x)
        order = []
        body([Lane(x) for x in sems], Lane(None), t, a, con, out, dbg, order, False)
        lanes, Y = [Lane(x) for x in sems], Lane(None)
        body(lanes, Y, t, a, con, out, dbg, order, True)
        P, V, S, G = lanes

        block = ctx.enter_context(nc.Block())

        @block.sync
        def _(eng):
            Y.emit(eng)

        @block.tensor
        def _(eng):
            P.emit(eng)

        @block.vector
        def _(eng):
            V.emit(eng)

        @block.scalar
        def _(eng):
            S.emit(eng)

        @block.gpsimd
        def _(eng):
            G.emit(eng)


def body(lanes, Y, t, a, con, out, dbg, order, known):
    P, V, S, G = lanes
    XT, HTF, HTL, HTH, RWF, RWL, RWH, A, AR, TM, VEC, M0, M1, M2, CC, SM, PS = (t[x] for x in (
        "XT", "HTF", "HTL", "HTH", "RWF", "RWL", "RWH", "A", "AR", "TM", "VEC", "M0", "M1", "M2", "CC", "SM", "PS"))
    ident, triF, triB, perm, ones, G0, epsc, onec = (t[x] for x in (
        "ident", "triF", "triB", "perm", "ones", "G0", "epsc", "onec"))
    wsem, lsem, osem = t["wsem"], t["lsem"], t["osem"]
    if True:
        cnt = {}
        held = [[], [], [], []]
        banks = Slots([PS[:, 1024 * i:1024 * i + 1024] for i in range(4)])
        specs = list(order) if known else []
        loaded, ready = {}, {}
        asked = [0]

        def bar():
            return [(l.sem, l.n) for l in (P, V, S, G) if l.n]

        def fetch(n):
            i = n % 4
            kind, nk, width, cuts = specs[n]
            free = held[i]
            assert free is not None
            held[i] = None
            raw = RWF[:, i, 0:nk * width].rearrange("p (k n) -> p k n", k=nk)
            at, tok = 0, None
            for src, w_ in cuts:
                tok = Y.dma(lambda e, d=raw[:, :, at:at + w_], s_=src: e.dma_start(d, s_), wsem[i], cnt, free)
                at += w_
            loaded[n] = (raw, tok, free)

        def divide(n):
            i = n % 4
            kind, nk, width, _ = specs[n]
            raw, tok, free = loaded[n]
            if kind == "raw":
                ready[n] = (i, raw, None, tok)
                return
            fl = slice(0, nk * width)
            t1 = copyS(RWH[:, i, fl], RWF[:, i, fl], tok, free)
            t2 = tt(RWL[:, i, fl], RWF[:, i, fl], RWH[:, i, fl].bitcast(F), ALU.subtract, t1,
                    eng=V if n % 3 == 0 else G)
            ready[n] = (i, RWH[:, i, fl].rearrange("p (k n) -> p k n", k=nk),
                        RWL[:, i, fl].rearrange("p (k n) -> p k n", k=nk), t2)

        def panel(kind, nk, *cuts):
            n = asked[0]
            width = sum(w_ for _, w_ in cuts)
            assert nk * width <= 1024
            if known:
                assert specs[n][0:3] == (kind, nk, width)
            else:
                specs.append((kind, nk, width, cuts))
                order.append(specs[-1])
            if n not in loaded:
                fetch(n)
            if n not in ready:
                divide(n)
            asked[0] += 1
            return ready[n]

        def release(i, tok):
            held[i] = [tok]
            if known:
                for n in range(asked[0], min(asked[0] + 3, len(specs))):
                    if n in loaded and n not in ready:
                        divide(n)
                for n in range(asked[0], min(asked[0] + 4, len(specs))):
                    if n not in loaded:
                        if held[n % 4] is None:
                            break
                        fetch(n)

        def wp(w, c0, n, r0=0, nk=8):
            return (w[r0:r0 + nk * 128, c0:c0 + n].rearrange("(k p) n -> p k n", p=128), n)

        nl = [0]

        def small(pairs, *deps):
            s = lsem[nl[0] % 8]
            nl[0] += 1
            tok = None
            for dst, src in pairs:
                tok = Y.dma(lambda e, d=dst, s_=src: e.dma_start(d, s_), s, cnt, *deps)
            return tok

        def mm(o, l, r, start, stop, *deps, inc=None):
            return P.do(lambda e: e.matmul(o, l, r, start=start, stop=stop, skip_group_check=True), *deps,
                        inc=stop if inc is None else inc)

        def tr(o, i, *deps, n=128):
            return P.do(lambda e: e.transpose(o, i, ident[0:n, 0:n]), *deps)

        def act(o, i, f, *deps, **kw):
            return S.do(lambda e: e.activation(o, i, f, **kw), *deps)

        def copyS(o, i, *deps):
            return S.do(lambda e: e.activation(o, i, ACT.Copy), *deps)

        def tt(o, i0, i1, op, *deps, eng=None):
            return (eng or V).do(lambda e: e.tensor_tensor(out=o, in0=i0, in1=i1, op=op), *deps)

        def ts(o, i, s1, s2, op0, op1, *deps, eng=None):
            if op1 is None:
                return (eng or V).do(lambda e: e.tensor_scalar(out=o, in0=i, scalar1=s1, scalar2=None, op0=op0), *deps)
            return (eng or V).do(lambda e: e.tensor_scalar(out=o, in0=i, scalar1=s1, scalar2=s2, op0=op0, op1=op1), *deps)

        def stt(o, i0, s, i1, op0, op1, *deps):
            return V.do(lambda e: e.scalar_tensor_tensor(out=o, in0=i0, scalar=s, in1=i1, op0=op0, op1=op1), *deps)

        def cpV(o, i, *deps):
            return V.do(lambda e: e.tensor_copy(o, i), *deps)

        def rcp(o, i, *deps):
            return V.do(lambda e: e.reciprocal(o, i), *deps)

        def ms(o, val, *deps, eng=None):
            return (eng or V).do(lambda e: e.memset(o, val), *deps)

        def proj(lhs, rhs, nk, t0, t1, *deps, perk=None, M=128):
            b, pv, free = banks.take()
            n = t1 - t0
            tok = None
            for c0 in range(0, n, 512):
                c1 = min(c0 + 512, n)
                for k in range(nk):
                    tok = mm(pv[0:M, c0:c1], lhs(k), rhs(k, t0 + c0, t0 + c1), k == 0, k == nk - 1,
                             free, deps, perk[k] if perk else None)
            return b, pv, tok

        def mm3(o, lh, ll, rh, rl, k, nk, *deps):
            mm(o, lh, rh, k == 0, False, *deps)
            mm(o, lh, rl, False, False)
            return mm(o, ll, rh, False, k == nk - 1)

        def proj3(wh, wl, cs, x, nk, t0, t1, *deps, perk=None, M=128, k0=0):
            b, pv, free = banks.take()
            n = t1 - t0
            tok = None
            for c0 in range(0, n, 512):
                c1 = min(c0 + 512, n)
                for k in range(nk):
                    tok = mm3(pv[0:M, c0:c1], wh[:, k, cs], wl[:, k, cs], x[0](k, t0 + c0, t0 + c1),
                              x[1](k, t0 + c0, t0 + c1), k, nk, free, deps, perk[k] if perk else None)
            return b, pv, tok

        def lin(cuts, x, nk, t0, t1, *deps, perk=None, M=128):
            i, wh, wl, tw = panel("w", nk, *cuts)
            b, pv, tk = proj3(wh, wl, slice(0, M), x, nk, t0, t1, tw, *deps, perk=perk, M=M)
            release(i, tk)
            return b, pv, tk

        def halves(kind, w, c0):
            return [panel(kind, 4, wp(w, c0, 256, 512 * x, 4)) for x in range(2)]

        def xw(c0, hv, o, *deps):
            tok = None
            for k in range(8):
                _, wh, wl, tw = hv[k // 4]
                tok = mm3(o, HTH[:, k, c0:c0 + 128], HTL[:, k, c0:c0 + 128], wh[:, k % 4, :], wl[:, k % 4, :], k, 8,
                          tw, *deps)
            return tok

        def split(hi, lo, raw, *deps, eng=None):
            t1 = copyS(hi, raw, *deps)
            return tt(lo, raw, hi.bitcast(F), ALU.subtract, t1, eng=eng)

        hx = (lambda k, t0, t1: HTH[:, k, t0:t1], lambda k, t0, t1: HTL[:, k, t0:t1])

        t_c = small([(CC[:, :, :], con["base"].rearrange("p (c n) -> p c n", c=4))])
        t_ones = ms(ones[:, :], 1.0)
        ms(epsc, EPS)
        t_cols = ms(onec, 1.0)
        ST = A[:, 0:640].rearrange("p (c n) -> p c n", c=5)
        t_z = ms(A[:, 0:640], 0.0)

        def rows(ap, n):
            return ap.rearrange("(r n) -> r n", n=128) if len(ap.shape) == 1 else ap

        spots = {}
        items = []
        fill = [0] * 5

        def put(col, key, ap, n):
            spots[key] = (col, fill[col], n)
            items.append((ST[fill[col]:fill[col] + n, col, :], ap))
            fill[col] += n

        r128 = "(r n) -> r n"
        put(0, "ln_g", a["ln_g"].rearrange("a b (r n) -> (a b r) n", n=128), 32)
        put(0, "ln_b", a["ln_b"].rearrange("a b (r n) -> (a b r) n", n=128), 32)
        put(0, "npre", a["norm_pre_2"].rearrange("o b (r n) -> (o b r) n", n=128), 24)
        put(0, "npost", a["norm_post_2"].rearrange("o b (r n) -> (o b r) n", n=128), 24)
        put(1, "mod_b", a["mod_b"].rearrange("a (r n) -> (a r) n", n=128), 96)
        put(2, "b_ada", a["b_ada_2"].rearrange("a (r n) -> (a r) n", n=128), 72)
        put(2, "c", a["c"].rearrange("a (r n) -> (a r) n", n=128), 8)
        put(2, "c_ctx", a["c_ctx"].rearrange(r128, n=128), 8)
        put(2, "c2", a["c_2"].rearrange("a (r n) -> (a r) n", n=128), 8)
        put(2, "c_ctx2", a["c_ctx_2"].rearrange(r128, n=128), 8)
        put(3, "conv_w", a["ssd_conv_w"].rearrange("o k (r n) -> (o k r) n", n=128), 120)
        put(4, "gla_b", a["gla_b_gate"].rearrange("o d (r n) -> (o d r) n", n=128), 4)
        put(4, "gla_n", a["gla_norm_w"], 1)
        put(4, "diff_n", a["diff_norm_w"], 1)
        put(4, "conv_b", a["ssd_conv_b"].rearrange("o (r n) -> (o r) n", n=128), 24)
        put(4, "ssd_n", a["ssd_norm_w"].rearrange("o (r n) -> (o r) n", n=128), 16)
        put(4, "lbf", a["hgrn_lb_fwd_2"].rearrange("o (r n) -> (o r) n", n=128), 8)
        put(4, "lbb", a["hgrn_lb_bwd_2"].rearrange("o (r n) -> (o r) n", n=128), 8)
        put(4, "hgn", a["hgrn_norm_2"].rearrange("o (r n) -> (o r) n", n=128), 4)
        t_st = small(items, t_z)
        b, pv, free = banks.take()
        for c in range(5):
            tk = tr(pv[:, c * 128:(c + 1) * 128], ST[:, c, :], t_st, t_c, free)
        t_vec = cpV(VEC[:, :, :], pv[:, 0:640].rearrange("p (c n) -> p c n", c=5), tk)
        banks.free[b] = [t_vec]

        def vec(key, i=0, n=1):
            c, r, _ = spots[key]
            return VEC[:, c, r + i:r + i + n]

        CS = SM[:, 0:32].rearrange("p (k v) -> p k v", v=4)
        t_cs = None
        for v, key in enumerate(("c", "c_ctx", "c2", "c_ctx2")):
            t_cs = act(CS[:, :, v], vec(key, 0, 8), ACT.Silu, t_vec)

        def load_tokens(src, ntile, t0, scale, *deps):
            stage = A[:, 1024:1024 + ntile * D].rearrange("p (i c) -> p i c", c=D)
            tl = small([(stage, src.rearrange("o (i p) c -> p (o i) c", p=128))], *deps)
            last = []
            for k in range(8):
                b, pv, free = banks.take()
                for i in range(ntile):
                    tk = tr(pv[:, i * 128:(i + 1) * 128], stage[:, i, k * 128:(k + 1) * 128], tl, free, t_c)
                tok = act(XT[:, k, t0:t0 + ntile * 128], pv[:, 0:ntile * 128], ACT.Copy, tk, deps, scale=scale)
                banks.free[b] = [tok]
                last.append(tok)
            return last

        l1 = load_tokens(a["x"], 4, TC, ALPHA)
        l2 = load_tokens(a["ctx"], 2, 0, ALPHA, l1)
        xt = [[p, q] for p, q in zip(l1, l2)]

        rb = Slots([SM[0:2, 256:512]])

        def mod_step(w, M, c, v0, bias, *deps):
            hv = halves("raw", w, c * 256)
            b, pv, free = banks.take()
            for k in range(8):
                tk = mm(pv[0:2, 0:256], CS[:, k, v0:v0 + 2], hv[k // 4][1][:, k % 4, :], k == 0, k == 7, hv[k // 4][3], free,
                        t_cs)
            for x in hv:
                release(x[0], tk)
            r, rv, rfree = rb.take()
            tcp = copyS(rv, pv[0:2, 0:256], tk, rfree)
            for q in range(2):
                tk = mm(pv[:, 512 + 2 * q:514 + 2 * q], rv[:, q * 128:(q + 1) * 128], ident[0:2, 0:2], True, True, tcp)
            rb.free[r] = [tk]
            tok = tt(M[:, 2 * c:2 * c + 2, :], pv[:, 512:516].rearrange("p (q v) -> p q v", v=2),
                     bias(2 * c, 2).unsqueeze(2).to_broadcast([128, 2, 2]), ALU.add, tk, t_vec)
            banks.free[b] = [tcp, tok]
            return tok

        later = [(a["mod_w"][1], M1, c, 0, lambda x, n: vec("mod_b", 48 + x, n)) for c in range(24)]
        later += [(a["w_ada_2"][0], M2, c, 2, lambda x, n: vec("b_ada", x, n)) for c in range(36)]
        mod_tok = [None]

        def mod_some(n, M=None):
            while later and (n > 0 or later[0][1] is M):
                mod_tok[0] = mod_step(*later.pop(0))
                n -= 1
            return mod_tok[0]

        PX = [(0, TC, 1), (TC, T, 0)]
        XX = [(TC, T, 0)]

        def ln_layer(l, M, *deps):
            tk = None
            for j in (1, 4):
                tk = ts(M[:, 8 * j:8 * j + 8, :], M[:, 8 * j:8 * j + 8, :], 1.0, 1.0 / ALPHA, ALU.add, ALU.mult, *deps)
            return tk

        sq = Slots([TM[:, 1024:1536], TM[:, 1536:2048]])
        rss = Slots([TM[:, 2048:2560], TM[:, 2560:3072]])

        def rstd(src, nk, t0, t1, div, *deps, perk=None):
            n = t1 - t0
            b, pv, free = banks.take()
            for k in range(nk):
                s, sv, sfree = sq.take()
                tq = act(sv[:, 0:n], src(k, t0, t1), ACT.Square, sfree, deps, perk[k] if perk else None)
                tk = mm(pv[:, 0:n], ones[:, :], sv[:, 0:n], k == 0, k == nk - 1, tq, free, t_ones, inc=True)
                sq.free[s] = [tk]
            t1_ = act(pv[:, 512:512 + n], pv[:, 0:n], ACT.Sqrt, tk, t_cols, bias=epsc, scale=1.0 / div)
            r, rv, rfree = rss.take()
            t2 = rcp(rv[:, 0:n], pv[:, 512:512 + n], t1_, rfree)
            banks.free[b] = [t2]
            return r, rv[:, 0:n], t2

        def layer_norm(l, j, parts, scale, M, mj, xt):
            new, ht = [[] for _ in range(8)], [[] for _ in range(8)]
            gb = SM[:, 32:48]
            tg = ts(gb[:, 0:8], vec("ln_g", (2 * l + j) * 8, 8), scale, None, ALU.mult, None, *bar())
            tb = ts(gb[:, 8:16], vec("ln_b", (2 * l + j) * 8, 8), scale, None, ALU.mult, None)

            def part(t0, t1, ci):
                n = t1 - t0
                b, pv, free = banks.take()
                for k in range(8):
                    tk = mm(pv[:, 0:n], ones[:, :], XT[:, k, t0:t1], k == 0, k == 7, xt[k], free)
                sub = []
                for k in range(8):
                    sub.append([stt(XT[:, k, t0:t1], pv[:, 0:n], -1.0 / D, XT[:, k, t0:t1], ALU.mult, ALU.add, tk)])
                banks.free[b] = sub[-1]
                yield
                r, rv, tr_ = rstd(lambda k, t0, t1: XT[:, k, t0:t1], 8, t0, t1, D, perk=sub)
                yield
                for k in range(8):
                    ta = tt(XT[:, k, t0:t1], XT[:, k, t0:t1], rv, ALU.mult, tr_)
                    tc = act(XT[:, k, t0:t1], XT[:, k, t0:t1], ACT.Identity, ta, tb,
                             scale=gb[:, k:k + 1], bias=gb[:, 8 + k:9 + k])
                    new[k].append(tc)
                rss.free[r] = [ta]
                if mj is not None:
                    for k in range(8):
                        th = ts(HTF[:, k, t0:t1], XT[:, k, t0:t1], M[:, 8 * (mj + 1) + k, ci:ci + 1],
                                M[:, 8 * mj + k, ci:ci + 1], ALU.mult, ALU.add, new[k])
                        ht[k].append(split(HTH[:, k, t0:t1], HTL[:, k, t0:t1], HTF[:, k, t0:t1], th,
                                           eng=G if k % 2 else V))
            weave([part(*x) for x in parts[::-1]], 2)
            return new, ht

        def modulate(parts, M, mj, xt, *deps):
            ht = [[] for _ in range(8)]
            for t0, t1, ci in parts:
                for k in range(8):
                    th = ts(HTF[:, k, t0:t1], XT[:, k, t0:t1], M[:, 8 * (mj + 1) + k, ci:ci + 1],
                            M[:, 8 * mj + k, ci:ci + 1], ALU.mult, ALU.add, xt[k], *deps)
                    ht[k].append(split(HTH[:, k, t0:t1], HTL[:, k, t0:t1], HTF[:, k, t0:t1], th))
            return ht

        def ffn(w_in, w_out, t0, ht, done):
            n = T - t0
            HH = AR[:, 0:6144].rearrange("p (f t) -> p f t", t=T)
            HL = AR[:, 6144:12288].rearrange("p (f t) -> p f t", t=T)
            HF = A[:, 6144:12288].rearrange("p (f t) -> p f t", t=T)
            start = bar()
            hfree = start
            res = [None] * 8
            for g, (f0, nf) in enumerate(((0, 8), (8, 8), (16, 6))):
                hid = []
                for c in range(0, nf, 2):
                    tgs = []
                    for f in range(2):
                        b, pv, tk = lin([wp(w_in, (f0 + c + f) * 128, 128)], hx, 8, t0, T, perk=ht)
                        ta = act(HF[:, c + f, 0:n], pv[:, 0:n], ACT.Silu, tk, hfree)
                        banks.free[b] = [ta]
                        tgs.append(ta)
                    for f in range(2):
                        b, pv, tk = lin([wp(w_in, FF + (f0 + c + f) * 128, 128)], hx, 8, t0, T)
                        h = HF[:, c + f, 0:n]
                        tm = tt(h, h, pv[:, 0:n], ALU.mult, tgs[f], tk)
                        banks.free[b] = [tm]
                        hid.append([split(HH[:, c + f, 0:n], HL[:, c + f, 0:n], h, tm, hfree)])
                hv = (lambda k, a0, a1: HH[:, k, a0 - t0:a1 - t0], lambda k, a0, a1: HL[:, k, a0 - t0:a1 - t0])
                for m in range(8):
                    b, pv, tk = lin([wp(w_out, m * 128, 128, f0 * 128, nf)], hv, nf, t0, T, perk=hid)
                    res[m] = done(m, pv, tk, g)
                    banks.free[b] = res[m]
                hfree = [tk]
            return res

        def mix_out(w, r0, nk, hi, lo, parts, M, t0, *deps):
            res = []
            per = 8 // nk
            for m in range(8):
                if m % per == 0:
                    i, wh, wl, tw = panel("w", nk, wp(w, m * 128, per * 128, r0, nk))
                o = 128 * (m % per)
                b, pv, tk = proj3(wh, wl, slice(o, o + 128), (lambda k, a0, a1: hi[:, k, a0 - t0:a1 - t0],
                                                              lambda k, a0, a1: lo[:, k, a0 - t0:a1 - t0]),
                                  nk, t0, T, tw, deps)
                res.append(residual(M, 2, parts, t0)(m, pv, tk, 0))
                banks.free[b] = res[-1]
                if m % per == per - 1:
                    release(i, tk)
            return res

        def residual(M, gj, parts, t0):
            def done(m, pv, tk, g):
                return [stt(XT[:, m, p0:p1], pv[:, p0 - t0:p1 - t0], M[:, 8 * gj + m, ci:ci + 1], XT[:, m, p0:p1],
                            ALU.mult, ALU.add, tk) for p0, p1, ci in parts]
            return done

        def dump(view, k):
            if dbg is not None and STOP == k:
                n = view.free_size() if callable(view.free_size) else view.free_size
                tk = Y.dma(lambda e: e.dma_start(dbg[:, 0:n], view), osem, cnt, bar())
                return True
            return False

        def layer0(xt):
            w = a["ev_w_in"][0]
            for c in range(24):
                tm0 = mod_step(a["mod_w"][0], M0, c, 0, lambda x, n: vec("mod_b", x, n))
            tm0 = ln_layer(0, M0, tm0)
            ht = modulate(PX, M0, 0, xt, tm0)
            MIX = A[:, 18 * T:20 * T].rearrange("p (m t) -> p m t", t=T)
            MIL = AR[:, 18 * T:20 * T].rearrange("p (m t) -> p m t", t=T)
            MIH = AR[:, 20 * T:22 * T].rearrange("p (m t) -> p m t", t=T)
            if dump(XT[:, :, :], 1):
                return None, None

            def u(i, n=1):
                return A[:, i * T:(i + n) * T]
            start = bar()
            W2 = TM[0:32, 3072:3584].rearrange("p (d n) -> p d n", d=2)
            t0_ = ms(TM[0:32, 3072:3584], 0.0, start)
            tw2 = small([(W2[0:16, 0, :], a["gla_w_gate2"][0, 0]), (W2[16:32, 1, :], a["gla_w_gate2"][0, 1])], t0_)
            MK = TM[:, 3584:3840].rearrange("p (d n) -> p d n", d=2)
            tmk = small([(MK, con["glam"].rearrange("p (d n) -> p d n", d=2))], start)
            RST = TM[:, 3840:4608]
            tq = ms(RST, 1.0, start)
            trs = ms(RST.rearrange("p (c t) -> p c t", t=64)[:, :, 0], 0.0, tq)
            R = u(0)
            b, pv, tk = lin([wp(w, 1536, 32)], hx, 8, 0, T, perk=ht, M=32)
            t_r = copyS(R[0:32, :], pv[0:32, 0:T], tk, start)
            banks.free[b] = [t_r]
            for j in range(2):
                start = bar()
                q, k_ = u(1), u(2)
                vt = u(3, 2).rearrange("p (c n) -> p c n", c=6)
                qd, kd = (u(5), u(6)), (u(7), u(8))
                klT = (u(9).rearrange("p (c n) -> p c n", c=6), u(10).rearrange("p (c n) -> p c n", c=6))
                SS = (u(11, 2).rearrange("p (c n) -> p c n", c=12), u(13, 2).rearrange("p (c n) -> p c n", c=12))
                tmp = ((u(15), u(16), u(17)), (u(22), u(23), u(10)))
                dec = (SM[:, 48:60], SM[:, 60:72])
                t_q, t_k, t_v, t_g = [], [], [], []
                t_qd, t_kd, t_S = {}, {}, {0: {}, 1: {}}
                gates = []

                def projections():
                    b, pv, tk = lin([wp(w, 128 * j, 128)], hx, 8, 0, T)
                    t_q.append(act(q, pv[:, 0:T], ACT.Copy, tk, start, scale=0.125))
                    banks.free[b] = [t_q[-1]]
                    b, pv, tk = lin([wp(w, 256 + 128 * j, 128)], hx, 8, 0, T)
                    t_k.append(copyS(k_, pv[:, 0:T], tk, start))
                    banks.free[b] = [t_k[-1]]
                    yield
                    hv = halves("w", w, 512 + 256 * j)
                    for c in range(6):
                        b, pv, free = banks.take()
                        tk = xw(c * 128, hv, pv[:, 0:256], free)
                        t_v.append(copyS(vt[:, c, :], pv[:, 0:256], tk, start))
                        banks.free[b] = [t_v[-1]]
                    for x in hv:
                        release(x[0], tk)
                    while len(gates) < 2:
                        yield
                    for hh in range(2):
                        b, pv, tk = lin([wp(w, 1024 + 256 * j + 128 * hh, 128)], hx, 8, 0, T)
                        t_g.append(act(u(15 + hh), pv[:, 0:T], ACT.Silu, tk, gates))
                        banks.free[b] = [t_g[-1]]
                    for _ in range(6):
                        mod_some(1)
                        yield

                def gate(d):
                    la, kl, bb = tmp[d]
                    b, pv, tk = proj(lambda k: W2[:, d, 128 * j:128 * j + 128], lambda k, a0, a1: R[0:32, a0:a1], 1,
                                     0, T, t_r, tw2)
                    tz = ts(la, pv[:, 0:T], vec("gla_b", 2 * d + j), None, ALU.add, None, tk, start)
                    banks.free[b] = [tz]
                    te = act(kl, la, ACT.Abs, tz)
                    te = act(kl, kl, ACT.Exp, te, scale=-1.0)
                    te = act(kl, kl, ACT.Ln, te, t_cols, bias=onec)
                    yield
                    te = stt(la, la, 0.0, kl, ALU.min, ALU.subtract, te)
                    sl = slice(None, None, 1 if d == 0 else -1)
                    tb = V.do(lambda e, o=bb[:, sl], i_=la[:, sl]: e.tensor_tensor_scan(
                        out=o, data0=RST, data1=i_, initial=0.0, op0=ALU.mult, op1=ALU.add), te, trs)
                    b3 = bb.rearrange("p (c t) -> p c t", t=64)
                    bl = b3[:, :, 63:64] if d == 0 else b3[:, :, 0:1]
                    tl = tt(la.rearrange("p (c t) -> p c t", t=64), bl.to_broadcast([128, 12, 64]), b3, ALU.subtract, tb)
                    tdec = act(dec[d], bl.squeeze(2), ACT.Exp, tb, start, scale=1 / 16)
                    te3 = act(kl, la, ACT.Exp, tl, scale=1 / 16)
                    te1 = act(qd[d], bb, ACT.Exp, tb, start, scale=1 / 16)
                    te2 = act(kd[d], bb, ACT.Exp, tb, start, scale=-1 / 16)
                    yield
                    while not t_k:
                        yield
                    tl = tt(kl, kl, k_, ALU.mult, te3, t_k)
                    b, pv, free = banks.take()
                    for c in range(6):
                        tk = tr(pv[:, c * 128:c * 128 + 128], kl[:, c * 128:(c + 1) * 128], tl, free)
                    t_qd[d] = tt(qd[d], qd[d], q, ALU.mult, te1, t_q)
                    t_kd[d] = tt(kd[d], kd[d], k_, ALU.mult, te2, t_k)
                    tc = cpV(klT[d], pv[:, 0:T].rearrange("p (c n) -> p c n", c=6), tk, start)
                    banks.free[b] = [tc]
                    gates.append([tk, tc])
                    yield
                    while len(t_v) < 6:
                        yield
                    order = list(range(12)) if d == 0 else [3, 2, 1, 0] + list(range(11, 3, -1))
                    tS = ms(SS[d][:, order[0], :], 0.0, start)
                    t_S[d][order[0]] = tS
                    for x in range(11):
                        c, nx = order[x], order[x + 1]
                        h0 = 64 * (c % 2)
                        b, pv, free = banks.take()
                        tk = mm(pv[:, 0:256], klT[d][h0:h0 + 64, c // 2, :], vt[h0:h0 + 64, c // 2, :], True, True,
                                tc, t_v[c // 2], free)
                        t2 = []
                        for hh in range(2):
                            r = slice(64 * hh, 64 * hh + 64)
                            t2.append(stt(SS[d][r, nx, :], SS[d][r, c, :], dec[d][r, c:c + 1],
                                          pv[r, 128 * hh:128 * hh + 128], ALU.mult, ALU.add, tk, tS, tdec))
                        tS = t2
                        banks.free[b] = tS
                        t_S[d][nx] = tS
                        if x % 2:
                            yield
                weave([gate(0), gate(1), projections()], 3)
                at = Slots([TM[:, 0:1024], G0[:, :, :].rearrange("p a b -> p (a b)")])
                at.free = [list(start), list(start)]
                t_n = []

                def output(h, p0, p1):
                    r = slice(64 * h, 64 * h + 64)
                    n = p1 - p0
                    b, pv, free = banks.take()
                    cc0 = p0 // 128
                    for c in range(cc0, p1 // 128):
                        cs = slice(128 * c, 128 * c + 128)
                        for d in range(2):
                            o = 256 * (c - cc0) + 128 * d
                            tk = mm(pv[:, o:o + 128], kd[d][r, cs], qd[d][r, cs], True, True, free,
                                    t_kd[d], t_qd[d])
                    s, sv, sfree = at.take()
                    tm = None
                    for o in range(0, 2 * n, 512):
                        tm = tt(sv[:, o:o + 512].rearrange("p (c n) -> p c n", c=2),
                                pv[:, o:o + 512].rearrange("p (c n) -> p c n", c=2),
                                MK.rearrange("p d n -> p (d n)").unsqueeze(1).to_broadcast([128, 2, 256]),
                                ALU.mult, tk, sfree, tmk)
                    banks.free[b] = [tm]
                    yield
                    bo, po, freeo = banks.take()
                    for c in range(cc0, p1 // 128):
                        o = slice(128 * (c - cc0), 128 * (c - cc0) + 128)
                        for d in range(2):
                            o1 = 256 * (c - cc0) + 128 * d
                            tk = mm(po[:, o], vt[:, c, 128 * h:128 * h + 128], sv[:, o1:o1 + 128],
                                    d == 0, False, tm, freeo)
                        for d in range(2):
                            for e2 in range(2):
                                cc = 2 * c + e2
                                o2 = slice(128 * (c - cc0) + 64 * e2, 128 * (c - cc0) + 64 * e2 + 64)
                                tk = mm(po[:, o2], SS[d][r, cc, :], qd[d][r, 64 * cc:64 * cc + 64], False,
                                        d == 1 and e2 == 1, t_S[d][cc])
                    at.free[s] = [tk]
                    to = cpV(MIX[:, h, p0:p1], po[:, 0:n], tk, start)
                    banks.free[bo] = [to]
                    yield
                    ri, rv, tr_ = rstd(lambda k, a0, a1: MIX[:, h, a0:a1], 1, p0, p1, 128, to)
                    yield
                    tn = stt(MIX[:, h, p0:p1], rv, vec("gla_n"), MIX[:, h, p0:p1], ALU.mult, ALU.mult, tr_)
                    rss.free[ri] = [tn]
                    tn = tt(MIX[:, h, p0:p1], MIX[:, h, p0:p1], u(15 + h)[:, p0:p1], ALU.mult, tn, t_g)
                    t_n.append(split(MIH[:, h, p0:p1], MIL[:, h, p0:p1], MIX[:, h, p0:p1], tn, start))
                weave([output(h, p0, p1) for h in range(2) for p0, p1, _ in PX], 2)
                res = mix_out(a["ev_w_out"][0], 256 * j, 2, MIH, MIL, PX, M0, 0, t_n)
            start = bar()
            CO = u(6, 1)[:, 0:512]
            SI = u(7, 1)[:, 0:512]
            tcs = small([(CO, con["cos"]), (SI, con["sin"])], start)
            LP = SM[:, 0:256]
            LQ = TM[:, 3072:3328]
            tlp = small([(LQ, a["diff_lambda"][0].rearrange("a n -> (a n)").partition_broadcast(128))], start)
            l4 = LQ.rearrange("p (a n) -> p a n", a=4)
            tl = tt(LQ[:, 0:64], l4[:, 0, :], l4[:, 1, :], ALU.mult, tlp)
            tl2 = tt(LQ[:, 128:192], l4[:, 2, :], l4[:, 3, :], ALU.mult, tlp)
            lam = SM[:, 80:84]
            ta = V.do(lambda e: e.reduce_sum(lam[:, 0:1], LQ[:, 0:64], AX.X), tl)
            tb = V.do(lambda e: e.reduce_sum(lam[:, 1:2], LQ[:, 128:192], AX.X), tl2)
            tl = act(lam[:, 0:2], lam[:, 0:2], ACT.Exp, ta, tb)
            tl = tt(lam[:, 2:3], lam[:, 1:2], lam[:, 0:1], ALU.subtract, tl)
            lam_init = 0.8 - 0.6 * math.exp(0.0)
            t_lam = ts(lam[:, 2:3], lam[:, 2:3], lam_init, None, ALU.subtract, None, tl)
            hb = Slots([(u(0), u(1), u(4)), (u(14), u(15), u(16))])
            st = Slots([SM[:, 96:104], SM[:, 104:112], SM[:, 112:120]])
            es = Slots([(u(8), u(9)), (u(10), u(11)), (u(22), u(23))])
            wt = Slots([u(12), u(13)])
            for x in (hb, st, es, wt):
                x.free = [[start] for _ in x.v]
            raw, rt, vc = u(2), u(3), u(5)
            heads = {}
            rope_end = [start]
            vc_end = [start]

            def head(h):
                hi_, (qq, kk, v_), hfree = hb.take()
                vt = v_.rearrange("p (c n) -> p c n", c=6)
                toks = []
                rw = []
                for x, dst in enumerate((qq, kk)):
                    b, pv, tk = lin([wp(w, 1568 + 512 * x + 128 * h, 128)], hx, 8, 0, T)
                    t1 = copyS(dst[:, 0:TC], pv[:, 0:TC], tk, hfree)
                    src = (raw, vc)[x][:, 0:512]
                    t2 = copyS(src, pv[:, TC:T], tk, rope_end, vc_end)
                    banks.free[b] = [t2]
                    toks.append(t1)
                    rw.append((src, t2, dst))
                yield
                for src, t2, dst in rw:
                    b, pv, free = banks.take()
                    tk = mm(pv[:, 0:512], perm, src, True, True, t2, free)
                    t3 = tt(rt[:, 0:512], pv[:, 0:512], SI, ALU.mult, tk, tcs, rope_end)
                    banks.free[b] = [t3]
                    t4 = tt(src, src, CO, ALU.mult, tk, tcs)
                    t5 = tt(dst[:, TC:T], src, rt[:, 0:512], ALU.add, t3, t4, hfree)
                    toks.append(t5)
                    rope_end[:] = [t5]
                vc_end[:] = [t5]
                b, pv, tk = lin([wp(w, 2592 + 128 * h, 128)], hx, 8, 0, T)
                t_vc = copyS(vc, pv[:, 0:T], tk, vc_end)
                banks.free[b] = [t_vc]
                yield
                b, pv, free = banks.take()
                for c in range(6):
                    tk = tr(pv[:, c * 128:c * 128 + 128], vc[:, c * 128:c * 128 + 128], t_vc, free)
                t_v = copyS(vt, pv[:, 0:T].rearrange("p (c n) -> p c n", c=6), tk, hfree)
                banks.free[b] = [t_v]
                vc_end[:] = [tk]
                heads[h] = (hi_, qq, kk, vt, toks, t_v)

            t_out = {}
            t_fin = {}
            mixed = {-1: start}
            ends = {}

            def attend(h, qt):
                while h not in heads:
                    yield
                hi_, qq, kk, vt, t_qk, t_v = heads[h]
                nk = TC if qt < 2 else T
                si, sv, sfree = st.take()
                ei, ev, efree = es.take()
                te = []
                for x in range(2):
                    r = slice(64 * x, 64 * x + 64)
                    b, pv, free = banks.take()
                    for c0 in range(0, nk, 512):
                        c1 = min(c0 + 512, nk)
                        tk = mm(pv[:, c0:c1], qq[r, qt * 128:qt * 128 + 128], kk[r, c0:c1], True, True, free, t_qk)
                    t1 = V.do(lambda e, o=sv[:, x:x + 1], i_=pv[:, 0:nk]: e.reduce_max(o, i_, AX.X), tk, sfree)
                    t1 = ts(sv[:, 2 + x:3 + x], sv[:, x:x + 1], -0.125, None, ALU.mult, None, t1)
                    t2 = act(ev[x][:, 0:nk], pv[:, 0:nk], ACT.Exp, t1, efree, bias=sv[:, 2 + x:3 + x],
                             scale=0.125, accum_out=sv[:, 4 + x:5 + x])
                    banks.free[b] = [t2]
                    te.append(t2)
                ends.setdefault(h, []).append(tk)
                yield
                t1 = rcp(sv[:, 6:8], sv[:, 4:6], te)
                t2 = tt(sv[:, 7:8], sv[:, 7:8], lam[:, 2:3], ALU.mult, t1, t_lam)
                t3 = ts(ev[1][:, 0:nk], ev[1][:, 0:nk], sv[:, 7:8], None, ALU.mult, None, t2)
                t4 = stt(ev[0][:, 0:nk], ev[0][:, 0:nk], sv[:, 6:7], ev[1][:, 0:nk], ALU.mult, ALU.add, t3)
                st.free[si] = [t4]
                b, pv, free = banks.take()
                for c in range(nk // 128):
                    tk = tr(pv[:, c * 128:c * 128 + 128], ev[0][:, c * 128:c * 128 + 128], t4, free)
                es.free[ei] = [tk, t4]
                wi, wvv, wfree = wt.take()
                t5 = copyS(wvv[:, 0:nk], pv[:, 0:nk], tk, wfree)
                banks.free[b] = [t5]
                yield
                while h // 2 - 1 not in mixed:
                    yield
                b, pv, free = banks.take()
                for c in range(nk // 128):
                    tk = mm(pv[:, 0:128], vt[:, c, :], wvv[:, c * 128:c * 128 + 128], c == 0,
                            c == nk // 128 - 1, t5, t_v, free)
                wt.free[wi] = [tk]
                ends[h].append(tk)
                if len(ends[h]) == 12:
                    hb.free[hi_] = ends[h]
                to = cpV(MIX[:, h % 2, qt * 128:qt * 128 + 128], pv[:, 0:128], tk, mixed[h // 2 - 1])
                banks.free[b] = [to]
                t_out.setdefault((h, qt >= 2), []).append(to)
                mod_some(1)

            def finish(h, p0, p1):
                x = p0 >= TC
                while len(t_out.get((h, x), [])) < (4 if x else 2):
                    yield
                ri, rv, tr_ = rstd(lambda k, a0, a1: MIX[:, h % 2, a0:a1], 1, p0, p1, 128, t_out[(h, x)])
                yield
                v = MIX[:, h % 2, p0:p1]
                tn = stt(v, rv, vec("diff_n"), v, ALU.mult, ALU.mult, tr_)
                rss.free[ri] = [tn]
                tn = ts(v, v, 1.0 - lam_init, None, ALU.mult, None, tn)
                t_fin.setdefault(h // 2, []).append(
                    split(MIH[:, h % 2, p0:p1], MIL[:, h % 2, p0:p1], v, tn, mixed[h // 2 - 1]))

            def mix(j):
                while len(t_fin.get(j, [])) < 4:
                    yield
                mixed[j] = mix_out(a["ev_w_out"][0], 512 + 256 * j, 2, MIH, MIL, PX, M0, 0, t_fin[j])
                mixed[j].append((P.sem, P.n))
            gens = [head(0)]
            for h in range(4):
                gens += [attend(h, 0), attend(h, 2)]
                if h < 3:
                    gens.append(head(h + 1))
                gens += [attend(h, 1), attend(h, 3), attend(h, 4), attend(h, 5),
                         finish(h, 0, TC), finish(h, TC, T)]
                if h % 2:
                    gens.append(mix(h // 2))
            weave(gens, 3)
            res = mixed[1][0:8]
            xt, ht = layer_norm(0, 0, PX, ALPHA, M0, 3, res)
            if dump(XT[:, :, :], 3):
                return None, None
            res = ffn(a["ffn_w_in"][0], a["ffn_w_out"][0], 0, ht, residual(M0, 5, PX, 0))
            tm1 = mod_some(0, M1)
            ln_layer(1, M1, tm1)
            return layer_norm(0, 1, PX, ALPHA, M1, 0, res)

        def layer1(xt, ht):
            w = a["ssd_w_in"][0]
            start = bar()
            at = [0]

            def al(n, buf=A):
                at[0] += n
                return A[:, at[0] - n:at[0]]
            YF = al(2048).rearrange("p (m t) -> p m t", t=512)
            YL = AR[:, 0:2048].rearrange("p (m t) -> p m t", t=512)
            YH = AR[:, 2048:4096].rearrange("p (m t) -> p m t", t=512)
            al(2048)
            xs = al(3072).rearrange("p (c n) -> p c n", c=6)
            zz = al(2048).rearrange("p (c n) -> p c n", c=4)
            Bc = al(768)
            Cc = al(768)
            Bt = al(768).rearrange("p (c n) -> p c n", c=6)
            assert at[0] == 11520
            SS = al(4096).rearrange("p (d c n) -> p d c n", d=2, c=4)
            DT = TM[:, 0:384].rearrange("p (c h) -> p c h", c=6)
            DA = TM[:, 384:768].rearrange("p (c h) -> p c h", c=6)
            AC = TM[:, 768:1152].rearrange("p (c h) -> p c h", c=6)
            ED = TM[:, 1152:1536].rearrange("p (c h) -> p c h", c=6)
            EL = TM[:, 1536:1920].rearrange("p (c h) -> p c h", c=6)
            EA = TM[:, 1920:2304].rearrange("p (c h) -> p c h", c=6)
            row = TM[:, 2304:2464]
            tro = small([(row[:, 0:64], a["ssd_dt_bias"][0].rearrange("a n -> (a n)").partition_broadcast(128)),
                         (row[:, 64:128], a["ssd_a_log"][0].rearrange("a n -> (a n)").partition_broadcast(128)),
                         (row[:, 128:160], a["ssd_d"][0].partition_broadcast(128))], start)
            MN = TM[:, 2560:2816].rearrange("p (d n) -> p d n", d=2)
            tmn = small([(MN, con["minm"].rearrange("p (d n) -> p d n", d=2))], start)
            ta = act(row[:, 64:128], row[:, 64:128], ACT.Exp, tro)
            b, pv, tk = lin([wp(w, 5120, 64)], hx, 8, 0, T, perk=ht, M=64)
            dtc = TM[0:64, 2816:3584]
            t1 = copyS(dtc, pv[0:64, 0:T], tk, start)
            banks.free[b] = [t1]
            b, pv, free = banks.take()
            for c in range(6):
                tk = tr(pv[:, c * 64:c * 64 + 64], dtc[:, c * 128:c * 128 + 128], t1, free, n=64)
            p6 = pv[:, 0:384].rearrange("p (c h) -> p c h", c=6)
            t1 = tt(DT, p6, row[:, 0:64].unsqueeze(1).to_broadcast([128, 6, 64]), ALU.add, tk, tro, start)
            banks.free[b] = [t1]
            t2 = act(DA, DT, ACT.Abs, t1)
            t2 = act(DA, DA, ACT.Exp, t2, scale=-1.0)
            t2 = act(DA, DA, ACT.Ln, t2, bias=onec)
            t2 = stt(DT, DT, 0.0, DA, ALU.max, ALU.add, t2)
            t_dt = t2
            t2 = stt(DA, DT, -1.0, row[:, 64:128].unsqueeze(1).to_broadcast([128, 6, 64]), ALU.mult, ALU.mult, t2, ta)
            t_da = t2
            b, pv, free = banks.take()
            for c in range(6):
                mm(pv[:, c * 64:c * 64 + 32], triF, DA[:, c, 0:32], True, True, t2, free)
                mm(pv[:, c * 64 + 32:c * 64 + 64], triB, DA[:, c, 32:64], True, True)
                tk = mm(pv[:, 512 + c * 64:576 + c * 64], ones[:, :], DA[:, c, :], True, True)
            p6 = pv[:, 0:384].rearrange("p (c h) -> p c h", c=6)
            p7 = pv[:, 512:896].rearrange("p (c h) -> p c h", c=6)
            t1 = cpV(AC, p6, tk)
            t3 = act(ED, p7, ACT.Exp, tk, start)
            t4 = tt(EL, p7, AC, ALU.subtract, t1, t3)
            banks.free[b] = [t3, t4]
            t4 = act(EL, EL, ACT.Exp, t4)
            t_el = tt(EL, EL, DT, ALU.mult, t4)
            t_ea = act(EA, AC, ACT.Exp, t1, start)
            t_ac = [t1, t3]
            sets = [(A[:, 11520 + 776 * x:12296 + 776 * x], v) for x, v in enumerate(
                (A[:, 13848:14620], A[:, 14620:15392], TM[:, 3584:4356]))]

            for g in range(4):
                start = bar()
                cvs = Slots(sets)
                cvs.free = []
                for cvb, _ in sets:
                    ms(cvb[:, 0:2], 0.0, start)
                    ms(cvb[:, 258:262], 0.0)
                    cvs.free.append([ms(cvb[:, 774:776], 0.0), start])
                tbc = {}
                t_bt, t_xs, t_z = [], [], []

                def conv(ch, col, fin):
                    si, (cvb, cv), sfree = cvs.take()
                    b, pv, tk = lin([wp(w, col, 128)], hx, 8, 0, T)
                    t1 = copyS(cvb[:, 2:258], pv[:, 0:TC], tk, sfree)
                    t2 = copyS(cvb[:, 262:774], pv[:, TC:T], tk)
                    banks.free[b] = [t2]
                    yield
                    prev = ts(cv, cvb[:, 0:772], vec("conv_w", ch), vec("conv_b", ch), ALU.mult, ALU.add, t1, t2, sfree)
                    for s_ in range(1, 5):
                        prev = stt(cv, cvb[:, s_:s_ + 772], vec("conv_w", s_ * 24 + ch), cv, ALU.mult, ALU.add, prev)
                    if fin == "xs":
                        m = ch - 4 * g
                        ta = act(cv, cv, ACT.Silu, prev)
                        src = cv
                    else:
                        src = Bc if fin == "B" else Cc
                        ta = act(src[:, 0:TC], cv[:, 0:TC], ACT.Silu, prev, start)
                        ta = act(src[:, TC:T], cv[:, 260:772], ACT.Silu, prev)
                        tbc[fin] = ta
                    cvs.free[si] = [ta]
                    if fin == "C":
                        return
                    cvs.free[si] = None
                    yield
                    b, pv, free = banks.take()
                    for c in range(6):
                        o = c * 128 + (4 if fin == "xs" and c >= 2 else 0)
                        tk = tr(pv[:, c * 128:c * 128 + 128], src[:, o:o + 128], ta, free)
                    dst = Bt if fin == "B" else xs[:, :, m * 128:m * 128 + 128]
                    tq = (copyS if ch % 2 else cpV)(dst, pv[:, 0:T].rearrange("p (c n) -> p c n", c=6), tk, start)
                    banks.free[b] = [tq]
                    (t_bt if fin == "B" else t_xs).append(tq)
                    cvs.free[si] = [tk, ta]

                def zproj(x):
                    hv = halves("w", w, 512 * g + 256 * x)
                    for c in range(4):
                        b, pv, free = banks.take()
                        tk = xw(TC + c * 128, hv, pv[:, 0:256], free)
                        t_z.append(act(zz[:, c, 256 * x:256 * x + 256], pv[:, 0:256], ACT.Silu, tk, start))
                        banks.free[b] = [t_z[-1]]
                    for y in hv:
                        release(y[0], tk)
                    yield
                gens = [conv(16 + g, 4096 + 128 * g, "B"), conv(20 + g, 4608 + 128 * g, "C")]
                gens += [conv(4 * g + m, 2048 + 512 * g + 128 * m, "xs") for m in range(4)]
                weave(gens + [zproj(0), zproj(1)], 3)
                work = TM[:, 2816:4992]
                w1 = Slots([work[:, 0:512], work[:, 512:1024]])
                conv_end = [x for x in cvs.free]
                w1.free = [[conv_end], [conv_end]]
                cur = [work[:, 1024:1536], work[:, 1536:2048]]
                tS = {}

                def h8(v):
                    return v.rearrange("p (h n) -> p h n", h=8)

                def hb(v, n=64):
                    return v.unsqueeze(2).to_broadcast([128, 8, n])

                def states(d):
                    order = [0, 1, 2, 3, 4] if d == 0 else [1, 0, 5, 4, 3]
                    hs = slice(32 * d + 8 * g, 32 * d + 8 * g + 8)
                    prev = None
                    src = None
                    for x, c in enumerate(order):
                        wi, wvv, wfree = w1.take()
                        t1 = tt(h8(wvv), h8(xs[:, c, :]), hb(EL[:, c, hs]), ALU.mult, wfree, t_xs, t_el)
                        b, pv, free = banks.take()
                        tk = mm(pv[:, 0:512], Bt[:, c, :], wvv, True, True, t1, t_bt, free)
                        w1.free[wi] = [tk]
                        nx = (order + [5 if d == 0 else 2])[x + 1]
                        dst = SS[:, d, nx - 2, :] if nx >= 2 else cur[d]
                        if src is not None:
                            t2 = tt(h8(dst), h8(src), hb(ED[:, c, hs]), ALU.mult, prev, t_ac, conv_end)
                        banks.free[b] = None
                        yield
                        if src is None:
                            prev = cpV(dst, pv[:, 0:512], tk, conv_end)
                        else:
                            prev = tt(dst, dst, pv[:, 0:512], ALU.add, t2, tk)
                        banks.free[b] = [prev]
                        src = dst
                        tS[(d, nx)] = prev

                def fill(n):
                    for _ in range(n):
                        mod_some(1)
                        yield
                weave([states(0), states(1), fill(6)], 3)
                xd = Slots([work[:, 0:512], work[:, 512:1024]])
                yy_ = Slots([work[:, 1152:1664], A[:, 16640:17152]])
                yo_ = Slots([work[:, 1664:2176], A[:, 17152:17664]])
                cb_ = Slots([work[:, 1024:1152], A[:, 17664:17792]])
                G1 = A[:, 15616:16640].rearrange("p (h n) -> p h n", h=8)
                GG = Slots([G0[:, :, :], G1])
                work_end = [w1.free, (P.sem, P.n), (V.sem, V.n)]
                for x in (xd, yy_, yo_, cb_, GG):
                    x.free = [[work_end, start] for _ in x.v]
                t_out = []
                shared = {}

                def unit(c, d):
                    cs = slice(c * 128, c * 128 + 128)
                    hs0 = 32 * d + 8 * g
                    hs = slice(hs0, hs0 + 8)
                    tri = triF if d == 0 else triB
                    if d == 0:
                        ci, cbt, cfree = cb_.take()
                        b, pv, free = banks.take()
                        tcb = mm(pv[:, 0:128], Bc[:, cs], Cc[:, cs], True, True, free, tbc["B"], tbc["C"])
                        tcb = copyS(cbt, pv[:, 0:128], tcb, cfree)
                        banks.free[b] = [tcb]
                        shared[c] = [ci, cbt, tcb]
                    ci, cbt, tcb = shared[c][0:3]
                    gi, gg, gfree = GG.take()
                    b, pv, free = banks.take()
                    for h in range(8):
                        tk = mm(pv[:, 128 * h:128 * h + 128],
                                DA[:, c, hs0 + h:hs0 + h + 1].to_broadcast([128, 128]), tri, True, True, free, t_da)
                    for h in range(8):
                        t1 = stt(gg[:, h, :], pv[:, 128 * h:128 * h + 128], AC[:, c, hs0 + h:hs0 + h + 1],
                                 MN[:, d, :], ALU.subtract, ALU.min, tk, t_ac, tmn, gfree)
                    banks.free[b] = [t1]
                    t2 = act(gg, gg, ACT.Exp, t1)
                    xi, xdv, xfree = xd.take()
                    txd = tt(h8(xdv), h8(xs[:, c, :]), hb(DT[:, c, hs]), ALU.mult, xfree, t_xs, t_dt, eng=G)
                    yield
                    tG = tt(gg, gg, cbt.unsqueeze(1).to_broadcast([128, 8, 128]), ALU.mult, t2, tcb)
                    if d:
                        cb_.free[ci] = [tG]
                    b, pv, free = banks.take()
                    tk2 = mm(pv[:, 512:1024], Cc[:, cs], SS[:, d, c - 2, :], True, True, tS[(d, c)], free)
                    for h in range(8):
                        tk = mm(pv[:, 64 * h:64 * h + 64], gg[:, h, :], xdv[:, 64 * h:64 * h + 64], True, True, tG, txd)
                    GG.free[gi] = [tk]
                    xd.free[xi] = [tk]
                    if d == 0:
                        yi, yy, yfree = yy_.take()
                        oi, yo, ofree = yo_.take()
                        shared[c] += [yi, yy, oi, yo]
                        t1 = tt(h8(yy), h8(pv[:, 512:1024]), hb(EA[:, c, hs]), ALU.mult, tk2, t_ea, yfree)
                        t1 = tt(yy, yy, pv[:, 0:512], ALU.add, t1, tk)
                        t2 = tt(h8(yo), h8(xs[:, c, :]), hb(row[:, 128 + 8 * g:136 + 8 * g]), ALU.mult, ofree, tro,
                                eng=G)
                        banks.free[b] = [t1]
                        shared[c].append(tt(yy, yy, yo, ALU.add, t1, t2))
                        return
                    yi, yy, oi, yo, t1 = shared[c][3:8]
                    t2 = tt(h8(yo), h8(pv[:, 512:1024]), hb(EA[:, c, hs]), ALU.mult, tk2, t_ea, t1)
                    t1 = tt(yy, yy, pv[:, 0:512], ALU.add, t1, tk)
                    banks.free[b] = [t1, t2]
                    t1 = tt(yy, yy, yo, ALU.add, t1, t2)
                    t1 = tt(yy, yy, zz[:, c - 2, :], ALU.mult, t1, t_z)
                    rs = SM[:, 112 + 4 * (c % 2):116 + 4 * (c % 2)]
                    t2 = act(yo, yy, ACT.Square, t1, accum_out=rs[:, 0:1])
                    yo_.free[oi] = [t2]
                    t2 = act(rs[:, 1:2], rs[:, 0:1], ACT.Sqrt, t2, bias=epsc, scale=1.0 / 512)
                    yield
                    t2 = rcp(rs[:, 2:3], rs[:, 1:2], t2)
                    t1 = ts(yy, yy, rs[:, 2:3], None, ALU.mult, None, t2)
                    b, pv, free = banks.take()
                    for m in range(4):
                        tk = tr(pv[:, m * 128:m * 128 + 128], yy[:, m * 128:m * 128 + 128], t1, free)
                    t3 = tt(YF[:, :, (c - 2) * 128:(c - 2) * 128 + 128], pv[:, 0:512].rearrange("p (m t) -> p m t", m=4),
                            vec("ssd_n", 4 * g, 4).unsqueeze(2).to_broadcast([128, 4, 128]), ALU.mult, tk, start)
                    banks.free[b] = [t3]
                    yy_.free[yi] = [tk]
                    t_out.append(t3)
                weave([unit(c, d) for c in range(2, 6) for d in range(2)], 2)
                tsp = split(YH, YL, YF, t_out)
                res = mix_out(a["ssd_w_out"][0], 512 * g, 4, YH, YL, XX, M1, TC, tsp)
            xt, ht = layer_norm(1, 0, XX, ALPHA, M1, 3, res)
            res = ffn(a["ffn_w_in"][1], a["ffn_w_out"][1], TC, ht, residual(M1, 5, XX, TC))
            return layer_norm(1, 1, XX, 1.0, M1, None, res)[0]

        def pre(j, parts, xt):
            ht = [[] for _ in range(8)]
            start = bar()

            def part(t0, t1, ci):
                gg = SM[:, 208 + 8 * ci:216 + 8 * ci]
                tg = ts(gg, M2[:, 8 * (3 * j + 1):8 * (3 * j + 1) + 8, ci], 1.0, None, ALU.add, None, start)
                tg = tt(gg, gg, vec("npre", 8 * j, 8), ALU.mult, tg)
                r, rv, tr_ = rstd(lambda k, a0, a1: XT[:, k, a0:a1], 8, t0, t1, D, perk=xt)
                yield
                for k in range(8):
                    ta = stt(HTF[:, k, t0:t1], XT[:, k, t0:t1], gg[:, k:k + 1], rv, ALU.mult, ALU.mult,
                             tr_, start, tg)
                    tc = act(HTF[:, k, t0:t1], HTF[:, k, t0:t1], ACT.Identity, ta,
                             bias=M2[:, 8 * 3 * j + k, ci:ci + 1])
                    ht[k].append(split(HTH[:, k, t0:t1], HTL[:, k, t0:t1], HTF[:, k, t0:t1], tc, eng=G if k % 2 else V))
                rss.free[r] = [ta]
            weave([part(*x) for x in parts[::-1]], 2)
            return ht

        def post(j, parts, yt, wgt, YA):
            xt = [[] for _ in range(8)]
            start = bar()

            def part(t0, t1, ci):
                gg = SM[:, 224 + 8 * ci:232 + 8 * ci]
                tg = stt(gg, M2[:, 8 * (3 * j + 2):8 * (3 * j + 2) + 8, ci], wgt, vec("npost", 8 * j, 8), ALU.mult,
                         ALU.mult, start)
                r, rv, tr_ = rstd(lambda k, a0, a1: YA[:, k, a0:a1], 8, t0, t1, D, perk=yt)
                yield
                for k in range(8):
                    ta = stt(YA[:, k, t0:t1], YA[:, k, t0:t1], gg[:, k:k + 1], rv, ALU.mult, ALU.mult,
                             tr_, tg)
                    xt[k].append(tt(XT[:, k, t0:t1], XT[:, k, t0:t1], YA[:, k, t0:t1], ALU.add, ta, eng=G if k % 2 else V))
                rss.free[r] = [ta]
            weave([part(*x) for x in parts[::-1]], 2)
            return xt

        YA = A[:, 12288:18432].rearrange("p (m t) -> p m t", t=T)

        def to_ya(t0):
            def done(m, pv, tk, g):
                if g == 0:
                    return [copyS(YA[:, m, t0:T], pv[:, 0:T - t0], tk)]
                return [tt(YA[:, m, t0:T], YA[:, m, t0:T], pv[:, 0:T - t0], ALU.add, tk)]
            return done

        def block2(xt):
            start = bar()
            l2 = load_tokens(a["ctx_2"], 2, 0, 1.0, start)
            xt = [x + [y] for x, y in zip(xt, l2)]
            tm = mod_some(0, M2)
            ht = pre(0, PX, xt)
            res = ffn(a["ffn1_w_in_2"][0], a["ffn1_w_out_2"][0], 0, ht, to_ya(0))
            xt = post(0, PX, res, 0.5, YA)
            if dump(XT[:, :, :], 7):
                return
            ht = pre(1, PX, xt)
            w = a["mix_w_in_2"][0]
            start = bar()
            at = [0]

            def al(n):
                at[0] += n
                return A[:, at[0] - n:at[0]]

            def parts3(c):
                return (A[:, c:c + 2048].rearrange("p (m t) -> p m t", t=512),
                        AR[:, c + 2048:c + 4096].rearrange("p (m t) -> p m t", t=512),
                        AR[:, c:c + 2048].rearrange("p (m t) -> p m t", t=512))
            OH, OHH, OHL = parts3(0)
            OA, OAH, OAL = parts3(4096)
            start = bar()
            at[0] = 4096
            MK = al(14 * 128).rearrange("p (d n) -> p d n", d=14)
            tmk = small([(MK, con["hgm"].rearrange("p (d n) -> p d n", d=14))], start)
            RST = TM[:, 0:768]
            t1 = ms(RST, 1.0, start)
            trs = ms(RST.rearrange("p (c t) -> p c t", t=128)[:, :, 0], 0.0, t1)
            LB = SM[:, 160:184]
            tl = []
            for d, key in enumerate(("lbf", "lbb")):
                x0, x1 = vec(key, 0, 4), vec(key, 4, 4)
                mx, e0, e1 = LB[:, 0:4], LB[:, 4:8], LB[:, 8:12]
                lb, om = LB[:, 12 + 4 * d:16 + 4 * d], SM[:, 184 + 4 * d:188 + 4 * d]
                t1 = tt(mx, x0, x1, ALU.max, start, tl)
                t2 = tt(e0, x0, mx, ALU.subtract, t1)
                t3 = tt(e1, x1, mx, ALU.subtract, t1)
                t2 = act(LB[:, 4:12], LB[:, 4:12], ACT.Exp, t2, t3)
                t3 = tt(e1, e0, e1, ALU.add, t2)
                t3 = rcp(e1, e1, t3)
                t3 = tt(lb, e0, e1, ALU.mult, t3)
                t4 = ts(om, lb, -1.0, 1.0, ALU.mult, ALU.add, t3)
                tl = [t4]
            q = al(512)
            kx = (al(768), al(768))
            bx = (al(768), al(768))
            vt = al(768).rearrange("p (c n) -> p c n", c=6)
            kl = al(768)
            klT = al(768).rearrange("p (c n) -> p c n", c=6)
            SS = al(8 * 128).rearrange("p (d c n) -> p d c n", d=2, c=4)
            cur = (al(128), al(128))
            SCT, ET, QT, KT, BT = al(1024), al(1024), al(1024), al(1024), al(1024)
            SC, QB = ((x[:, 0:512], x[:, 512:1024]) for x in (SCT, BT))
            EE, QQ, KK = (Slots([x[:, 0:512], x[:, 512:1024]]) for x in (ET, QT, KT))
            kl1 = SCT[:, 0:T]
            klT1 = BT[:, 0:T].rearrange("p (c n) -> p c n", c=6)
            DC = SM[:, 192:204]
            for h in range(4):
                start = bar()
                for s_ in (EE, QQ, KK):
                    s_.free = [[start], [start]]
                c0 = 768 + 128 * h
                b, pv, tk = lin([wp(w, c0, 128)], hx, 8, TC, T, perk=ht)
                vtmp = QT[:, 0:T]
                t_q = act(q, pv[:, 0:512], ACT.Silu, tk, start)
                banks.free[b] = [t_q]
                b, pv, tk = lin([wp(w, c0 + 1536, 128)], hx, 8, 0, T)
                t_vc = copyS(vtmp, pv[:, 0:T], tk, start)
                banks.free[b] = [t_vc]
                t_v = []
                t_kb, t_S = {}, {0: {}, 1: {}}
                kls = (kl, kl1)
                klTs = (klT, klT1)

                def prep(d):
                    kl, klT = kls[d], klTs[d]
                    b, pv, tk = lin([wp(w, c0 + 512 + 512 * d, 128)], hx, 8, 0, T)
                    t1 = act(kx[d], pv[:, 0:T], ACT.Sigmoid, tk, start)
                    banks.free[b] = [t1]
                    t2 = ts(kl, kx[d], SM[:, 184 + 4 * d + h:185 + 4 * d + h], LB[:, 12 + 4 * d + h:13 + 4 * d + h],
                            ALU.mult, ALU.add, t1, tl, start)
                    t3 = ts(kx[d], kl, -1.0, 1.0, ALU.mult, ALU.add, t2)
                    t4 = act(kl, kl, ACT.Ln, t3)
                    if d == 0:
                        b, pv, free = banks.take()
                        for c in range(6):
                            tk = tr(pv[:, c * 128:c * 128 + 128], vtmp[:, c * 128:c * 128 + 128], t_vc, free)
                        t_v.append(copyS(vt, pv[:, 0:T].rearrange("p (c n) -> p c n", c=6), tk, start))
                        banks.free[b] = [t_v[-1]]
                        t_v.append(tk)
                    yield
                    sl = slice(None, None, 1 if d == 0 else -1)
                    tb = V.do(lambda e, o=bx[d][:, sl], i_=kl[:, sl]: e.tensor_tensor_scan(
                        out=o, data0=RST, data1=i_, initial=0.0, op0=ALU.mult, op1=ALU.add), t4, trs, start)
                    t_kb[d] = [t3, tb]
                    b3 = bx[d].rearrange("p (c t) -> p c t", t=128)
                    bl = b3[:, :, 127:128] if d == 0 else b3[:, :, 0:1]
                    dec = DC[:, 6 * d:6 * d + 6]
                    tdec = act(dec, bl.squeeze(2), ACT.Exp, tb, start)
                    t5 = tt(kl.rearrange("p (c t) -> p c t", t=128), bl.to_broadcast([128, 6, 128]), b3, ALU.subtract,
                            tb)
                    t5 = act(kl, kl, ACT.Exp, t5)
                    yield
                    t5 = tt(kl, kl, kx[d], ALU.mult, t5, t3)
                    b, pv, free = banks.take()
                    for c in range(6):
                        tk2 = tr(pv[:, c * 128:c * 128 + 128], kl[:, c * 128:c * 128 + 128], t5, free)
                    banks.free[b] = None
                    yield
                    t6 = cpV(klT, pv[:, 0:T].rearrange("p (c n) -> p c n", c=6), tk2, start)
                    banks.free[b] = [t6]
                    klfree[d] = tk2
                    order = [0, 1, 2, 3, 4] if d == 0 else [1, 0, 5, 4, 3]
                    src, prev = None, None
                    for x, c in enumerate(order):
                        b, pv, free = banks.take()
                        tk2 = mm(pv[:, 0:128], klT[:, c, :], vt[:, c, :], True, True, t6, t_v, free)
                        nx = (order + [5 if d == 0 else 2])[x + 1]
                        dst = SS[:, d, nx - 2, :] if nx >= 2 else cur[d]
                        banks.free[b] = None
                        yield
                        if src is None:
                            prev = cpV(dst, pv[:, 0:128], tk2, start)
                        else:
                            prev = stt(dst, src, dec[:, c:c + 1], pv[:, 0:128], ALU.mult, ALU.add, tk2, prev, tdec)
                        banks.free[b] = [prev]
                        src = dst
                        t_S[d][nx] = prev
                    klTfree[d] = tk2
                klfree, klTfree = {}, {}
                tsc = {}

                def level(d, lv):
                    while d not in t_kb:
                        yield
                    if lv == 7:
                        b, pv, free = banks.take()
                        for c in range(4):
                            tk = mm(pv[:, c * 128:c * 128 + 128], kx[d][:, TC + c * 128:TC + c * 128 + 128],
                                    q[:, c * 128:c * 128 + 128], True, True, free, t_kb[d], t_q)
                        mask = ident
                    else:
                        m = 64 >> lv
                        b4 = bx[d][:, TC:T].rearrange("p (c e m) -> p c e m", e=2, m=m)
                        nb = 512 // (2 * m)
                        ei, ev, efree = EE.take()
                        e4 = ev.rearrange("p (c e m) -> p c e m", e=2, m=m)
                        ref = b4[:, :, 0, m - 1:m] if d == 0 else b4[:, :, 1, 0:1]
                        ref = ref.to_broadcast([128, nb, m])
                        up, dn = (1, 0) if d == 0 else (0, 1)
                        t1 = tt(e4[:, :, up, :], b4[:, :, up, :], ref, ALU.subtract, efree, t_kb[d])
                        t2 = tt(e4[:, :, dn, :], ref, b4[:, :, dn, :], ALU.subtract)
                        t2 = act(ev, ev, ACT.Exp, t1, t2)
                        qi, qv, qfree = QQ.take()
                        ki, kv_, kfree = KK.take()
                        t3 = tt(qv, q, ev, ALU.mult, t2, qfree, t_q, eng=G)
                        yield
                        t4 = tt(kv_, kx[d][:, TC:T], ev, ALU.mult, t2, kfree, t_kb[d])
                        EE.free[ei] = [t3, t4]
                        b, pv, free = banks.take()
                        for c in range(4):
                            tk = mm(pv[:, c * 128:c * 128 + 128], kv_[:, c * 128:c * 128 + 128],
                                    qv[:, c * 128:c * 128 + 128], True, True, free, t3, t4)
                        QQ.free[qi] = [tk]
                        KK.free[ki] = [tk]
                        mask = MK[:, 7 * d + lv, :]
                    banks.free[b] = None
                    yield
                    while lv != 7 and d not in tsc:
                        yield
                    while lv == 7 and (d not in klfree or 1 not in klfree):
                        yield
                    p4 = pv[:, 0:512].rearrange("p (c n) -> p c n", c=4)
                    s4 = SC[d].rearrange("p (c n) -> p c n", c=4)
                    mb = mask.unsqueeze(1).to_broadcast([128, 4, 128])
                    if lv == 7:
                        tsc[d] = tt(s4, p4, mb, ALU.mult, tk, tmk, klfree[0], klfree[1], start)
                    else:
                        tsc[d] = V.do(lambda e, o=s4, m_=mb.bitcast(U32), i_=p4: e.copy_predicated(o, m_, i_), tk,
                                      tsc[d])
                    banks.free[b] = [tsc[d]]
                weave([prep(0), prep(1)], 2)
                gens = []
                for d in range(2):
                    gens += [level(d, lv) for lv in (7, 0, 1, 2, 3, 4, 5, 6)]
                QQ.free = [[start, t_v] for _ in QQ.v]
                weave(gens, 2)
                t_sc = [tsc[0], tsc[1]]
                t_qb = []
                for d in range(2):
                    t1 = act(QB[d], bx[d][:, TC:T], ACT.Exp, t_kb[d], klTfree[1], start)
                    t_qb.append(tt(QB[d], QB[d], q, ALU.mult, t1, t_q))
                b, pv, free = banks.take()
                for c in range(4):
                    cs = slice(c * 128, c * 128 + 128)
                    mm(pv[:, cs], vt[:, 2 + c, :], SC[0][:, cs], True, False, t_sc, free, t_v)
                    mm(pv[:, cs], vt[:, 2 + c, :], SC[1][:, cs], False, False)
                    mm(pv[:, cs], SS[:, 0, c, :], QB[0][:, cs], False, False, t_qb, t_S[0][c + 2], t_S[1][c + 2])
                    tk = mm(pv[:, cs], SS[:, 1, c, :], QB[1][:, cs], False, True)
                t1 = copyS(OH[:, h, :], pv[:, 0:512], tk, start)
                banks.free[b] = [t1]
                if h == 0:
                    t_oh = []
                t_oh.append([t1])
            if dump(A[:, 0:2048], 9):
                return
            ri, rv, tr_ = rstd(lambda k, a0, a1: OH[:, k, a0 - TC:a1 - TC], 4, TC, T, 512, perk=t_oh)
            t_r = []
            start = bar()
            for m in range(4):
                ta = stt(OH[:, m, :], OH[:, m, :], vec("hgn", m), rv, ALU.mult, ALU.mult, tr_)
                b, pv, tk = lin([wp(w, 2816 + 128 * m, 128)], hx, 8, TC, T)
                s, sv, sfree = sq.take()
                tb = act(sv, pv[:, 0:512], ACT.Silu, tk, sfree)
                banks.free[b] = [tb]
                t2 = tt(OH[:, m, :], OH[:, m, :], sv, ALU.mult, ta, tb)
                sq.free[s] = [t2]
                t_r.append(split(OHH[:, m, :], OHL[:, m, :], OH[:, m, :], t2))
            rss.free[ri] = [t2]
            start = bar()
            at[0] = 8192
            CO, SI = al(512), al(512)
            WM = al(256).rearrange("p (d n) -> p d n", d=2)
            q = al(2048).rearrange("p (m t) -> p m t", t=512)
            kk = al(1536).rearrange("p (m t) -> p m t", t=768)
            vt = al(768).rearrange("p (c n) -> p c n", c=6)
            rr = al(1024)
            raw, rt = rr[:, 0:512], rr[:, 512:1024]
            tcs = small([(CO, con["cos"]), (SI, con["sin"]), (WM, con["winm"].rearrange("p (d n) -> p d n", d=2))],
                        start)
            SK = SM[:, 136:144]
            tsk = small([(SK, a["attn_sink_2"][0].partition_broadcast(128))], start)
            tprev = [None]

            def rope(dst, t_raw):
                b, pv, free = banks.take()
                tk = mm(pv[:, 0:512], perm, raw, True, True, t_raw, free)
                t3 = tt(rt, pv[:, 0:512], SI, ALU.mult, tk, tcs)
                banks.free[b] = [t3]
                t4 = tt(raw, raw, CO, ALU.mult, tk)
                tprev[0] = tt(dst, raw, rt, ALU.add, t3, t4)
                return tprev[0]
            b, pv, tk = lin([wp(w, 640, 128)], hx, 8, 0, T)
            t_vc = copyS(rr[:, 0:T], pv[:, 0:T], tk, start)
            banks.free[b] = [t_vc]
            b, pv, free = banks.take()
            for c in range(6):
                tk = tr(pv[:, c * 128:c * 128 + 128], rr[:, c * 128:c * 128 + 128], t_vc, free)
            t_v = copyS(vt, pv[:, 0:T].rearrange("p (c n) -> p c n", c=6), tk)
            banks.free[b] = [t_v]
            tprev[0] = t_v
            t_q = []
            for m in range(4):
                b, pv, tk = lin([wp(w, 128 * m, 128)], hx, 8, TC, T)
                t1 = copyS(raw, pv[:, 0:512], tk, tprev[0], start)
                banks.free[b] = [t1]
                t_q.append(rope(q[:, m, :], t1))
            t_k = []
            for m in range(2):
                b, pv, tk = lin([wp(w, 512 + 64 * m, 64), wp(w, 512 + 64 * m, 64)], hx, 8, 0, T)
                t_k.append(copyS(kk[:, m, 0:TC], pv[:, 0:TC], tk))
                t1 = copyS(raw, pv[:, TC:T], tk, tprev[0])
                banks.free[b] = [t1]
                t_k.append(rope(kk[:, m, TC:T], t1))
            st = Slots([SM[:, 144:152], SM[:, 152:160], SM[:, 240:248]])
            es = Slots([al(640), al(640), TM[:, 3072:3712]])
            wt = Slots([al(640), al(640), TM[:, 3712:4352]])
            oo = Slots([al(512), al(512)])
            for s_ in (st, es, wt, oo):
                s_.free = [[start] for _ in s_.v]
            outs = {}

            def wunit(n, h):
                lo = 0 if n > 0 else 128
                hi = 384 if n < 3 else 256
                nb = hi - lo
                nk = nb + TC
                kv = h // 4
                r = slice(64 * (h % 2), 64 * (h % 2) + 64)
                si, sv, sfree = st.take()
                ei, ev, efree = es.take()
                b, pv, free = banks.take()
                k0 = TC + (n - 1) * 128 + lo
                lq = q[r, h // 2, n * 128:n * 128 + 128]
                mm(pv[:, 0:nb], lq, kk[r, kv, k0:k0 + nb], True, True, free, t_q, t_k)
                tk = mm(pv[:, 512:768], lq, kk[r, kv, 0:TC], True, True)
                ts_ = [act(ev[:, nb:nk], pv[:, 512:768], ACT.Copy, tk, efree, scale=0.125)]
                mid = 128 - lo
                if n > 0:
                    ts_.append(stt(ev[:, 0:128], pv[:, 0:128], 0.125, WM[:, 0, :], ALU.mult, ALU.add, tk, efree, tcs))
                ts_.append(ts(ev[:, mid:mid + 128], pv[:, mid:mid + 128], 0.125, None, ALU.mult, None, tk, efree))
                if n < 3:
                    ts_.append(stt(ev[:, mid + 128:mid + 256], pv[:, mid + 128:mid + 256], 0.125, WM[:, 1, :],
                                   ALU.mult, ALU.add, tk, efree, tcs))
                banks.free[b] = ts_
                t1 = V.do(lambda e, o=sv[:, 0:1], i_=ev[:, 0:nk]: e.reduce_max(o, i_, AX.X), ts_, sfree)
                t1 = ts(sv[:, 1:2], sv[:, 0:1], SK[:, h:h + 1], -1.0, ALU.max, ALU.mult, t1, tsk)
                t2 = act(ev[:, 0:nk], ev[:, 0:nk], ACT.Exp, t1, bias=sv[:, 1:2], accum_out=sv[:, 2:3])
                t3 = act(sv[:, 3:4], SK[:, h:h + 1], ACT.Exp, t1, bias=sv[:, 1:2])
                yield
                t4 = tt(sv[:, 4:5], sv[:, 2:3], sv[:, 3:4], ALU.add, t2, t3)
                t4 = rcp(sv[:, 5:6], sv[:, 4:5], t4)
                b, pv, free = banks.take()
                for c in range(nk // 128):
                    tk = tr(pv[:, c * 128:c * 128 + 128], ev[:, c * 128:c * 128 + 128], t2, free)
                es.free[ei] = [tk]
                wi, wvv, wfree = wt.take()
                t5 = copyS(wvv[:, 0:nk], pv[:, 0:nk], tk, wfree)
                banks.free[b] = [t5]
                yield
                if n not in outs:
                    outs[n] = [*oo.take(), []]
                oi, ov, ofree, t_o = outs[n]
                b, pv, free = banks.take()
                vc = [2 + n - 1 + (lo // 128) + c for c in range(nb // 128)] + [0, 1]
                for x, c in enumerate(vc):
                    tk = mm(pv[:, 0:64], wvv[:, x * 128:x * 128 + 128], vt[:, c, 64 * kv:64 * kv + 64], x == 0,
                            x == len(vc) - 1, t5, t_v, free)
                wt.free[wi] = [tk]
                t6 = act(ov[:, 64 * h:64 * h + 64], pv[:, 0:64], ACT.Copy, tk, t4, ofree, scale=sv[:, 5:6])
                banks.free[b] = [t6]
                st.free[si] = [t6]
                t_o.append(t6)
                if len(t_o) < 8:
                    return
                yield
                b, pv, free = banks.take()
                for m in range(4):
                    tk = tr(pv[:, m * 128:m * 128 + 128], ov[:, m * 128:m * 128 + 128], t_o, free)
                oo.free[oi] = [tk]
                t7 = cpV(OA[:, :, n * 128:n * 128 + 128], pv[:, 0:512].rearrange("p (m t) -> p m t", m=4), tk, start)
                banks.free[b] = [t7]
            weave([wunit(n, h) for n in range(4) for h in range(8)], 3)
            if dump(A[:, 4096:6144], 8):
                return
            t_oa = split(OAH, OAL, OA, bar())
            start = bar()
            MG = A[:, 8192:12288].rearrange("p (m t) -> p m t", t=512)
            MGL = AR[:, 8192:12288].rearrange("p (m t) -> p m t", t=512)
            MGH = AR[:, 12288:16384].rearrange("p (m t) -> p m t", t=512)
            s1 = Slots([A[:, 16384 + 512 * x:16896 + 512 * x] for x in range(4)])
            s1.free = [[start] for _ in range(4)]
            t_mg = []
            for m in range(0, 8, 2):
                res = {}
                for x in range(2):
                    for f in range(2):
                        b, pv, tk = lin([wp(w, 3328 + 1024 * x + 128 * (m + f), 128)], hx, 8, TC, T)
                        si, sv, sfree = s1.take()
                        t1 = act(sv, pv[:, 0:512], ACT.Sigmoid, tk, sfree)
                        banks.free[b] = [t1]
                        res[(x, f)] = (sv, t1, si)
                for f in range(2):
                    for x in range(2):
                        sh, slo = ((OAH, OAL), (OHH, OHL))[x]
                        b, pv, tk = lin([wp((a["w_o_attn_2"], a["w_o_hgrn_2"])[x][0], 128 * (m + f), 128, 0, 4)],
                                        (lambda k, a0, a1: sh[:, k, a0 - TC:a1 - TC],
                                         lambda k, a0, a1: slo[:, k, a0 - TC:a1 - TC]),
                                        4, TC, T, t_r, t_oa, start)
                        sv, t1, si = res[(x, f)]
                        t2 = tt(sv, sv, pv[:, 0:512], ALU.mult, t1, tk)
                        banks.free[b] = [t2]
                        res[(x, f)] = (sv, t2, si)
                    t3 = tt(MG[:, m + f, :], res[(0, f)][0], res[(1, f)][0], ALU.add, res[(0, f)][1], res[(1, f)][1])
                    for x in range(2):
                        s1.free[res[(x, f)][2]] = [t3]
                    t_mg.append([split(MGH[:, m + f, :], MGL[:, m + f, :], MG[:, m + f, :], t3)])
            start = bar()
            res = []
            YB = A[:, 0:6144].rearrange("p (m t) -> p m t", t=T)
            for m in range(8):
                b, pv, tk = lin([wp(a["w_out_2"][0], 128 * m, 128)],
                                (lambda k, a0, a1: MGH[:, k, a0 - TC:a1 - TC],
                                 lambda k, a0, a1: MGL[:, k, a0 - TC:a1 - TC]), 8, TC, T, perk=t_mg)
                res.append([copyS(YB[:, m, TC:T], pv[:, 0:512], tk, start)])
                banks.free[b] = res[-1]
            xt = post(1, XX, res, 1.0, YB)
            ht = pre(2, XX, xt)
            res = ffn(a["ffn2_w_in_2"][0], a["ffn2_w_out_2"][0], TC, ht, to_ya(TC))
            xt = post(2, XX, res, 0.5, YA)
            start = bar()
            stage = A[:, 0:4096].rearrange("p (i c) -> p i c", c=D)
            for k in range(8):
                b, pv, free = banks.take()
                for i in range(4):
                    tk = tr(pv[:, i * 128:i * 128 + 128], XT[:, k, TC + i * 128:TC + i * 128 + 128], xt[k], free)
                t1 = copyS(stage[:, :, k * 128:k * 128 + 128], pv[:, 0:512].rearrange("p (i n) -> p i n", i=4), tk,
                           start)
                banks.free[b] = [t1]
            for i in range(4):
                Y.dma(lambda e, i=i: e.dma_start(out[0, i * 128:i * 128 + 128, :], stage[:, i, :]), osem, cnt, t1)

        
        xt, ht = layer0(xt)
        if xt is not None and not dump(XT[:, :, :], 4):
            xt = layer1(xt, ht)
            if xt is not None and xt[0] is not None and not dump(XT[:, :, :], 6):
                block2(xt)
        Y.wait([(osem, cnt[id(osem)])])


def constants():
    i = np.arange(128)
    r, c = i[:, None], i[None, :]
    f = np.float32
    perm = np.zeros((128, 128), f)
    for m in range(128):
        if m % 32 < 16:
            perm[m + 16, m] = -1
        else:
            perm[m - 16, m] = 1
    base = np.concatenate([np.eye(128), r <= c, r >= c, perm], 1).astype(f)
    blk = r // 64 == c // 64
    glam = np.concatenate([blk & (r <= c), blk & (r >= c)], 1).astype(f)
    minm = np.concatenate([np.where(r <= c, 0, -1e30), np.where(r >= c, 0, -1e30)], 1).astype(f)
    winm = np.concatenate([np.where(c >= r, 0, -1e30), np.where(c <= r, 0, -1e30)], 1).astype(f)
    lv = []
    for m in (64, 32, 16, 8, 4, 2, 1):
        same = r // (2 * m) == c // (2 * m)
        lv.append(same & (r % (2 * m) < m) & (c % (2 * m) >= m))
    hgm = np.concatenate(lv + [x.T for x in lv], 1).astype(f)
    t = np.arange(512)
    inv = (f(10000.0) ** (-np.arange(16, dtype=f) / f(16))).astype(f)
    pos = np.stack([t // 64, t % 64]).astype(f)
    ang = np.empty((128, 512), f)
    for p in range(128):
        ang[p] = pos[(p // 32) % 2] * inv[p % 16]
    return {"base": base, "glam": glam, "minm": minm, "winm": winm, "hgm": hgm,
            "cos": np.cos(ang).astype(f), "sin": np.sin(ang).astype(f)}


def kernel(**inputs):
    import numpy as _np
    import concourse.bacc as _bacc
    from concourse import mybir as _mybir
    from concourse.bass_utils import run_bass_kernel_spmd as _run

    nc = _bacc.Bacc("TRN2", target_bir_lowering=False, num_devices=1)
    arrays, a, con = {}, {}, {}
    for name, x in inputs.items():
        x = _np.ascontiguousarray(x)
        arrays[f"in_{name}"] = x
        a[name] = nc.dram_tensor(f"in_{name}", x.shape, _mybir.dt.from_np(x.dtype), kind="ExternalInput").ap()
    for name, x in constants().items():
        arrays[f"con_{name}"] = x
        con[name] = nc.dram_tensor(f"con_{name}", x.shape, _mybir.dt.from_np(x.dtype), kind="ExternalInput").ap()
    out = nc.dram_tensor("out_0", (1, 512, 1024), _mybir.dt.float32, kind="ExternalOutput").ap()
    dbg = None
    if STOP < 99:
        dbg = nc.dram_tensor("dbg", (128, 8192), _mybir.dt.float32, kind="ExternalOutput").ap()
    program(nc, a, con, out, dbg)
    r = _run(nc, [arrays], core_ids=[0])
    return r.results[0]["out_0"]
```

```python
import math

import numpy as np
import concourse.bass as bass
from concourse import mybir

F = mybir.dt.float32
U32 = mybir.dt.uint32
FR = mybir.dt.float32r
ALU = mybir.AluOpType
ACT = mybir.ActivationFunctionType
AX = mybir.AxisListType
D = 1024
T = 768
TC = 256
ALPHA = 4 ** 0.25
EPS = 1e-6
NEG = -1e30
FF = 2816
FT = 22


class Lane:

    def __init__(self, sem):
        self.sem, self.n, self.seen, self.list = sem, 0, {}, []

    def wait(self, deps):
        for d in deps:
            if isinstance(d, list) or isinstance(d, tuple) and not (len(d) == 2 and isinstance(d[1], int)):
                self.wait(d)
            elif d is not None:
                sem, val = d
                if self.seen.get(id(sem), 0) < val:
                    self.seen[id(sem)] = val
                    self.list.append((None, sem, val))

    def do(self, fn, *deps, inc=True):
        self.wait(deps)
        if not inc:
            self.list.append((fn, None, 0))
            return None
        self.n += 1
        self.list.append((fn, self.sem, 1))
        return (self.sem, self.n)

    def dma(self, fn, sem, counts, *deps):
        self.wait(deps)
        counts[id(sem)] = counts.get(id(sem), 0) + 16
        self.list.append((fn, sem, 16))
        return (sem, counts[id(sem)])

    def emit(self, eng):
        for fn, sem, val in self.list:
            if fn is None:
                eng.wait_ge(sem, val)
            else:
                ins = fn(eng)
                if sem is not None:
                    ins.then_inc(sem, val)


class Slots:

    def __init__(self, views):
        self.v, self.free, self.i = views, [[] for _ in views], -1

    def take(self):
        for _ in self.v:
            self.i = (self.i + 1) % len(self.v)
            free = self.free[self.i]
            if free is not None:
                self.free[self.i] = None
                return self.i, self.v[self.i], free
        raise RuntimeError("no buffer is free")


def weave(gens, width):
    gens, live = list(gens), []
    while gens or live:
        while gens and len(live) < width:
            live.append(gens.pop(0))
        for g in list(live):
            try:
                next(g)
            except StopIteration:
                live.remove(g)
                if gens:
                    live.append(gens.pop(0))


def program(nc, a, con, out):
    from contextlib import ExitStack
    ctx = ExitStack()
    with ctx:
        def sb(name, shape, dt=F):
            return ctx.enter_context(nc.sbuf_tensor(name, shape, dt))

        def sb2(name, shape):
            with nc.sbuf_tensor(name, shape, F) as f:
                pass
            return f, sb(name + "r", shape, FR)

        def sem(name):
            return ctx.enter_context(nc.semaphore(name))

        XT = sb("XT", [128, 8, T])
        HTF, HTL = sb2("HT", [128, 8, T])
        HTH = sb("HTH", [128, 8, T], FR)
        RWF, RWL = sb2("RW", [128, 4, 1024])
        RWH = sb("RWH", [128, 4, 1024], FR)
        A, AR = sb2("A", [128, 18432])
        TM = sb("TM", [128, 4992])
        VEC = sb("VEC", [128, 5, 128])
        CS4 = sb("CS4", [128, 2, 8, 4], FR)
        sel2 = sb("sel2", [4, 2])
        rowb = sb("rowb", [4, 256])
        M0 = sb("M0", [128, 48, 2])
        M1 = sb("M1", [128, 48, 2])
        M2 = sb("M2", [128, 72, 2])
        CC = sb("CC", [128, 4, 128])
        SM = sb("SM", [128, 280])
        PS = ctx.enter_context(nc.psum_tensor("PS", [128, 4096], F))
        ident, triF, triB, perm = (CC[:, i, :] for i in range(4))
        ones = sb("ones", [128, 1])
        cols = sb("cols", [128, 8])
        G0 = sb("G0", [128, 8, 128])
        epsc, onec = cols[:, 0:1], cols[:, 1:2]
        sems = [sem(n) for n in ("s_pe", "s_dve", "s_act", "s_pool")]
        wsem = [sem(f"s_w{i}") for i in range(4)]
        lsem = [sem(f"s_l{i}") for i in range(8)]
        osem = sem("s_out")
        t = dict(locals())
        for x in ("nc", "a", "con", "out", "ctx", "sb", "sb2", "sem", "ExitStack", "sems"):
            t.pop(x)
        order = []
        body([Lane(x) for x in sems], Lane(None), t, a, con, out, order, False)
        lanes, Y = [Lane(x) for x in sems], Lane(None)
        body(lanes, Y, t, a, con, out, order, True)
        P, V, S, G = lanes

        block = ctx.enter_context(nc.Block())

        @block.sync
        def _(eng):
            Y.emit(eng)

        @block.tensor
        def _(eng):
            P.emit(eng)

        @block.vector
        def _(eng):
            V.emit(eng)

        @block.scalar
        def _(eng):
            S.emit(eng)

        @block.gpsimd
        def _(eng):
            G.emit(eng)


def body(lanes, Y, t, a, con, out, order, known):
    P, V, S, G = lanes
    XT, HTF, HTL, HTH, RWF, RWL, RWH, A, AR, TM, VEC, M0, M1, M2, CC, SM, PS = (t[x] for x in (
        "XT", "HTF", "HTL", "HTH", "RWF", "RWL", "RWH", "A", "AR", "TM", "VEC", "M0", "M1", "M2", "CC", "SM", "PS"))
    ident, triF, triB, perm, ones, G0, epsc, onec = (t[x] for x in (
        "ident", "triF", "triB", "perm", "ones", "G0", "epsc", "onec"))
    wsem, lsem, osem = t["wsem"], t["lsem"], t["osem"]
    cnt = {}
    held = [[], [], [], []]
    banks = Slots([PS[:, 1024 * i:1024 * i + 1024] for i in range(4)])
    specs = list(order) if known else []
    loaded, ready = {}, {}
    asked = [0]

    def bar():
        return [(l.sem, l.n) for l in (P, V, S, G) if l.n]

    def fetch(n):
        i = n % 4
        kind, nk, width, cuts = specs[n]
        free = held[i]
        assert free is not None
        held[i] = None
        raw = RWF[:, i, 0:nk * width].rearrange("p (k n) -> p k n", k=nk)
        at, tok = 0, None
        for src, w_ in cuts:
            tok = Y.dma(lambda e, d=raw[:, :, at:at + w_], s_=src: e.dma_start(d, s_), wsem[i], cnt, free)
            at += w_
        loaded[n] = (raw, tok, free)

    def divide(n):
        i = n % 4
        kind, nk, width, _ = specs[n]
        raw, tok, free = loaded[n]
        fl = slice(0, nk * width)
        t1 = copyS(RWH[:, i, fl], RWF[:, i, fl], tok, free)
        t2 = tt(RWL[:, i, fl], RWF[:, i, fl], RWH[:, i, fl].bitcast(F), ALU.subtract, t1,
                eng=V if n % 3 == 0 else G)
        ready[n] = (i, RWH[:, i, fl].rearrange("p (k n) -> p k n", k=nk),
                    RWL[:, i, fl].rearrange("p (k n) -> p k n", k=nk), t2)

    def panel(kind, nk, *cuts):
        n = asked[0]
        width = sum(w_ for _, w_ in cuts)
        assert nk * width <= 1024
        if known:
            assert specs[n][0:3] == (kind, nk, width)
        else:
            specs.append((kind, nk, width, cuts))
            order.append(specs[-1])
        if n not in loaded:
            fetch(n)
        if n not in ready:
            divide(n)
        asked[0] += 1
        return ready[n]

    def release(i, tok):
        held[i] = [tok]
        if known:
            for n in range(asked[0], min(asked[0] + 3, len(specs))):
                if n in loaded and n not in ready:
                    divide(n)
            for n in range(asked[0], min(asked[0] + 4, len(specs))):
                if n not in loaded:
                    if held[n % 4] is None:
                        break
                    fetch(n)

    def wp(w, c0, n, r0=0, nk=8):
        return (w[r0:r0 + nk * 128, c0:c0 + n].rearrange("(k p) n -> p k n", p=128), n)

    nl = [0]

    def small(pairs, *deps):
        s = lsem[nl[0] % 8]
        nl[0] += 1
        tok = None
        for dst, src in pairs:
            tok = Y.dma(lambda e, d=dst, s_=src: e.dma_start(d, s_), s, cnt, *deps)
        return tok

    def mm(o, l, r, start, stop, *deps, inc=None):
        return P.do(lambda e: e.matmul(o, l, r, start=start, stop=stop, skip_group_check=True), *deps,
                    inc=stop if inc is None else inc)

    def tr(o, i, *deps, n=128):
        return P.do(lambda e: e.transpose(o, i, ident[0:n, 0:n]), *deps)

    def act(o, i, f, *deps, **kw):
        return S.do(lambda e: e.activation(o, i, f, **kw), *deps)

    def copyS(o, i, *deps):
        return S.do(lambda e: e.activation(o, i, ACT.Copy), *deps)

    def tt(o, i0, i1, op, *deps, eng=None):
        return (eng or V).do(lambda e: e.tensor_tensor(out=o, in0=i0, in1=i1, op=op), *deps)

    def ts(o, i, s1, s2, op0, op1, *deps, eng=None):
        if op1 is None:
            return (eng or V).do(lambda e: e.tensor_scalar(out=o, in0=i, scalar1=s1, scalar2=None, op0=op0), *deps)
        return (eng or V).do(lambda e: e.tensor_scalar(out=o, in0=i, scalar1=s1, scalar2=s2, op0=op0, op1=op1), *deps)

    def stt(o, i0, s, i1, op0, op1, *deps):
        return V.do(lambda e: e.scalar_tensor_tensor(out=o, in0=i0, scalar=s, in1=i1, op0=op0, op1=op1), *deps)

    def cpV(o, i, *deps):
        return V.do(lambda e: e.tensor_copy(o, i), *deps)

    def rcp(o, i, *deps):
        return V.do(lambda e: e.reciprocal(o, i), *deps)

    def ms(o, val, *deps, eng=None):
        return (eng or V).do(lambda e: e.memset(o, val), *deps)

    def proj(lhs, rhs, nk, t0, t1, *deps, perk=None, M=128):
        b, pv, free = banks.take()
        n = t1 - t0
        tok = None
        for c0 in range(0, n, 512):
            c1 = min(c0 + 512, n)
            for k in range(nk):
                tok = mm(pv[0:M, c0:c1], lhs(k), rhs(k, t0 + c0, t0 + c1), k == 0, k == nk - 1,
                         free, deps, perk[k] if perk else None)
        return b, pv, tok

    def mm3(o, lh, ll, rh, rl, k, nk, *deps):
        mm(o, lh, rh, k == 0, False, *deps)
        mm(o, lh, rl, False, False)
        return mm(o, ll, rh, False, k == nk - 1)

    def proj3(wh, wl, cs, x, nk, t0, t1, *deps, perk=None, M=128, k0=0):
        b, pv, free = banks.take()
        n = t1 - t0
        tok = None
        for c0 in range(0, n, 512):
            c1 = min(c0 + 512, n)
            for k in range(nk):
                tok = mm3(pv[0:M, c0:c1], wh[:, k, cs], wl[:, k, cs], x[0](k, t0 + c0, t0 + c1),
                          x[1](k, t0 + c0, t0 + c1), k, nk, free, deps, perk[k] if perk else None)
        return b, pv, tok

    def lin(cuts, x, nk, t0, t1, *deps, perk=None, M=128):
        i, wh, wl, tw = panel("w", nk, *cuts)
        b, pv, tk = proj3(wh, wl, slice(0, M), x, nk, t0, t1, tw, *deps, perk=perk, M=M)
        release(i, tk)
        return b, pv, tk

    def halves(kind, w, c0):
        return [panel(kind, 4, wp(w, c0, 256, 512 * x, 4)) for x in range(2)]

    def xw(c0, hv, o, *deps):
        tok = None
        for k in range(8):
            _, wh, wl, tw = hv[k // 4]
            tok = mm3(o, HTH[:, k, c0:c0 + 128], HTL[:, k, c0:c0 + 128], wh[:, k % 4, :], wl[:, k % 4, :], k, 8,
                      tw, *deps)
        return tok

    def split(hi, lo, raw, *deps, eng=None):
        t1 = copyS(hi, raw, *deps)
        return tt(lo, raw, hi.bitcast(F), ALU.subtract, t1, eng=eng)

    hx = (lambda k, t0, t1: HTH[:, k, t0:t1], lambda k, t0, t1: HTL[:, k, t0:t1])

    t_c = small([(CC[:, :, :], con["base"].rearrange("p (c n) -> p c n", c=4))])
    t_ones = ms(ones[:, :], 1.0)
    ms(epsc, EPS)
    t_cols = ms(onec, 1.0)
    ST = A[:, 0:640].rearrange("p (c n) -> p c n", c=5)
    t_z = ms(A[:, 0:640], 0.0)

    def rows(ap, n):
        return ap.rearrange("(r n) -> r n", n=128) if len(ap.shape) == 1 else ap

    spots = {}
    items = []
    fill = [0] * 5

    def put(col, key, ap, n):
        spots[key] = (col, fill[col], n)
        items.append((ST[fill[col]:fill[col] + n, col, :], ap))
        fill[col] += n

    r128 = "(r n) -> r n"
    put(0, "ln_g", a["ln_g"].rearrange("a b (r n) -> (a b r) n", n=128), 32)
    put(0, "ln_b", a["ln_b"].rearrange("a b (r n) -> (a b r) n", n=128), 32)
    put(0, "npre", a["norm_pre_2"].rearrange("o b (r n) -> (o b r) n", n=128), 24)
    put(0, "npost", a["norm_post_2"].rearrange("o b (r n) -> (o b r) n", n=128), 24)
    put(1, "mod_b", a["mod_b"].rearrange("a (r n) -> (a r) n", n=128), 96)
    put(2, "b_ada", a["b_ada_2"].rearrange("a (r n) -> (a r) n", n=128), 72)
    put(2, "c", a["c"].rearrange("a (r n) -> (a r) n", n=128), 8)
    put(2, "c_ctx", a["c_ctx"].rearrange(r128, n=128), 8)
    put(2, "c2", a["c_2"].rearrange("a (r n) -> (a r) n", n=128), 8)
    put(2, "c_ctx2", a["c_ctx_2"].rearrange(r128, n=128), 8)
    put(3, "conv_w", a["ssd_conv_w"].rearrange("o k (r n) -> (o k r) n", n=128), 120)
    put(4, "gla_b", a["gla_b_gate"].rearrange("o d (r n) -> (o d r) n", n=128), 4)
    put(4, "gla_n", a["gla_norm_w"], 1)
    put(4, "diff_n", a["diff_norm_w"], 1)
    put(4, "conv_b", a["ssd_conv_b"].rearrange("o (r n) -> (o r) n", n=128), 24)
    put(4, "ssd_n", a["ssd_norm_w"].rearrange("o (r n) -> (o r) n", n=128), 16)
    put(4, "lbf", a["hgrn_lb_fwd_2"].rearrange("o (r n) -> (o r) n", n=128), 8)
    put(4, "lbb", a["hgrn_lb_bwd_2"].rearrange("o (r n) -> (o r) n", n=128), 8)
    put(4, "hgn", a["hgrn_norm_2"].rearrange("o (r n) -> (o r) n", n=128), 4)
    t_st = small(items, t_z)
    b, pv, free = banks.take()
    for c in range(5):
        tk = tr(pv[:, c * 128:(c + 1) * 128], ST[:, c, :], t_st, t_c, free)
    t_vec = cpV(VEC[:, :, :], pv[:, 0:640].rearrange("p (c n) -> p c n", c=5), tk)
    banks.free[b] = [t_vec]

    def vec(key, i=0, n=1):
        c, r, _ = spots[key]
        return VEC[:, c, r + i:r + i + n]

    CS = SM[:, 0:32].rearrange("p (k v) -> p k v", v=4)
    CS4, sel2 = t["CS4"], t["sel2"]
    t_sel = tt(sel2[:, :], ident[0:4, 0:2], ident[0:4, 2:4], ALU.add, t_c)
    t_cs = None
    for v, key in enumerate(("c", "c_ctx", "c2", "c_ctx2")):
        t_cs = act(CS[:, :, v], vec(key, 0, 8), ACT.Silu, t_vec)
    for x in range(2):
        t_hi = copyS(CS4[:, x, :, 0:2], CS[:, :, 2 * x:2 * x + 2], t_cs)
        t_c4 = tt(CS4[:, x, :, 2:4], CS[:, :, 2 * x:2 * x + 2], CS4[:, x, :, 0:2].bitcast(F), ALU.subtract, t_hi)

    def load_tokens(src, ntile, t0, scale, *deps):
        stage = A[:, 1024:1024 + ntile * D].rearrange("p (i c) -> p i c", c=D)
        tl = small([(stage, src.rearrange("o (i p) c -> p (o i) c", p=128))], *deps)
        last = []
        for k in range(8):
            b, pv, free = banks.take()
            for i in range(ntile):
                tk = tr(pv[:, i * 128:(i + 1) * 128], stage[:, i, k * 128:(k + 1) * 128], tl, free, t_c)
            tok = act(XT[:, k, t0:t0 + ntile * 128], pv[:, 0:ntile * 128], ACT.Copy, tk, deps, scale=scale)
            banks.free[b] = [tok]
            last.append(tok)
        return last

    l1 = load_tokens(a["x"], 4, TC, ALPHA)
    l2 = load_tokens(a["ctx"], 2, 0, ALPHA, l1)
    xt = [[p, q] for p, q in zip(l1, l2)]

    rowb = t["rowb"][:, :]
    pend, row_end = [], [None]

    def transpose_row(pv, *free):
        M, c, bias, tcp = pend.pop()
        for q in range(2):
            tk = mm(pv[:, 512 + 2 * q:514 + 2 * q], rowb[:, q * 128:(q + 1) * 128], sel2[:, :], True, True, tcp,
                    t_sel, *free)
        row_end[0] = tk
        tok = tt(M[:, 2 * c:2 * c + 2, :], pv[:, 512:516].rearrange("p (q v) -> p q v", v=2),
                 bias(2 * c, 2).unsqueeze(2).to_broadcast([128, 2, 2]), ALU.add, tk, t_vec)
        mod_tok[0] = tok
        return tok

    def mod_step(w, M, c, v0, bias):
        b, pv, free = banks.take()
        for x in range(2):
            i, wh, wl, tw = panel("w", 4, wp(w, c * 256, 256, 512 * x, 4))
            for k in range(4):
                l = CS4[:, v0 // 2, 4 * x + k, :]
                mm(pv[0:4, 0:256], l, wh[:, k, :], x == 0 and k == 0, False, tw, free, t_c4)
                tk = mm(pv[0:4, 0:256], l, wl[:, k, :], False, x == 1 and k == 3, inc=True)
            release(i, tk)
        tok = transpose_row(pv, free) if pend else None
        tcp = copyS(rowb, pv[0:4, 0:256], tk, row_end[0])
        pend.append((M, c, bias, tcp))
        banks.free[b] = [tcp, tok]

    def mod_end():
        b, pv, free = banks.take()
        banks.free[b] = [transpose_row(pv, free)]
        return mod_tok[0]

    later = [(a["mod_w"][0], M0, c, 0, lambda x, n: vec("mod_b", x, n)) for c in range(8, 24)]
    later += [(a["mod_w"][1], M1, c, 0, lambda x, n: vec("mod_b", 48 + x, n)) for c in range(24)]
    later += [(a["w_ada_2"][0], M2, c, 2, lambda x, n: vec("b_ada", x, n)) for c in range(36)]
    mod_tok = [None]

    def mod_some(n, left=0):
        for _ in range(min(n, len(later) - left)):
            mod_step(*later.pop(0))

    def mod_until(left):
        mod_some(len(later), left)
        return mod_end() if pend else mod_tok[0]

    def mod_pace(left):
        todo, at = max(len(later) - left, 0), 0
        for i in range(68):
            while at < todo * (i + 1) // 68:
                mod_some(1)
                at += 1
            yield

    PX = [(0, TC, 1), (TC, T, 0)]
    XX = [(TC, T, 0)]

    def ln_layer(l, M, *deps):
        tk = None
        for j in (1, 4):
            tk = ts(M[:, 8 * j:8 * j + 8, :], M[:, 8 * j:8 * j + 8, :], 1.0, 1.0 / ALPHA, ALU.add, ALU.mult, *deps)
        return tk


    def fold(v0, v1, n, pv, free, t0, t1):
        for i in range(n // 128):
            c = slice(i * 128, i * 128 + 128)
            tk = mm(pv[:, i:i + 1], v0[:, c], ones[:, 0:1], True, v1 is None, free, t_ones, t0)
            if v1 is not None:
                tk = mm(pv[:, i:i + 1], v1[:, c], ones[:, 0:1], False, True, t1)
        return tk

    SHARE = (V, G, V, G, V, V, G, V)

    def colsum(src, n, perk):
        b, pv, free = banks.take()
        acc = {}
        for e in (V, G):
            ks = [k for k in range(8) if SHARE[k] is e]
            s, sv, sfree = sqb.take()
            tok = tt(sv[:, 0:n], src(ks[0]), src(ks[1]), ALU.add, sfree, perk[ks[0]], perk[ks[1]], eng=e)
            for k in ks[2:]:
                tok = tt(sv[:, 0:n], sv[:, 0:n], src(k), ALU.add, tok, perk[k], eng=e)
            acc[e] = (s, sv, tok)
        tk = fold(acc[V][1], acc[G][1], n, pv, free, acc[V][2], acc[G][2])
        for e in (V, G):
            sqb.free[acc[e][0]] = [tk]
        return b, pv, tk

    def spread(b, pv, st, n, *deps):
        for i in range(n // 128):
            tk = mm(pv[:, 512 + i * 128:640 + i * 128], st[:, i:i + 1].to_broadcast([128, 128]), ident, True, True,
                    *deps)
        return pv[:, 512:512 + n], tk

    stats = Slots([SM[:, 256 + 8 * i:264 + 8 * i] for i in range(3)])
    sqb = Slots([TM[:, 1024 + 512 * i:1536 + 512 * i] for i in range(4)])

    def rstd(src, nk, t0, t1, div, *deps, perk=None):
        n = t1 - t0
        b, pv, free = banks.take()
        acc = {}
        for k in range(nk):
            e = SHARE[k]
            s, sv, sfree = sqb.take()
            tq = act(sv[:, 0:n], src(k, t0, t1), ACT.Square, sfree, deps, perk[k] if perk else None)
            if e in acc:
                s0, v0, tok = acc[e]
                tq = tt(v0[:, 0:n], v0[:, 0:n], sv[:, 0:n], ALU.add, tok, tq, eng=e)
                sqb.free[s] = [tq]
                s, sv = s0, v0
            acc[e] = (s, sv, tq)
        s1, v1, tq1 = acc.get(G, (None, None, None))
        tk = fold(acc[V][1], v1, n, pv, free, acc[V][2], tq1)
        for s, _, _ in acc.values():
            sqb.free[s] = [tk]
        si, st, sfree = stats.take()
        m = n // 128
        t2 = act(st[:, 4:4 + m], pv[:, 0:m], ACT.Sqrt, tk, sfree, t_cols, bias=epsc, scale=1.0 / div)
        t2 = rcp(st[:, 4:4 + m], st[:, 4:4 + m], t2)
        rv, tk = spread(b, pv, st[:, 4:4 + m], n, t2)
        stats.free[si] = [tk]
        return b, rv, tk

    def layer_norm(l, j, parts, scale, M, mj, xt):
        new, ht = [[] for _ in range(8)], [[] for _ in range(8)]
        gb = SM[:, 32:48]
        tg = ts(gb[:, 0:8], vec("ln_g", (2 * l + j) * 8, 8), scale, None, ALU.mult, None, *bar())
        tb = ts(gb[:, 8:16], vec("ln_b", (2 * l + j) * 8, 8), scale, None, ALU.mult, None)

        ab = {}
        if mj is not None:
            for _, _, ci in parts:
                v = SM[:, 48 + 16 * ci:64 + 16 * ci]
                sc, sh = M[:, 8 * mj + 8:8 * mj + 16, ci], M[:, 8 * mj:8 * mj + 8, ci]
                t1 = tt(v[:, 0:8], gb[:, 0:8], sc, ALU.mult, tg, tb)
                t2 = tt(v[:, 8:16], gb[:, 8:16], sc, ALU.mult, tb)
                ab[ci] = (v, tt(v[:, 8:16], v[:, 8:16], sh, ALU.add, t1, t2))

        def part(t0, t1, ci):
            n = t1 - t0
            m = n // 128
            b, pv, tk = colsum(lambda k: XT[:, k, t0:t1], n, xt)
            si, st, sfree = stats.take()
            t2 = ts(st[:, 0:m], pv[:, 0:m], -1.0 / D, None, ALU.mult, None, tk, sfree)
            rv, tk = spread(b, pv, st, n, t2)
            stats.free[si] = [tk]
            sub = []
            for k in range(8):
                sub.append([tt(XT[:, k, t0:t1], XT[:, k, t0:t1], rv, ALU.add, tk)])
            banks.free[b] = sub[-1]
            yield
            r, rv, tr_ = rstd(lambda k, t0, t1: XT[:, k, t0:t1], 8, t0, t1, D, perk=sub)
            yield
            late = []
            for k in range(8):
                ta = tt(XT[:, k, t0:t1], XT[:, k, t0:t1], rv, ALU.mult, tr_)
                if mj is not None:
                    v, tv = ab[ci]
                    t1_ = act(HTH[:, k, t0:t1], XT[:, k, t0:t1], ACT.Identity, ta, tv,
                              scale=v[:, k:k + 1], bias=v[:, 8 + k:9 + k])
                    if k % 2:
                        th = act(HTF[:, k, t0:t1], XT[:, k, t0:t1], ACT.Identity, ta, tv,
                                 scale=v[:, k:k + 1], bias=v[:, 8 + k:9 + k])
                    else:
                        th = ts(HTF[:, k, t0:t1], XT[:, k, t0:t1], v[:, k:k + 1], v[:, 8 + k:9 + k], ALU.mult,
                                ALU.add, ta, tv)
                    ht[k].append(tt(HTL[:, k, t0:t1], HTF[:, k, t0:t1], HTH[:, k, t0:t1].bitcast(F), ALU.subtract,
                                    t1_, th, eng=G if k % 2 else V))
                    late.append([ta, th])
                else:
                    late.append([ta])
                yield
            banks.free[r] = [ta]
            for k in range(8):
                new[k].append(act(XT[:, k, t0:t1], XT[:, k, t0:t1], ACT.Identity, late[k], tb,
                                  scale=gb[:, k:k + 1], bias=gb[:, 8 + k:9 + k]))
        weave([part(*x) for x in parts[::-1]], 2)
        return new, ht

    def modulate(parts, M, mj, xt, *deps):
        ht = [[] for _ in range(8)]
        for t0, t1, ci in parts:
            for k in range(8):
                sc, sh = M[:, 8 * (mj + 1) + k, ci:ci + 1], M[:, 8 * mj + k, ci:ci + 1]
                t1_ = act(HTH[:, k, t0:t1], XT[:, k, t0:t1], ACT.Identity, xt[k], deps, scale=sc, bias=sh)
                th = ts(HTF[:, k, t0:t1], XT[:, k, t0:t1], sc, sh, ALU.mult, ALU.add, xt[k], *deps)
                ht[k].append(tt(HTL[:, k, t0:t1], HTF[:, k, t0:t1], HTH[:, k, t0:t1].bitcast(F), ALU.subtract,
                                t1_, th, eng=G if k % 2 else V))
        return ht

    def ffn(w_in, w_out, t0, ht, done, beside=None):
        n = T - t0
        beside = beside or iter(())
        HH = AR[:, 0:6144].rearrange("p (f t) -> p f t", t=T)
        HL = AR[:, 6144:12288].rearrange("p (f t) -> p f t", t=T)
        HF = A[:, 6144:12288].rearrange("p (f t) -> p f t", t=T)
        start = bar()
        hfree = start
        res = [None] * 8
        for g, (f0, nf) in enumerate(((0, 8), (8, 8), (16, 6))):
            hid = []
            for c in range(0, nf, 2):
                tgs = []
                for f in range(2):
                    b, pv, tk = lin([wp(w_in, (f0 + c + f) * 128, 128)], hx, 8, t0, T, perk=ht)
                    ta = act(HF[:, c + f, 0:n], pv[:, 0:n], ACT.Silu, tk, hfree)
                    banks.free[b] = [ta]
                    tgs.append(ta)
                    next(beside, None)
                for f in range(2):
                    b, pv, tk = lin([wp(w_in, FF + (f0 + c + f) * 128, 128)], hx, 8, t0, T)
                    h = HF[:, c + f, 0:n]
                    tm = tt(h, h, pv[:, 0:n], ALU.mult, tgs[f], tk)
                    banks.free[b] = [tm]
                    hid.append([split(HH[:, c + f, 0:n], HL[:, c + f, 0:n], h, tm, hfree)])
                    next(beside, None)
            hv = (lambda k, a0, a1: HH[:, k, a0 - t0:a1 - t0], lambda k, a0, a1: HL[:, k, a0 - t0:a1 - t0])
            for m in range(8):
                b, pv, tk = lin([wp(w_out, m * 128, 128, f0 * 128, nf)], hv, nf, t0, T, perk=hid)
                res[m] = done(m, pv, tk, g)
                banks.free[b] = res[m]
                next(beside, None)
            hfree = [tk]
        return res

    def mix_out(w, r0, nk, hi, lo, parts, M, t0, *deps):
        res = []
        per = 8 // nk
        for m in range(8):
            if m % per == 0:
                i, wh, wl, tw = panel("w", nk, wp(w, m * 128, per * 128, r0, nk))
            o = 128 * (m % per)
            b, pv, tk = proj3(wh, wl, slice(o, o + 128), (lambda k, a0, a1: hi[:, k, a0 - t0:a1 - t0],
                                                          lambda k, a0, a1: lo[:, k, a0 - t0:a1 - t0]),
                              nk, t0, T, tw, deps)
            res.append(residual(M, 2, parts, t0)(m, pv, tk, 0))
            banks.free[b] = res[-1]
            if m % per == per - 1:
                release(i, tk)
        return res

    def residual(M, gj, parts, t0):
        def done(m, pv, tk, g):
            return [stt(XT[:, m, p0:p1], pv[:, p0 - t0:p1 - t0], M[:, 8 * gj + m, ci:ci + 1], XT[:, m, p0:p1],
                        ALU.mult, ALU.add, tk) for p0, p1, ci in parts]
        return done

    def layer0(xt):
        w = a["ev_w_in"][0]
        for c in range(8):
            mod_step(a["mod_w"][0], M0, c, 0, lambda x, n: vec("mod_b", x, n))
        tm0 = mod_end()
        tm0 = ts(M0[:, 8:16, :], M0[:, 8:16, :], 1.0, 1.0 / ALPHA, ALU.add, ALU.mult, tm0)
        ht = modulate(PX, M0, 0, xt, tm0)
        MIX = A[:, 18 * T:20 * T].rearrange("p (m t) -> p m t", t=T)
        MIL = AR[:, 18 * T:20 * T].rearrange("p (m t) -> p m t", t=T)
        MIH = AR[:, 20 * T:22 * T].rearrange("p (m t) -> p m t", t=T)

        def u(i, n=1):
            return A[:, i * T:(i + n) * T]
        start = bar()
        W2 = TM[0:32, 3072:3584].rearrange("p (d n) -> p d n", d=2)
        t0_ = ms(TM[0:32, 3072:3584], 0.0, start)
        tw2 = small([(W2[0:16, 0, :], a["gla_w_gate2"][0, 0]), (W2[16:32, 1, :], a["gla_w_gate2"][0, 1])], t0_)
        MK = TM[:, 3584:3840].rearrange("p (d n) -> p d n", d=2)
        tmk = small([(MK, con["glam"].rearrange("p (d n) -> p d n", d=2))], start)
        RST = TM[:, 3840:4608]
        tq = ms(RST, 1.0, start)
        trs = ms(RST.rearrange("p (c t) -> p c t", t=64)[:, :, 0], 0.0, tq)
        R = u(0)
        b, pv, tk = lin([wp(w, 1536, 32)], hx, 8, 0, T, perk=ht, M=32)
        t_r = copyS(R[0:32, :], pv[0:32, 0:T], tk, start)
        banks.free[b] = [t_r]
        nstart = mstart = bar()
        for j in range(2):
            start = nstart
            q, k_ = u(1), u(2)
            vt = u(3, 2).rearrange("p (c n) -> p c n", c=6)
            qd, kd = (u(5), u(6)), (u(7), u(8))
            klT = (u(9).rearrange("p (c n) -> p c n", c=6), u(10).rearrange("p (c n) -> p c n", c=6))
            SS = (u(11, 2).rearrange("p (c n) -> p c n", c=12), u(13, 2).rearrange("p (c n) -> p c n", c=12))
            tmp = ((u(15), u(16), u(17)), (u(22), u(23), u(10)))
            dec = (SM[:, 48:60], SM[:, 60:72])
            t_q, t_k, t_v, t_g = [], [], [], []
            t_qd, t_kd, t_S = {}, {}, {0: {}, 1: {}}
            gates = []

            def projections():
                b, pv, tk = lin([wp(w, 128 * j, 128)], hx, 8, 0, T)
                t_q.append(act(q, pv[:, 0:T], ACT.Copy, tk, start, scale=0.125))
                banks.free[b] = [t_q[-1]]
                b, pv, tk = lin([wp(w, 256 + 128 * j, 128)], hx, 8, 0, T)
                t_k.append(copyS(k_, pv[:, 0:T], tk, start))
                banks.free[b] = [t_k[-1]]
                yield
                hv = halves("w", w, 512 + 256 * j)
                for c in range(6):
                    b, pv, free = banks.take()
                    tk = xw(c * 128, hv, pv[:, 0:256], free)
                    t_v.append(copyS(vt[:, c, :], pv[:, 0:256], tk, start))
                    banks.free[b] = [t_v[-1]]
                for x in hv:
                    release(x[0], tk)
                while len(gates) < 2:
                    yield
                for hh in range(2):
                    b, pv, tk = lin([wp(w, 1024 + 256 * j + 128 * hh, 128)], hx, 8, 0, T)
                    t_g.append(act(u(15 + hh), pv[:, 0:T], ACT.Silu, tk, gates))
                    banks.free[b] = [t_g[-1]]
                for _ in range(5):
                    mod_some(1, 72 if j == 0 else 60)
                    yield

            def gate(d):
                la, kl, bb = tmp[d]
                b, pv, tk = proj(lambda k: W2[:, d, 128 * j:128 * j + 128], lambda k, a0, a1: R[0:32, a0:a1], 1,
                                 0, T, t_r, tw2)
                tz = ts(la, pv[:, 0:T], vec("gla_b", 2 * d + j), None, ALU.add, None, tk, start)
                banks.free[b] = [tz]
                te = act(kl, la, ACT.Abs, tz)
                te = act(kl, kl, ACT.Exp, te, scale=-1.0)
                te = act(kl, kl, ACT.Ln, te, t_cols, bias=onec)
                yield
                te = stt(la, la, 0.0, kl, ALU.min, ALU.subtract, te)
                sl = slice(None, None, 1 if d == 0 else -1)
                tb = V.do(lambda e, o=bb[:, sl], i_=la[:, sl]: e.tensor_tensor_scan(
                    out=o, data0=RST, data1=i_, initial=0.0, op0=ALU.mult, op1=ALU.add), te, trs)
                b3 = bb.rearrange("p (c t) -> p c t", t=64)
                bl = b3[:, :, 63:64] if d == 0 else b3[:, :, 0:1]
                tl = tt(la.rearrange("p (c t) -> p c t", t=64), bl.to_broadcast([128, 12, 64]), b3, ALU.subtract, tb)
                tdec = act(dec[d], bl.squeeze(2), ACT.Exp, tb, start, scale=1 / 16)
                te3 = act(kl, la, ACT.Exp, tl, scale=1 / 16)
                te1 = act(qd[d], bb, ACT.Exp, tb, start, scale=1 / 16)
                te2 = act(kd[d], bb, ACT.Exp, tb, start, scale=-1 / 16)
                yield
                while not t_k:
                    yield
                tl = tt(kl, kl, k_, ALU.mult, te3, t_k)
                b, pv, free = banks.take()
                for c in range(6):
                    tk = tr(pv[:, c * 128:c * 128 + 128], kl[:, c * 128:(c + 1) * 128], tl, free)
                t_qd[d] = tt(qd[d], qd[d], q, ALU.mult, te1, t_q)
                t_kd[d] = tt(kd[d], kd[d], k_, ALU.mult, te2, t_k)
                tc = cpV(klT[d], pv[:, 0:T].rearrange("p (c n) -> p c n", c=6), tk, start)
                banks.free[b] = [tc]
                gates.append([tk, tc])
                yield
                while len(t_v) < 6:
                    yield
                order = list(range(12)) if d == 0 else [3, 2, 1, 0] + list(range(11, 3, -1))
                tS = ms(SS[d][:, order[0], :], 0.0, start)
                t_S[d][order[0]] = tS
                for x in range(11):
                    c, nx = order[x], order[x + 1]
                    h0 = 64 * (c % 2)
                    b, pv, free = banks.take()
                    tk = mm(pv[:, 0:256], klT[d][h0:h0 + 64, c // 2, :], vt[h0:h0 + 64, c // 2, :], True, True,
                            tc, t_v[c // 2], free)
                    t2 = []
                    for hh in range(2):
                        r = slice(64 * hh, 64 * hh + 64)
                        t2.append(stt(SS[d][r, nx, :], SS[d][r, c, :], dec[d][r, c:c + 1],
                                      pv[r, 128 * hh:128 * hh + 128], ALU.mult, ALU.add, tk, tS, tdec))
                    tS = t2
                    banks.free[b] = tS
                    t_S[d][nx] = tS
                    if x % 2:
                        yield
            weave([gate(0), gate(1), projections()], 3)
            at = Slots([TM[:, 0:1024], G0[:, :, :].rearrange("p a b -> p (a b)")])
            at.free = [list(start), list(start)]
            t_n = []

            def output(h, p0, p1):
                r = slice(64 * h, 64 * h + 64)
                n = p1 - p0
                b, pv, free = banks.take()
                cc0 = p0 // 128
                for c in range(cc0, p1 // 128):
                    cs = slice(128 * c, 128 * c + 128)
                    for d in range(2):
                        o = 256 * (c - cc0) + 128 * d
                        tk = mm(pv[:, o:o + 128], kd[d][r, cs], qd[d][r, cs], True, True, free,
                                t_kd[d], t_qd[d])
                s, sv, sfree = at.take()
                tm = None
                for o in range(0, 2 * n, 512):
                    tm = tt(sv[:, o:o + 512].rearrange("p (c n) -> p c n", c=2),
                            pv[:, o:o + 512].rearrange("p (c n) -> p c n", c=2),
                            MK.rearrange("p d n -> p (d n)").unsqueeze(1).to_broadcast([128, 2, 256]),
                            ALU.mult, tk, sfree, tmk)
                banks.free[b] = [tm]
                yield
                bo, po, freeo = banks.take()
                for c in range(cc0, p1 // 128):
                    o = slice(128 * (c - cc0), 128 * (c - cc0) + 128)
                    for d in range(2):
                        o1 = 256 * (c - cc0) + 128 * d
                        tk = mm(po[:, o], vt[:, c, 128 * h:128 * h + 128], sv[:, o1:o1 + 128],
                                d == 0, False, tm, freeo)
                    for d in range(2):
                        for e2 in range(2):
                            cc = 2 * c + e2
                            o2 = slice(128 * (c - cc0) + 64 * e2, 128 * (c - cc0) + 64 * e2 + 64)
                            tk = mm(po[:, o2], SS[d][r, cc, :], qd[d][r, 64 * cc:64 * cc + 64], False,
                                    d == 1 and e2 == 1, t_S[d][cc])
                at.free[s] = [tk]
                to = cpV(MIX[:, h, p0:p1], po[:, 0:n], tk, mstart)
                banks.free[bo] = [to]
                yield
                ri, rv, tr_ = rstd(lambda k, a0, a1: MIX[:, h, a0:a1], 1, p0, p1, 128, to)
                yield
                tn = stt(MIX[:, h, p0:p1], rv, vec("gla_n"), MIX[:, h, p0:p1], ALU.mult, ALU.mult, tr_)
                banks.free[ri] = [tn]
                tn = tt(MIX[:, h, p0:p1], MIX[:, h, p0:p1], u(15 + h)[:, p0:p1], ALU.mult, tn, t_g)
                t_n.append(split(MIH[:, h, p0:p1], MIL[:, h, p0:p1], MIX[:, h, p0:p1], tn, mstart))
            weave([output(h, p0, p1) for h in range(2) for p0, p1, _ in PX], 2)
            if j == 0:
                tm0 = mod_until(72)
            nstart = bar()
            res = mix_out(a["ev_w_out"][0], 256 * j, 2, MIH, MIL, PX, M0, 0, t_n, tm0)
            mstart = [nstart, (P.sem, P.n)]
        start = nstart
        CO = u(6, 1)[:, 0:512]
        SI = u(7, 1)[:, 0:512]
        tcs = small([(CO, con["cos"]), (SI, con["sin"])], start)
        LP = SM[:, 0:256]
        LQ = TM[:, 3072:3328]
        tlp = small([(LQ, a["diff_lambda"][0].rearrange("a n -> (a n)").partition_broadcast(128))], start)
        l4 = LQ.rearrange("p (a n) -> p a n", a=4)
        tl = tt(LQ[:, 0:64], l4[:, 0, :], l4[:, 1, :], ALU.mult, tlp)
        tl2 = tt(LQ[:, 128:192], l4[:, 2, :], l4[:, 3, :], ALU.mult, tlp)
        lam = SM[:, 80:84]
        ta = V.do(lambda e: e.reduce_sum(lam[:, 0:1], LQ[:, 0:64], AX.X), tl)
        tb = V.do(lambda e: e.reduce_sum(lam[:, 1:2], LQ[:, 128:192], AX.X), tl2)
        tl = act(lam[:, 0:2], lam[:, 0:2], ACT.Exp, ta, tb)
        tl = tt(lam[:, 2:3], lam[:, 1:2], lam[:, 0:1], ALU.subtract, tl)
        lam_init = 0.8 - 0.6 * math.exp(0.0)
        t_lam = ts(lam[:, 2:3], lam[:, 2:3], lam_init, None, ALU.subtract, None, tl)
        hb = Slots([(u(0), u(1), u(4)), (u(14), u(15), u(16))])
        st = Slots([SM[:, 96:104], SM[:, 104:112], SM[:, 112:120]])
        es = Slots([(u(8), u(9)), (u(10), u(11)), (u(22), u(23))])
        wt = Slots([u(12), u(13)])
        for x in (hb, st, es, wt):
            x.free = [[start] for _ in x.v]
        raw, rt, vc = u(2), u(3), u(5)
        heads = {}
        rope_end = [start]
        vc_end = [start]

        def head(h):
            hi_, (qq, kk, v_), hfree = hb.take()
            vt = v_.rearrange("p (c n) -> p c n", c=6)
            toks = []
            rw = []
            for x, dst in enumerate((qq, kk)):
                b, pv, tk = lin([wp(w, 1568 + 512 * x + 128 * h, 128)], hx, 8, 0, T)
                t1 = copyS(dst[:, 0:TC], pv[:, 0:TC], tk, hfree)
                src = (raw, vc)[x][:, 0:512]
                t2 = copyS(src, pv[:, TC:T], tk, rope_end, vc_end)
                banks.free[b] = [t2]
                toks.append(t1)
                rw.append((src, t2, dst))
            yield
            for src, t2, dst in rw:
                b, pv, free = banks.take()
                tk = mm(pv[:, 0:512], perm, src, True, True, t2, free)
                t3 = tt(rt[:, 0:512], pv[:, 0:512], SI, ALU.mult, tk, tcs, rope_end)
                banks.free[b] = [t3]
                t4 = tt(src, src, CO, ALU.mult, tk, tcs)
                t5 = tt(dst[:, TC:T], src, rt[:, 0:512], ALU.add, t3, t4, hfree)
                toks.append(t5)
                rope_end[:] = [t5]
            vc_end[:] = [t5]
            b, pv, tk = lin([wp(w, 2592 + 128 * h, 128)], hx, 8, 0, T)
            t_vc = copyS(vc, pv[:, 0:T], tk, vc_end)
            banks.free[b] = [t_vc]
            yield
            b, pv, free = banks.take()
            for c in range(6):
                tk = tr(pv[:, c * 128:c * 128 + 128], vc[:, c * 128:c * 128 + 128], t_vc, free)
            t_v = copyS(vt, pv[:, 0:T].rearrange("p (c n) -> p c n", c=6), tk, hfree)
            banks.free[b] = [t_v]
            vc_end[:] = [tk]
            heads[h] = (hi_, qq, kk, vt, toks, t_v)

        t_out = {}
        t_fin = {}
        mixed = {-1: mstart}
        ends = {}

        def attend(h, qt):
            while h not in heads:
                yield
            hi_, qq, kk, vt, t_qk, t_v = heads[h]
            nk = TC if qt < 2 else T
            si, sv, sfree = st.take()
            ei, ev, efree = es.take()
            te = []
            for x in range(2):
                r = slice(64 * x, 64 * x + 64)
                b, pv, free = banks.take()
                for c0 in range(0, nk, 512):
                    c1 = min(c0 + 512, nk)
                    tk = mm(pv[:, c0:c1], qq[r, qt * 128:qt * 128 + 128], kk[r, c0:c1], True, True, free, t_qk)
                t1 = V.do(lambda e, o=sv[:, x:x + 1], i_=pv[:, 0:nk]: e.reduce_max(o, i_, AX.X), tk, sfree)
                t1 = ts(sv[:, 2 + x:3 + x], sv[:, x:x + 1], -0.125, None, ALU.mult, None, t1)
                t2 = act(ev[x][:, 0:nk], pv[:, 0:nk], ACT.Exp, t1, efree, bias=sv[:, 2 + x:3 + x],
                         scale=0.125, accum_out=sv[:, 4 + x:5 + x])
                banks.free[b] = [t2]
                te.append(t2)
            ends.setdefault(h, []).append(tk)
            yield
            t1 = rcp(sv[:, 6:8], sv[:, 4:6], te)
            t2 = tt(sv[:, 7:8], sv[:, 7:8], lam[:, 2:3], ALU.mult, t1, t_lam)
            t3 = ts(ev[1][:, 0:nk], ev[1][:, 0:nk], sv[:, 7:8], None, ALU.mult, None, t2)
            t4 = stt(ev[0][:, 0:nk], ev[0][:, 0:nk], sv[:, 6:7], ev[1][:, 0:nk], ALU.mult, ALU.add, t3)
            st.free[si] = [t4]
            b, pv, free = banks.take()
            for c in range(nk // 128):
                tk = tr(pv[:, c * 128:c * 128 + 128], ev[0][:, c * 128:c * 128 + 128], t4, free)
            es.free[ei] = [tk, t4]
            wi, wvv, wfree = wt.take()
            t5 = copyS(wvv[:, 0:nk], pv[:, 0:nk], tk, wfree)
            banks.free[b] = [t5]
            yield
            while h // 2 - 1 not in mixed:
                yield
            b, pv, free = banks.take()
            for c in range(nk // 128):
                tk = mm(pv[:, 0:128], vt[:, c, :], wvv[:, c * 128:c * 128 + 128], c == 0,
                        c == nk // 128 - 1, t5, t_v, free)
            wt.free[wi] = [tk]
            ends[h].append(tk)
            if len(ends[h]) == 12:
                hb.free[hi_] = ends[h]
            to = cpV(MIX[:, h % 2, qt * 128:qt * 128 + 128], pv[:, 0:128], tk, mixed[h // 2 - 1])
            banks.free[b] = [to]
            t_out.setdefault((h, qt >= 2), []).append(to)
            mod_some(qt % 2, 60)

        def finish(h, p0, p1):
            x = p0 >= TC
            while len(t_out.get((h, x), [])) < (4 if x else 2):
                yield
            ri, rv, tr_ = rstd(lambda k, a0, a1: MIX[:, h % 2, a0:a1], 1, p0, p1, 128, t_out[(h, x)])
            yield
            v = MIX[:, h % 2, p0:p1]
            tn = stt(v, rv, vec("diff_n"), v, ALU.mult, ALU.mult, tr_)
            banks.free[ri] = [tn]
            tn = ts(v, v, 1.0 - lam_init, None, ALU.mult, None, tn)
            t_fin.setdefault(h // 2, []).append(
                split(MIH[:, h % 2, p0:p1], MIL[:, h % 2, p0:p1], v, tn, mixed[h // 2 - 1]))

        def mix(j):
            while len(t_fin.get(j, [])) < 4:
                yield
            mixed[j] = mix_out(a["ev_w_out"][0], 512 + 256 * j, 2, MIH, MIL, PX, M0, 0, t_fin[j])
            mixed[j].append((P.sem, P.n))
        gens = [head(0)]
        for h in range(4):
            gens += [attend(h, 0), attend(h, 2)]
            if h < 3:
                gens.append(head(h + 1))
            gens += [attend(h, 1), attend(h, 3), attend(h, 4), attend(h, 5),
                     finish(h, 0, TC), finish(h, TC, T)]
            if h % 2:
                gens.append(mix(h // 2))
        weave(gens, 3)
        res = mixed[1][0:8]
        tm0 = mod_until(60)
        ts(M0[:, 32:40, :], M0[:, 32:40, :], 1.0, 1.0 / ALPHA, ALU.add, ALU.mult, tm0)
        xt, ht = layer_norm(0, 0, PX, ALPHA, M0, 3, res)
        res = ffn(a["ffn_w_in"][0], a["ffn_w_out"][0], 0, ht, residual(M0, 5, PX, 0), mod_pace(24))
        tm1 = mod_until(36)
        ln_layer(1, M1, tm1)
        return layer_norm(0, 1, PX, ALPHA, M1, 0, res)

    def layer1(xt, ht):
        w = a["ssd_w_in"][0]
        start = bar()
        at = [0]

        def al(n, buf=A):
            at[0] += n
            return A[:, at[0] - n:at[0]]
        YF = al(2048).rearrange("p (m t) -> p m t", t=512)
        YL = AR[:, 0:2048].rearrange("p (m t) -> p m t", t=512)
        YH = AR[:, 2048:4096].rearrange("p (m t) -> p m t", t=512)
        al(2048)
        xs = al(3072).rearrange("p (c n) -> p c n", c=6)
        zz = al(2048).rearrange("p (c n) -> p c n", c=4)
        Bc = al(768)
        Cc = al(768)
        Bt = al(768).rearrange("p (c n) -> p c n", c=6)
        assert at[0] == 11520
        SS = al(4096).rearrange("p (d c n) -> p d c n", d=2, c=4)
        DT = TM[:, 0:384].rearrange("p (c h) -> p c h", c=6)
        DA = TM[:, 384:768].rearrange("p (c h) -> p c h", c=6)
        AC = TM[:, 768:1152].rearrange("p (c h) -> p c h", c=6)
        ED = TM[:, 1152:1536].rearrange("p (c h) -> p c h", c=6)
        EL = TM[:, 1536:1920].rearrange("p (c h) -> p c h", c=6)
        EA = TM[:, 1920:2304].rearrange("p (c h) -> p c h", c=6)
        row = TM[:, 2304:2464]
        tro = small([(row[:, 0:64], a["ssd_dt_bias"][0].rearrange("a n -> (a n)").partition_broadcast(128)),
                     (row[:, 64:128], a["ssd_a_log"][0].rearrange("a n -> (a n)").partition_broadcast(128)),
                     (row[:, 128:160], a["ssd_d"][0].partition_broadcast(128))], start)
        MN = TM[:, 2560:2816].rearrange("p (d n) -> p d n", d=2)
        tmn = small([(MN, con["minm"].rearrange("p (d n) -> p d n", d=2))], start)
        ta = act(row[:, 64:128], row[:, 64:128], ACT.Exp, tro)
        b, pv, tk = lin([wp(w, 5120, 64)], hx, 8, 0, T, perk=ht, M=64)
        dtc = TM[0:64, 2816:3584]
        t1 = copyS(dtc, pv[0:64, 0:T], tk, start)
        banks.free[b] = [t1]
        b, pv, free = banks.take()
        for c in range(6):
            tk = tr(pv[:, c * 64:c * 64 + 64], dtc[:, c * 128:c * 128 + 128], t1, free, n=64)
        p6 = pv[:, 0:384].rearrange("p (c h) -> p c h", c=6)
        t1 = tt(DT, p6, row[:, 0:64].unsqueeze(1).to_broadcast([128, 6, 64]), ALU.add, tk, tro, start)
        banks.free[b] = [t1]
        t2 = act(DA, DT, ACT.Abs, t1)
        t2 = act(DA, DA, ACT.Exp, t2, scale=-1.0)
        t2 = act(DA, DA, ACT.Ln, t2, bias=onec)
        t2 = stt(DT, DT, 0.0, DA, ALU.max, ALU.add, t2)
        t_dt = t2
        t2 = stt(DA, DT, -1.0, row[:, 64:128].unsqueeze(1).to_broadcast([128, 6, 64]), ALU.mult, ALU.mult, t2, ta)
        t_da = t2
        b, pv, free = banks.take()
        for c in range(6):
            mm(pv[:, c * 64:c * 64 + 32], triF, DA[:, c, 0:32], True, True, t2, free)
            mm(pv[:, c * 64 + 32:c * 64 + 64], triB, DA[:, c, 32:64], True, True)
            tk = mm(pv[:, 512 + c * 64:576 + c * 64], ones[:, :].to_broadcast([128, 128]), DA[:, c, :], True, True)
        p6 = pv[:, 0:384].rearrange("p (c h) -> p c h", c=6)
        p7 = pv[:, 512:896].rearrange("p (c h) -> p c h", c=6)
        t1 = cpV(AC, p6, tk)
        t3 = act(ED, p7, ACT.Exp, tk, start)
        t4 = tt(EL, p7, AC, ALU.subtract, t1, t3)
        banks.free[b] = [t3, t4]
        t4 = act(EL, EL, ACT.Exp, t4)
        t_el = tt(EL, EL, DT, ALU.mult, t4)
        t_ea = act(EA, AC, ACT.Exp, t1, start)
        t_ac = [t1, t3]
        sets = [(A[:, 11520 + 776 * x:12296 + 776 * x], v) for x, v in enumerate(
            (A[:, 13848:14620], A[:, 14620:15392], TM[:, 3584:4356]))]

        nstart = bar()
        ymix, mixes, shares = [], [], {}
        for g in range(4):
            start = nstart
            cvs = Slots(sets)
            cvs.free = []
            for cvb, _ in sets:
                ms(cvb[:, 0:2], 0.0, start)
                ms(cvb[:, 258:262], 0.0)
                cvs.free.append([ms(cvb[:, 774:776], 0.0), start])
            tbc = {}
            t_bt, t_xs, t_zz = [], [], {}

            def conv(ch, col, fin):
                si, (cvb, cv), sfree = cvs.take()
                b, pv, tk = lin([wp(w, col, 128)], hx, 8, 0, T)
                t1 = copyS(cvb[:, 2:258], pv[:, 0:TC], tk, sfree)
                t2 = copyS(cvb[:, 262:774], pv[:, TC:T], tk)
                banks.free[b] = [t2]
                yield
                prev = ts(cv, cvb[:, 0:772], vec("conv_w", ch), vec("conv_b", ch), ALU.mult, ALU.add, t1, t2, sfree)
                for s_ in range(1, 5):
                    prev = stt(cv, cvb[:, s_:s_ + 772], vec("conv_w", s_ * 24 + ch), cv, ALU.mult, ALU.add, prev)
                if fin == "xs":
                    m = ch - 4 * g
                    ta = act(cv, cv, ACT.Silu, prev)
                    src = cv
                else:
                    src = Bc if fin == "B" else Cc
                    ta = act(src[:, 0:TC], cv[:, 0:TC], ACT.Silu, prev, start)
                    ta = act(src[:, TC:T], cv[:, 260:772], ACT.Silu, prev)
                    tbc[fin] = ta
                cvs.free[si] = [ta]
                if fin == "C":
                    return
                cvs.free[si] = None
                yield
                b, pv, free = banks.take()
                for c in range(6):
                    o = c * 128 + (4 if fin == "xs" and c >= 2 else 0)
                    tk = tr(pv[:, c * 128:c * 128 + 128], src[:, o:o + 128], ta, free)
                dst = Bt if fin == "B" else xs[:, :, m * 128:m * 128 + 128]
                tq = (copyS if ch % 2 else cpV)(dst, pv[:, 0:T].rearrange("p (c n) -> p c n", c=6), tk, start)
                banks.free[b] = [tq]
                (t_bt if fin == "B" else t_xs).append(tq)
                cvs.free[si] = [tk, ta]

            def zproj(x):
                hv = halves("w", w, 512 * g + 256 * x)
                for c in range(4):
                    b, pv, free = banks.take()
                    tk = xw(TC + c * 128, hv, pv[:, 0:256], free)
                    t_zz[(c, x)] = act(zz[:, c, 256 * x:256 * x + 256], pv[:, 0:256], ACT.Silu, tk, start)
                    banks.free[b] = [t_zz[(c, x)]]
                    if c == 3:
                        for y in hv:
                            release(y[0], tk)
                    yield
                    if x:
                        yield
            gens = [conv(16 + g, 4096 + 128 * g, "B"), conv(20 + g, 4608 + 128 * g, "C")]
            gens += [conv(4 * g + m, 2048 + 512 * g + 128 * m, "xs") for m in range(4)]
            if g:
                gens.insert(2, mixgen(g - 1))
            weave(gens, 3)
            work = TM[:, 2816:4992]
            w1 = Slots([work[:, 0:512], work[:, 512:1024]])
            conv_end = [x for x in cvs.free]
            w1.free = [[conv_end], [conv_end]]
            cur = [work[:, 1024:1536], work[:, 1536:2048]]
            tS = {}

            def h8(v):
                return v.rearrange("p (h n) -> p h n", h=8)

            def hb(v, n=64):
                return v.unsqueeze(2).to_broadcast([128, 8, n])

            def states(d):
                order = [0, 1, 2, 3, 4] if d == 0 else [1, 0, 5, 4, 3]
                hs = slice(32 * d + 8 * g, 32 * d + 8 * g + 8)
                prev = None
                src = None
                for x, c in enumerate(order):
                    wi, wvv, wfree = w1.take()
                    t1 = tt(h8(wvv), h8(xs[:, c, :]), hb(EL[:, c, hs]), ALU.mult, wfree, t_xs, t_el)
                    b, pv, free = banks.take()
                    tk = mm(pv[:, 0:512], Bt[:, c, :], wvv, True, True, t1, t_bt, free)
                    w1.free[wi] = [tk]
                    nx = (order + [5 if d == 0 else 2])[x + 1]
                    dst = SS[:, d, nx - 2, :] if nx >= 2 else cur[d]
                    if src is not None:
                        t2 = tt(h8(dst), h8(src), hb(ED[:, c, hs]), ALU.mult, prev, t_ac, conv_end)
                    banks.free[b] = None
                    yield
                    if src is None:
                        prev = cpV(dst, pv[:, 0:512], tk, conv_end)
                    else:
                        prev = tt(dst, dst, pv[:, 0:512], ALU.add, t2, tk)
                    banks.free[b] = [prev]
                    src = dst
                    tS[(d, nx)] = prev

            def fill(n):
                for _ in range(n):
                    yield
            weave([states(0), states(1), zproj(0), fill(4)], 3)
            xd = Slots([work[:, 0:512], work[:, 512:1024]])
            yy_ = Slots([work[:, 1152:1664], A[:, 16640:17152]])
            yo_ = Slots([work[:, 1664:2176], A[:, 17152:17664]])
            cb_ = Slots([work[:, 1024:1152], A[:, 17664:17792]])
            G1 = A[:, 15616:16640].rearrange("p (h n) -> p h n", h=8)
            GG = Slots([G0[:, :, :], G1])
            work_end = [w1.free, (P.sem, P.n), (V.sem, V.n)]
            for x in (xd, yy_, yo_, cb_, GG):
                x.free = [[work_end, start] for _ in x.v]
            t_out = []
            shared = {}

            def unit(c, d):
                cs = slice(c * 128, c * 128 + 128)
                hs0 = 32 * d + 8 * g
                hs = slice(hs0, hs0 + 8)
                tri = triF if d == 0 else triB
                if d == 0:
                    ci, cbt, cfree = cb_.take()
                    b, pv, free = banks.take()
                    tcb = mm(pv[:, 0:128], Bc[:, cs], Cc[:, cs], True, True, free, tbc["B"], tbc["C"])
                    tcb = copyS(cbt, pv[:, 0:128], tcb, cfree)
                    banks.free[b] = [tcb]
                    shared[c] = [ci, cbt, tcb]
                ci, cbt, tcb = shared[c][0:3]
                gi, gg, gfree = GG.take()
                b, pv, free = banks.take()
                for h in range(8):
                    tk = mm(pv[:, 128 * h:128 * h + 128],
                            DA[:, c, hs0 + h:hs0 + h + 1].to_broadcast([128, 128]), tri, True, True, free, t_da)
                for h in range(8):
                    t1 = stt(gg[:, h, :], pv[:, 128 * h:128 * h + 128], AC[:, c, hs0 + h:hs0 + h + 1],
                             MN[:, d, :], ALU.subtract, ALU.min, tk, t_ac, tmn, gfree)
                banks.free[b] = [t1]
                t2 = act(gg, gg, ACT.Exp, t1)
                xi, xdv, xfree = xd.take()
                txd = tt(h8(xdv), h8(xs[:, c, :]), hb(DT[:, c, hs]), ALU.mult, xfree, t_xs, t_dt, eng=G)
                yield
                tG = tt(gg, gg, cbt.unsqueeze(1).to_broadcast([128, 8, 128]), ALU.mult, t2, tcb)
                if d:
                    cb_.free[ci] = [tG]
                b, pv, free = banks.take()
                tk2 = mm(pv[:, 512:1024], Cc[:, cs], SS[:, d, c - 2, :], True, True, tS[(d, c)], free)
                for h in range(8):
                    tk = mm(pv[:, 64 * h:64 * h + 64], gg[:, h, :], xdv[:, 64 * h:64 * h + 64], True, True, tG, txd)
                GG.free[gi] = [tk]
                xd.free[xi] = [tk]
                if d == 0:
                    yi, yy, yfree = yy_.take()
                    oi, yo, ofree = yo_.take()
                    shared[c] += [yi, yy, oi, yo]
                    t1 = tt(h8(yy), h8(pv[:, 512:1024]), hb(EA[:, c, hs]), ALU.mult, tk2, t_ea, yfree)
                    t1 = tt(yy, yy, pv[:, 0:512], ALU.add, t1, tk)
                    t2 = tt(h8(yo), h8(xs[:, c, :]), hb(row[:, 128 + 8 * g:136 + 8 * g]), ALU.mult, ofree, tro,
                            eng=G)
                    banks.free[b] = [t1]
                    shared[c].append(tt(yy, yy, yo, ALU.add, t1, t2))
                    return
                yi, yy, oi, yo, t1 = shared[c][3:8]
                t2 = tt(h8(yo), h8(pv[:, 512:1024]), hb(EA[:, c, hs]), ALU.mult, tk2, t_ea, t1)
                t1 = tt(yy, yy, pv[:, 0:512], ALU.add, t1, tk)
                banks.free[b] = [t1, t2]
                t1 = tt(yy, yy, yo, ALU.add, t1, t2)
                t1 = tt(yy, yy, zz[:, c - 2, :], ALU.mult, t1, t_zz[(c - 2, 0)], t_zz[(c - 2, 1)])
                rs = SM[:, 112 + 4 * (c % 2):116 + 4 * (c % 2)]
                t2 = act(yo, yy, ACT.Square, t1, accum_out=rs[:, 0:1])
                yo_.free[oi] = [t2]
                t2 = act(rs[:, 1:2], rs[:, 0:1], ACT.Sqrt, t2, bias=epsc, scale=1.0 / 512)
                yield
                t2 = rcp(rs[:, 2:3], rs[:, 1:2], t2)
                t1 = ts(yy, yy, rs[:, 2:3], None, ALU.mult, None, t2)
                b, pv, free = banks.take()
                for m in range(4):
                    tk = tr(pv[:, m * 128:m * 128 + 128], yy[:, m * 128:m * 128 + 128], t1, free)
                t3 = tt(YF[:, :, (c - 2) * 128:(c - 2) * 128 + 128], pv[:, 0:512].rearrange("p (m t) -> p m t", m=4),
                        vec("ssd_n", 4 * g, 4).unsqueeze(2).to_broadcast([128, 4, 128]), ALU.mult, tk, start, ymix)
                banks.free[b] = [t3]
                yy_.free[yi] = [tk]
                t_out.append(t3)

            def z_rest():
                yield from zproj(1)
                yield from fill(16)
            weave([z_rest()] + [unit(c, d) for c in range(2, 6) for d in range(2)], 3)
            nstart = bar()
            tsp = split(YH, YL, YF, t_out, ymix)
            shares[g] = tsp

            def mixgen(g):
                mixes.append(mix_out(a["ssd_w_out"][0], 512 * g, 4, YH, YL, XX, M1, TC, shares[g]))
                ymix[:] = [(P.sem, P.n)]
                yield
        for _ in mixgen(3):
            pass
        res = mixes[-1]
        xt, ht = layer_norm(1, 0, XX, ALPHA, M1, 3, res)
        res = ffn(a["ffn_w_in"][1], a["ffn_w_out"][1], TC, ht, residual(M1, 5, XX, TC), mod_pace(0))
        return layer_norm(1, 1, XX, 1.0, M1, None, res)[0]

    def pre(j, parts, xt):
        ht = [[] for _ in range(8)]
        start = bar()

        def part(t0, t1, ci):
            gg = SM[:, 208 + 8 * ci:216 + 8 * ci]
            tg = ts(gg, M2[:, 8 * (3 * j + 1):8 * (3 * j + 1) + 8, ci], 1.0, None, ALU.add, None, start)
            tg = tt(gg, gg, vec("npre", 8 * j, 8), ALU.mult, tg)
            r, rv, tr_ = rstd(lambda k, a0, a1: XT[:, k, a0:a1], 8, t0, t1, D, perk=xt)
            yield
            for k in range(8):
                ta = stt(HTF[:, k, t0:t1], XT[:, k, t0:t1], gg[:, k:k + 1], rv, ALU.mult, ALU.mult,
                         tr_, start, tg)
                sh = M2[:, 8 * 3 * j + k, ci:ci + 1]
                tc = act(HTH[:, k, t0:t1], HTF[:, k, t0:t1], ACT.Identity, ta, bias=sh)
                if k % 2:
                    td = act(HTF[:, k, t0:t1], HTF[:, k, t0:t1], ACT.Identity, tc, bias=sh)
                    ht[k].append(tt(HTL[:, k, t0:t1], HTF[:, k, t0:t1], HTH[:, k, t0:t1].bitcast(F),
                                    ALU.subtract, td, eng=G))
                else:
                    ht[k].append(stt(HTL[:, k, t0:t1], HTF[:, k, t0:t1], sh, HTH[:, k, t0:t1].bitcast(F), ALU.add,
                                     ALU.subtract, tc))
                yield
            banks.free[r] = [ta]
        weave([part(*x) for x in parts[::-1]], 2)
        return ht

    def post(j, parts, yt, wgt, YA):
        xt = [[] for _ in range(8)]
        start = bar()

        def part(t0, t1, ci):
            gg = SM[:, 224 + 8 * ci:232 + 8 * ci]
            tg = stt(gg, M2[:, 8 * (3 * j + 2):8 * (3 * j + 2) + 8, ci], wgt, vec("npost", 8 * j, 8), ALU.mult,
                     ALU.mult, start)
            r, rv, tr_ = rstd(lambda k, a0, a1: YA[:, k, a0:a1], 8, t0, t1, D, perk=yt)
            yield
            for k in range(8):
                ta = stt(YA[:, k, t0:t1], YA[:, k, t0:t1], gg[:, k:k + 1], rv, ALU.mult, ALU.mult,
                         tr_, tg)
                xt[k].append(tt(XT[:, k, t0:t1], XT[:, k, t0:t1], YA[:, k, t0:t1], ALU.add, ta, eng=G if k % 2 else V))
                yield
            banks.free[r] = [ta]
        weave([part(*x) for x in parts[::-1]], 2)
        return xt

    YA = A[:, 12288:18432].rearrange("p (m t) -> p m t", t=T)

    def to_ya(t0):
        def done(m, pv, tk, g):
            if g == 0:
                return [copyS(YA[:, m, t0:T], pv[:, 0:T - t0], tk)]
            return [tt(YA[:, m, t0:T], YA[:, m, t0:T], pv[:, 0:T - t0], ALU.add, tk)]
        return done

    def block2(xt):
        start = bar()
        l2 = load_tokens(a["ctx_2"], 2, 0, 1.0, start)
        xt = [x + [y] for x, y in zip(xt, l2)]
        tm = mod_until(0)
        ht = pre(0, PX, xt)
        res = ffn(a["ffn1_w_in_2"][0], a["ffn1_w_out_2"][0], 0, ht, to_ya(0))
        xt = post(0, PX, res, 0.5, YA)
        ht = pre(1, PX, xt)
        w = a["mix_w_in_2"][0]
        start = bar()
        at = [0]

        def al(n):
            at[0] += n
            return A[:, at[0] - n:at[0]]

        def parts3(c):
            return (A[:, c:c + 2048].rearrange("p (m t) -> p m t", t=512),
                    AR[:, c + 2048:c + 4096].rearrange("p (m t) -> p m t", t=512),
                    AR[:, c:c + 2048].rearrange("p (m t) -> p m t", t=512))
        OH, OHH, OHL = parts3(0)
        OA, OAH, OAL = parts3(4096)
        start = bar()
        at[0] = 4096
        MK = al(14 * 128).rearrange("p (d n) -> p d n", d=14)
        tmk = small([(MK, con["hgm"].rearrange("p (d n) -> p d n", d=14))], start)
        RST = TM[:, 0:768]
        t1 = ms(RST, 1.0, start)
        trs = ms(RST.rearrange("p (c t) -> p c t", t=128)[:, :, 0], 0.0, t1)
        LB = SM[:, 160:184]
        tl = []
        for d, key in enumerate(("lbf", "lbb")):
            x0, x1 = vec(key, 0, 4), vec(key, 4, 4)
            mx, e0, e1 = LB[:, 0:4], LB[:, 4:8], LB[:, 8:12]
            lb, om = LB[:, 12 + 4 * d:16 + 4 * d], SM[:, 184 + 4 * d:188 + 4 * d]
            t1 = tt(mx, x0, x1, ALU.max, start, tl)
            t2 = tt(e0, x0, mx, ALU.subtract, t1)
            t3 = tt(e1, x1, mx, ALU.subtract, t1)
            t2 = act(LB[:, 4:12], LB[:, 4:12], ACT.Exp, t2, t3)
            t3 = tt(e1, e0, e1, ALU.add, t2)
            t3 = rcp(e1, e1, t3)
            t3 = tt(lb, e0, e1, ALU.mult, t3)
            t4 = ts(om, lb, -1.0, 1.0, ALU.mult, ALU.add, t3)
            tl = [t4]
        sets = [(al(512), (al(768), al(768)), (al(768), al(768)), al(768).rearrange("p (c n) -> p c n", c=6)),
                (G0[:, 0:4, :].rearrange("p a b -> p (a b)"), (TM[:, 1024:1792], TM[:, 1792:2560]),
                 (TM[:, 2560:3328], TM[:, 3328:4096]), TM[:, 4096:4864].rearrange("p (c n) -> p c n", c=6))]
        kl = al(768)
        klT = al(768).rearrange("p (c n) -> p c n", c=6)
        SS = al(8 * 128).rearrange("p (d c n) -> p d c n", d=2, c=4)
        cur = (al(128), al(128))
        SCT, ET, QT, KT, BT = al(1024), al(1024), al(1024), al(1024), al(1024)
        SC, QB = ((x[:, 0:512], x[:, 512:1024]) for x in (SCT, BT))
        EE, QQ, KK = (Slots([x[:, 0:512], x[:, 512:1024]]) for x in (ET, QT, KT))
        DC = SM[:, 192:204]
        klf = [start]
        ins = {}

        def inputs(h, *free):
            q, kx, bx, vt = sets[h % 2]
            c0 = 768 + 128 * h
            b, pv, tk = lin([wp(w, c0, 128)], hx, 8, TC, T, perk=ht)
            t_q = act(q, pv[:, 0:512], ACT.Silu, tk, free)
            banks.free[b] = [t_q]
            b, pv, tk = lin([wp(w, c0 + 1536, 128)], hx, 8, 0, T)
            t_vc = copyS(kl, pv[:, 0:T], tk, klf)
            banks.free[b] = [t_vc]
            yield
            t_s = []
            for d in range(2):
                b, pv, tk = lin([wp(w, c0 + 512 + 512 * d, 128)], hx, 8, 0, T)
                t_s.append(act(kx[d], pv[:, 0:T], ACT.Sigmoid, tk, free))
                banks.free[b] = [t_s[-1]]
                if d == 0:
                    b, pv, free_ = banks.take()
                    for c in range(6):
                        tk = tr(pv[:, c * 128:c * 128 + 128], kl[:, c * 128:c * 128 + 128], t_vc, free_)
                    t_v = copyS(vt, pv[:, 0:T].rearrange("p (c n) -> p c n", c=6), tk, free)
                    banks.free[b] = [t_v]
                    klf[:] = [tk]
                yield
            t_kb = []
            for d in range(2):
                t2 = ts(kl, kx[d], SM[:, 184 + 4 * d + h:185 + 4 * d + h], LB[:, 12 + 4 * d + h:13 + 4 * d + h],
                        ALU.mult, ALU.add, t_s[d], tl, klf)
                t3 = ts(kx[d], kl, -1.0, 1.0, ALU.mult, ALU.add, t2)
                t4 = act(kl, kl, ACT.Ln, t3)
                yield
                sl = slice(None, None, 1 if d == 0 else -1)
                tb = V.do(lambda e, o=bx[d][:, sl], i_=kl[:, sl]: e.tensor_tensor_scan(
                    out=o, data0=RST, data1=i_, initial=0.0, op0=ALU.mult, op1=ALU.add), t4, trs, free)
                t_kb.append([t3, tb])
                klf[:] = [tb]
                yield
            ins[h] = (t_q, t_kb, [t_v])
        for _ in inputs(0, start):
            pass
        for h in range(4):
            start = bar()
            for s_ in (EE, QQ, KK):
                s_.free = [[start], [start]]
            q, kx, bx, vt = sets[h % 2]
            t_q, t_kb, t_v = ins[h]
            t_S = {0: {}, 1: {}}

            def chain(h):
                kT = [start]
                for d in range(2):
                    b3 = bx[d].rearrange("p (c t) -> p c t", t=128)
                    bl = b3[:, :, 127:128] if d == 0 else b3[:, :, 0:1]
                    dec = DC[:, 6 * d:6 * d + 6]
                    tdec = act(dec, bl.squeeze(2), ACT.Exp, t_kb[d], start)
                    t5 = tt(kl.rearrange("p (c t) -> p c t", t=128), bl.to_broadcast([128, 6, 128]), b3,
                            ALU.subtract, t_kb[d], klf)
                    t5 = act(kl, kl, ACT.Exp, t5)
                    yield
                    t5 = tt(kl, kl, kx[d], ALU.mult, t5)
                    b, pv, free = banks.take()
                    for c in range(6):
                        tk2 = tr(pv[:, c * 128:c * 128 + 128], kl[:, c * 128:c * 128 + 128], t5, free)
                    klf[:] = [tk2]
                    banks.free[b] = None
                    yield
                    t6 = copyS(klT, pv[:, 0:T].rearrange("p (c n) -> p c n", c=6), tk2, kT)
                    banks.free[b] = [t6]
                    order = [0, 1, 2, 3, 4] if d == 0 else [1, 0, 5, 4, 3]
                    src, prev = None, None
                    for x, c in enumerate(order):
                        b, pv, free = banks.take()
                        tk2 = mm(pv[:, 0:128], klT[:, c, :], vt[:, c, :], True, True, t6, t_v, free)
                        nx = (order + [5 if d == 0 else 2])[x + 1]
                        dst = SS[:, d, nx - 2, :] if nx >= 2 else cur[d]
                        banks.free[b] = None
                        yield
                        if src is None:
                            prev = cpV(dst, pv[:, 0:128], tk2, start)
                        else:
                            prev = stt(dst, src, dec[:, c:c + 1], pv[:, 0:128], ALU.mult, ALU.add, tk2, prev,
                                       tdec)
                        banks.free[b] = [prev]
                        src = dst
                        t_S[d][nx] = prev
                    kT = [tk2]
                if h < 3:
                    yield from inputs(h + 1, start)
            tsc = {}

            def level(d, lv):
                if lv == 7:
                    b, pv, free = banks.take()
                    for c in range(4):
                        tk = mm(pv[:, c * 128:c * 128 + 128], kx[d][:, TC + c * 128:TC + c * 128 + 128],
                                q[:, c * 128:c * 128 + 128], True, True, free, t_kb[d], t_q)
                    mask = ident
                else:
                    m = 64 >> lv
                    b4 = bx[d][:, TC:T].rearrange("p (c e m) -> p c e m", e=2, m=m)
                    nb = 512 // (2 * m)
                    ei, ev, efree = EE.take()
                    e4 = ev.rearrange("p (c e m) -> p c e m", e=2, m=m)
                    ref = b4[:, :, 0, m - 1:m] if d == 0 else b4[:, :, 1, 0:1]
                    ref = ref.to_broadcast([128, nb, m])
                    up, dn = (1, 0) if d == 0 else (0, 1)
                    t1 = tt(e4[:, :, up, :], b4[:, :, up, :], ref, ALU.subtract, efree, t_kb[d])
                    t2 = tt(e4[:, :, dn, :], ref, b4[:, :, dn, :], ALU.subtract)
                    t2 = act(ev, ev, ACT.Exp, t1, t2)
                    qi, qv, qfree = QQ.take()
                    ki, kv_, kfree = KK.take()
                    t3 = tt(qv, q, ev, ALU.mult, t2, qfree, t_q, eng=G)
                    yield
                    t4 = tt(kv_, kx[d][:, TC:T], ev, ALU.mult, t2, kfree, t_kb[d])
                    EE.free[ei] = [t3, t4]
                    b, pv, free = banks.take()
                    for c in range(4):
                        tk = mm(pv[:, c * 128:c * 128 + 128], kv_[:, c * 128:c * 128 + 128],
                                qv[:, c * 128:c * 128 + 128], True, True, free, t3, t4)
                    QQ.free[qi] = [tk]
                    KK.free[ki] = [tk]
                    mask = MK[:, 7 * d + lv, :]
                banks.free[b] = None
                yield
                while lv != 7 and d not in tsc:
                    yield
                p4 = pv[:, 0:512].rearrange("p (c n) -> p c n", c=4)
                s4 = SC[d].rearrange("p (c n) -> p c n", c=4)
                mb = mask.unsqueeze(1).to_broadcast([128, 4, 128])
                if lv == 7:
                    tsc[d] = tt(s4, p4, mb, ALU.mult, tk, tmk, start)
                else:
                    tsc[d] = V.do(lambda e, o=s4, m_=mb.bitcast(U32), i_=p4: e.copy_predicated(o, m_, i_), tk,
                                  tsc[d])
                banks.free[b] = [tsc[d]]
            gens = [chain(h)]
            for d in range(2):
                gens += [level(d, lv) for lv in (7, 0, 1, 2, 3, 4, 5, 6)]
            weave(gens, 3)
            t_sc = [tsc[0], tsc[1]]
            t_qb = []
            for d in range(2):
                t1 = act(QB[d], bx[d][:, TC:T], ACT.Exp, t_kb[d], start)
                t_qb.append(tt(QB[d], QB[d], q, ALU.mult, t1, t_q))
            b, pv, free = banks.take()
            for c in range(4):
                cs = slice(c * 128, c * 128 + 128)
                mm(pv[:, cs], vt[:, 2 + c, :], SC[0][:, cs], True, False, t_sc, free, t_v)
                mm(pv[:, cs], vt[:, 2 + c, :], SC[1][:, cs], False, False)
                mm(pv[:, cs], SS[:, 0, c, :], QB[0][:, cs], False, False, t_qb, t_S[0][c + 2], t_S[1][c + 2])
                tk = mm(pv[:, cs], SS[:, 1, c, :], QB[1][:, cs], False, True)
            t1 = copyS(OH[:, h, :], pv[:, 0:512], tk, start)
            banks.free[b] = [t1]
            if h == 0:
                t_oh = []
            t_oh.append([t1])
        ri, rv, tr_ = rstd(lambda k, a0, a1: OH[:, k, a0 - TC:a1 - TC], 4, TC, T, 512, perk=t_oh)
        t_r = []
        start = bar()
        for m in range(4):
            ta = stt(OH[:, m, :], OH[:, m, :], vec("hgn", m), rv, ALU.mult, ALU.mult, tr_)
            b, pv, tk = lin([wp(w, 2816 + 128 * m, 128)], hx, 8, TC, T)
            s, sv, sfree = sqb.take()
            tb = act(sv, pv[:, 0:512], ACT.Silu, tk, sfree)
            banks.free[b] = [tb]
            t2 = tt(OH[:, m, :], OH[:, m, :], sv, ALU.mult, ta, tb)
            sqb.free[s] = [t2]
            t_r.append(split(OHH[:, m, :], OHL[:, m, :], OH[:, m, :], t2))
        banks.free[ri] = [t2]
        start = bar()
        at[0] = 8192
        CO, SI = al(512), al(512)
        WM = al(256).rearrange("p (d n) -> p d n", d=2)
        q = al(2048).rearrange("p (m t) -> p m t", t=512)
        kk = al(1536).rearrange("p (m t) -> p m t", t=768)
        vt = al(768).rearrange("p (c n) -> p c n", c=6)
        rr = al(1024)
        raw, rt = rr[:, 0:512], rr[:, 512:1024]
        tcs = small([(CO, con["cos"]), (SI, con["sin"]), (WM, con["winm"].rearrange("p (d n) -> p d n", d=2))],
                    start)
        SK = SM[:, 136:144]
        tsk = small([(SK, a["attn_sink_2"][0].partition_broadcast(128))], start)
        tprev = [None]

        def rope(dst, t_raw):
            b, pv, free = banks.take()
            tk = mm(pv[:, 0:512], perm, raw, True, True, t_raw, free)
            t3 = tt(rt, pv[:, 0:512], SI, ALU.mult, tk, tcs)
            banks.free[b] = [t3]
            t4 = tt(raw, raw, CO, ALU.mult, tk)
            tprev[0] = tt(dst, raw, rt, ALU.add, t3, t4)
            return tprev[0]
        b, pv, tk = lin([wp(w, 640, 128)], hx, 8, 0, T)
        t_vc = copyS(rr[:, 0:T], pv[:, 0:T], tk, start)
        banks.free[b] = [t_vc]
        b, pv, free = banks.take()
        for c in range(6):
            tk = tr(pv[:, c * 128:c * 128 + 128], rr[:, c * 128:c * 128 + 128], t_vc, free)
        t_v = copyS(vt, pv[:, 0:T].rearrange("p (c n) -> p c n", c=6), tk)
        banks.free[b] = [t_v]
        tprev[0] = t_v
        t_q = []
        for m in range(4):
            b, pv, tk = lin([wp(w, 128 * m, 128)], hx, 8, TC, T)
            t1 = copyS(raw, pv[:, 0:512], tk, tprev[0], start)
            banks.free[b] = [t1]
            t_q.append(rope(q[:, m, :], t1))
        t_k = []
        for m in range(2):
            b, pv, tk = lin([wp(w, 512 + 64 * m, 64), wp(w, 512 + 64 * m, 64)], hx, 8, 0, T)
            t_k.append(copyS(kk[:, m, 0:TC], pv[:, 0:TC], tk))
            t1 = copyS(raw, pv[:, TC:T], tk, tprev[0])
            banks.free[b] = [t1]
            t_k.append(rope(kk[:, m, TC:T], t1))
        st = Slots([SM[:, 144:152], SM[:, 152:160], SM[:, 240:248]])
        es = Slots([al(640), al(640), TM[:, 3072:3712]])
        wt = Slots([al(640), al(640), TM[:, 3712:4352]])
        oo = Slots([al(512), al(512)])
        for s_ in (st, es, wt, oo):
            s_.free = [[start] for _ in s_.v]
        outs = {}

        def wunit(n, h):
            lo = 0 if n > 0 else 128
            hi = 384 if n < 3 else 256
            nb = hi - lo
            nk = nb + TC
            kv = h // 4
            r = slice(64 * (h % 2), 64 * (h % 2) + 64)
            si, sv, sfree = st.take()
            ei, ev, efree = es.take()
            b, pv, free = banks.take()
            k0 = TC + (n - 1) * 128 + lo
            lq = q[r, h // 2, n * 128:n * 128 + 128]
            mm(pv[:, 0:nb], lq, kk[r, kv, k0:k0 + nb], True, True, free, t_q, t_k)
            tk = mm(pv[:, 512:768], lq, kk[r, kv, 0:TC], True, True)
            ts_ = [act(ev[:, nb:nk], pv[:, 512:768], ACT.Copy, tk, efree, scale=0.125)]
            mid = 128 - lo
            if n > 0:
                ts_.append(stt(ev[:, 0:128], pv[:, 0:128], 0.125, WM[:, 0, :], ALU.mult, ALU.add, tk, efree, tcs))
            ts_.append(ts(ev[:, mid:mid + 128], pv[:, mid:mid + 128], 0.125, None, ALU.mult, None, tk, efree))
            if n < 3:
                ts_.append(stt(ev[:, mid + 128:mid + 256], pv[:, mid + 128:mid + 256], 0.125, WM[:, 1, :],
                               ALU.mult, ALU.add, tk, efree, tcs))
            banks.free[b] = ts_
            t1 = V.do(lambda e, o=sv[:, 0:1], i_=ev[:, 0:nk]: e.reduce_max(o, i_, AX.X), ts_, sfree)
            t1 = ts(sv[:, 1:2], sv[:, 0:1], SK[:, h:h + 1], -1.0, ALU.max, ALU.mult, t1, tsk)
            t2 = act(ev[:, 0:nk], ev[:, 0:nk], ACT.Exp, t1, bias=sv[:, 1:2], accum_out=sv[:, 2:3])
            t3 = act(sv[:, 3:4], SK[:, h:h + 1], ACT.Exp, t1, bias=sv[:, 1:2])
            yield
            t4 = tt(sv[:, 4:5], sv[:, 2:3], sv[:, 3:4], ALU.add, t2, t3)
            t4 = rcp(sv[:, 5:6], sv[:, 4:5], t4)
            b, pv, free = banks.take()
            for c in range(nk // 128):
                tk = tr(pv[:, c * 128:c * 128 + 128], ev[:, c * 128:c * 128 + 128], t2, free)
            es.free[ei] = [tk]
            wi, wvv, wfree = wt.take()
            t5 = copyS(wvv[:, 0:nk], pv[:, 0:nk], tk, wfree)
            banks.free[b] = [t5]
            yield
            if n not in outs:
                outs[n] = [*oo.take(), []]
            oi, ov, ofree, t_o = outs[n]
            b, pv, free = banks.take()
            vc = [2 + n - 1 + (lo // 128) + c for c in range(nb // 128)] + [0, 1]
            for x, c in enumerate(vc):
                tk = mm(pv[:, 0:64], wvv[:, x * 128:x * 128 + 128], vt[:, c, 64 * kv:64 * kv + 64], x == 0,
                        x == len(vc) - 1, t5, t_v, free)
            wt.free[wi] = [tk]
            t6 = act(ov[:, 64 * h:64 * h + 64], pv[:, 0:64], ACT.Copy, tk, t4, ofree, scale=sv[:, 5:6])
            banks.free[b] = [t6]
            st.free[si] = [t6]
            t_o.append(t6)
            if len(t_o) < 8:
                return
            yield
            b, pv, free = banks.take()
            for m in range(4):
                tk = tr(pv[:, m * 128:m * 128 + 128], ov[:, m * 128:m * 128 + 128], t_o, free)
            oo.free[oi] = [tk]
            t7 = cpV(OA[:, :, n * 128:n * 128 + 128], pv[:, 0:512].rearrange("p (m t) -> p m t", m=4), tk, start)
            banks.free[b] = [t7]
        weave([wunit(n, h) for n in range(4) for h in range(8)], 3)
        t_oa = split(OAH, OAL, OA, bar())
        start = bar()
        MG = A[:, 8192:12288].rearrange("p (m t) -> p m t", t=512)
        MGL = AR[:, 8192:12288].rearrange("p (m t) -> p m t", t=512)
        MGH = AR[:, 12288:16384].rearrange("p (m t) -> p m t", t=512)
        s1 = Slots([A[:, 16384 + 512 * x:16896 + 512 * x] for x in range(4)])
        s1.free = [[start] for _ in range(4)]
        t_mg = []
        for m in range(0, 8, 2):
            res = {}
            for x in range(2):
                for f in range(2):
                    b, pv, tk = lin([wp(w, 3328 + 1024 * x + 128 * (m + f), 128)], hx, 8, TC, T)
                    si, sv, sfree = s1.take()
                    t1 = act(sv, pv[:, 0:512], ACT.Sigmoid, tk, sfree)
                    banks.free[b] = [t1]
                    res[(x, f)] = (sv, t1, si)
            for f in range(2):
                for x in range(2):
                    sh, slo = ((OAH, OAL), (OHH, OHL))[x]
                    b, pv, tk = lin([wp((a["w_o_attn_2"], a["w_o_hgrn_2"])[x][0], 128 * (m + f), 128, 0, 4)],
                                    (lambda k, a0, a1: sh[:, k, a0 - TC:a1 - TC],
                                     lambda k, a0, a1: slo[:, k, a0 - TC:a1 - TC]),
                                    4, TC, T, t_r, t_oa, start)
                    sv, t1, si = res[(x, f)]
                    t2 = tt(sv, sv, pv[:, 0:512], ALU.mult, t1, tk)
                    banks.free[b] = [t2]
                    res[(x, f)] = (sv, t2, si)
                t3 = tt(MG[:, m + f, :], res[(0, f)][0], res[(1, f)][0], ALU.add, res[(0, f)][1], res[(1, f)][1])
                for x in range(2):
                    s1.free[res[(x, f)][2]] = [t3]
                t_mg.append([split(MGH[:, m + f, :], MGL[:, m + f, :], MG[:, m + f, :], t3)])
        start = bar()
        res = []
        YB = A[:, 0:6144].rearrange("p (m t) -> p m t", t=T)
        for m in range(8):
            b, pv, tk = lin([wp(a["w_out_2"][0], 128 * m, 128)],
                            (lambda k, a0, a1: MGH[:, k, a0 - TC:a1 - TC],
                             lambda k, a0, a1: MGL[:, k, a0 - TC:a1 - TC]), 8, TC, T, perk=t_mg)
            res.append([copyS(YB[:, m, TC:T], pv[:, 0:512], tk, start)])
            banks.free[b] = res[-1]
        xt = post(1, XX, res, 1.0, YB)
        ht = pre(2, XX, xt)
        res = ffn(a["ffn2_w_in_2"][0], a["ffn2_w_out_2"][0], TC, ht, to_ya(TC))
        xt = post(2, XX, res, 0.5, YA)
        start = bar()
        stage = A[:, 0:4096].rearrange("p (i c) -> p i c", c=D)
        for k in range(8):
            b, pv, free = banks.take()
            for i in range(4):
                tk = tr(pv[:, i * 128:i * 128 + 128], XT[:, k, TC + i * 128:TC + i * 128 + 128], xt[k], free)
            t1 = copyS(stage[:, :, k * 128:k * 128 + 128], pv[:, 0:512].rearrange("p (i n) -> p i n", i=4), tk,
                       start)
            banks.free[b] = [t1]
        for i in range(4):
            Y.dma(lambda e, i=i: e.dma_start(out[0, i * 128:i * 128 + 128, :], stage[:, i, :]), osem, cnt, t1)

        
    xt, ht = layer0(xt)
    xt = layer1(xt, ht)
    block2(xt)
    Y.wait([(osem, cnt[id(osem)])])


def constants():
    i = np.arange(128)
    r, c = i[:, None], i[None, :]
    f = np.float32
    perm = np.zeros((128, 128), f)
    for m in range(128):
        if m % 32 < 16:
            perm[m + 16, m] = -1
        else:
            perm[m - 16, m] = 1
    base = np.concatenate([np.eye(128), r <= c, r >= c, perm], 1).astype(f)
    blk = r // 64 == c // 64
    glam = np.concatenate([blk & (r <= c), blk & (r >= c)], 1).astype(f)
    minm = np.concatenate([np.where(r <= c, 0, -1e30), np.where(r >= c, 0, -1e30)], 1).astype(f)
    winm = np.concatenate([np.where(c >= r, 0, -1e30), np.where(c <= r, 0, -1e30)], 1).astype(f)
    lv = []
    for m in (64, 32, 16, 8, 4, 2, 1):
        same = r // (2 * m) == c // (2 * m)
        lv.append(same & (r % (2 * m) < m) & (c % (2 * m) >= m))
    hgm = np.concatenate(lv + [x.T for x in lv], 1).astype(f)
    t = np.arange(512)
    inv = (f(10000.0) ** (-np.arange(16, dtype=f) / f(16))).astype(f)
    pos = np.stack([t // 64, t % 64]).astype(f)
    ang = np.empty((128, 512), f)
    for p in range(128):
        ang[p] = pos[(p // 32) % 2] * inv[p % 16]
    return {"base": base, "glam": glam, "minm": minm, "winm": winm, "hgm": hgm,
            "cos": np.cos(ang).astype(f), "sin": np.sin(ang).astype(f)}


def kernel(**inputs):
    import numpy as _np
    import concourse.bacc as _bacc
    from concourse import mybir as _mybir
    from concourse.bass_utils import run_bass_kernel_spmd as _run

    nc = _bacc.Bacc("TRN2", target_bir_lowering=False, num_devices=1)
    arrays, a, con = {}, {}, {}
    for name, x in inputs.items():
        x = _np.ascontiguousarray(x)
        arrays[f"in_{name}"] = x
        a[name] = nc.dram_tensor(f"in_{name}", x.shape, _mybir.dt.from_np(x.dtype), kind="ExternalInput").ap()
    for name, x in constants().items():
        arrays[f"con_{name}"] = x
        con[name] = nc.dram_tensor(f"con_{name}", x.shape, _mybir.dt.from_np(x.dtype), kind="ExternalInput").ap()
    out = nc.dram_tensor("out_0", (1, 512, 1024), _mybir.dt.float32, kind="ExternalOutput").ap()
    program(nc, a, con, out)
    r = _run(nc, [arrays], core_ids=[0])
    return r.results[0]["out_0"]
```
